# Optimizing a Trainium2 kernel written in Bass

```python
import jax, jax.numpy as jnp
from jax import lax
import numpy as np

D_MODEL = 1024
BATCH = 1
SEQ = 512
DEPTH = 1

N_HEADS_NSA = 8
HEAD_DIM = 64
N_KV_GROUPS = 2
HPG = N_HEADS_NSA // N_KV_GROUPS
CMP_BLOCK = 32
CMP_STRIDE = 16
CMP_HIDDEN = 128
SEL_BLOCK = 64
N_SELECT = 16
WINDOW = 512
Q_BLOCK = 128
NSA_W = N_HEADS_NSA * HEAD_DIM
GMLP_WIDTH = 512
GMLP_GROUPS = 4
GMLP_CHUNK = 128
GMLP_GROUP_DIM = GMLP_WIDTH // GMLP_GROUPS
MEM_TOKENS = 256
MEM_HEADS = 4
MEM_HEAD_DIM = 128
MEM_W = MEM_HEADS * MEM_HEAD_DIM
D_FF = -(-8 * D_MODEL // (3 * 256)) * 256
KV_W = 2 * N_KV_GROUPS * HEAD_DIM
GATE_W = 3 * N_HEADS_NSA
IN_W = NSA_W + 3 * KV_W + 2 * GMLP_WIDTH + GATE_W
SPLITS = [NSA_W, NSA_W + KV_W, NSA_W + 2 * KV_W, NSA_W + 3 * KV_W, NSA_W + 3 * KV_W + 2 * GMLP_WIDTH]

EPS = 1e-6
NEG = -1e30
FORCE_SCORE = 1e6

kernel_name = "nsa_gmlp_griffin_gated_hybrid"

def rmsnorm(x, g):
    xf = x.astype(jnp.float32)
    y = xf * lax.rsqrt(jnp.mean(xf * xf, axis=-1, keepdims=True) + EPS)
    return (y * g.astype(jnp.float32)).astype(x.dtype)

def layernorm(x, g):
    xf = x.astype(jnp.float32)
    xc = xf - jnp.mean(xf, axis=-1, keepdims=True)
    y = xc * lax.rsqrt(jnp.mean(xc * xc, axis=-1, keepdims=True) + EPS)
    return (y * g.astype(jnp.float32)).astype(x.dtype)

def masked_softmax(s, mask):
    s = jnp.where(mask, s, NEG)
    m = jnp.max(s, axis=-1, keepdims=True)
    p = jnp.where(mask, jnp.exp(s - m), 0.0)
    return p / jnp.maximum(jnp.sum(p, axis=-1, keepdims=True), 1e-30)

def alibi_slopes(n):
    return jnp.asarray([2.0 ** (-8.0 * (h + 1) / n) for h in range(n)], dtype=jnp.float32)

def compress(x, pe, w1, w2):
    B, T, G, Dh = x.shape
    c = x.reshape(B, T // CMP_STRIDE, CMP_STRIDE, G, Dh)
    blk = jnp.concatenate([c[:, :-1], c[:, 1:]], axis=2) + pe[None, None, :, None, :]
    flat = blk.transpose(0, 1, 3, 2, 4).reshape(B, T // CMP_STRIDE - 1, G, CMP_BLOCK * Dh)
    return jax.nn.gelu(flat @ w1) @ w2

def nsa_attention(q, k_cmp, v_cmp, k_slc, v_slc, k_win, v_win, gates):
    B, T = q.shape[0], q.shape[1]
    G, Dh = N_KV_GROUPS, HEAD_DIM
    n_cmp = k_cmp.shape[1]
    n_slc = T // SEL_BLOCK
    n_sel = min(N_SELECT, n_slc)
    n_qb = T // Q_BLOCK
    scale = Dh ** -0.5
    slopes = alibi_slopes(N_HEADS_NSA).reshape(G, HPG)[None, :, :, None, None]
    cmp_start = jnp.arange(n_cmp) * CMP_STRIDE
    cmp_end = cmp_start + CMP_BLOCK - 1
    sel_start = jnp.arange(n_slc) * SEL_BLOCK
    overlap = ((cmp_start[:, None] < sel_start[None, :] + SEL_BLOCK)
               & (cmp_end[:, None] >= sel_start[None, :])).astype(jnp.float32)
    kb = k_slc.reshape(B, n_slc, SEL_BLOCK, G, Dh).transpose(0, 3, 1, 2, 4)
    vb = v_slc.reshape(B, n_slc, SEL_BLOCK, G, Dh).transpose(0, 3, 1, 2, 4)
    kw = jnp.pad(k_win, ((0, 0), (WINDOW, 0), (0, 0), (0, 0)))
    vw = jnp.pad(v_win, ((0, 0), (WINDOW, 0), (0, 0), (0, 0)))
    qb = q.reshape(B, n_qb, Q_BLOCK, G, HPG, Dh).transpose(1, 0, 2, 3, 4, 5)
    gb = gates.reshape(B, n_qb, Q_BLOCK, G, HPG, 3).transpose(1, 0, 2, 3, 4, 5)
    starts = jnp.arange(n_qb, dtype=jnp.int32) * Q_BLOCK
    b_idx = jnp.arange(B)[:, None, None, None]
    g_idx = jnp.arange(G)[None, :, None, None]
    blk_ids = jnp.arange(n_slc)
    key_off = jnp.arange(SEL_BLOCK)
    win_off = jnp.arange(WINDOW + Q_BLOCK)

    def one_block(args):
        qi, gi, start = args
        t = start + jnp.arange(Q_BLOCK)
        s = jnp.einsum('bqghd,bigd->bghqi', qi, k_cmp).astype(jnp.float32) * scale
        s = s - slopes * (t[:, None] - cmp_end[None, :]).astype(jnp.float32)
        p_cmp = masked_softmax(s, cmp_end[None, :] <= t[:, None])
        o_cmp = jnp.einsum('bghqi,bigd->bqghd', p_cmp.astype(v_cmp.dtype), v_cmp)
        imp = jnp.einsum('bghqi,ij->bgqj', p_cmp, overlap)
        cur = t // SEL_BLOCK
        causal_blk = blk_ids[None, :] <= cur[:, None]
        forced = ((blk_ids[None, :] == 0) | (blk_ids[None, :] == cur[:, None])
                  | (blk_ids[None, :] == cur[:, None] - 1))
        rank = jnp.where(causal_blk, jnp.where(forced, FORCE_SCORE, imp), NEG)
        top_val, top_idx = lax.top_k(rank, n_sel)
        k_sel = kb[b_idx, g_idx, top_idx].reshape(B, G, Q_BLOCK, n_sel * SEL_BLOCK, Dh)
        v_sel = vb[b_idx, g_idx, top_idx].reshape(B, G, Q_BLOCK, n_sel * SEL_BLOCK, Dh)
        pos = top_idx[..., None] * SEL_BLOCK + key_off
        ok = (pos <= t[None, None, :, None, None]) & (top_val > NEG / 2)[..., None]
        pos = pos.reshape(B, G, Q_BLOCK, n_sel * SEL_BLOCK)
        ok = ok.reshape(B, G, Q_BLOCK, n_sel * SEL_BLOCK)
        s = jnp.einsum('bqghd,bgqsd->bghqs', qi, k_sel).astype(jnp.float32) * scale
        s = s - slopes * (t[None, None, :, None] - pos)[:, :, None].astype(jnp.float32)
        p = masked_softmax(s, ok[:, :, None])
        o_slc = jnp.einsum('bghqs,bgqsd->bqghd', p.astype(v_sel.dtype), v_sel)
        k_w = lax.dynamic_slice_in_dim(kw, start, WINDOW + Q_BLOCK, axis=1)
        v_w = lax.dynamic_slice_in_dim(vw, start, WINDOW + Q_BLOCK, axis=1)
        pos_w = start - WINDOW + win_off
        dist = t[:, None] - pos_w[None, :]
        s = jnp.einsum('bqghd,bsgd->bghqs', qi, k_w).astype(jnp.float32) * scale
        s = s - slopes * dist.astype(jnp.float32)
        p = masked_softmax(s, (dist >= 0) & (dist < WINDOW) & (pos_w[None, :] >= 0))
        o_win = jnp.einsum('bghqs,bsgd->bqghd', p.astype(v_w.dtype), v_w)
        return gi[..., 0:1] * o_cmp + gi[..., 1:2] * o_slc + gi[..., 2:3] * o_win

    out = lax.map(one_block, (qb, gb, starts))
    return out.transpose(1, 0, 2, 3, 4, 5).reshape(B, T, NSA_W)

def chunked_sgu(u, v, ln_g, w_s, b_s):
    B, T, _ = v.shape
    v = layernorm(v, ln_g)
    vc = v.reshape(B, T // GMLP_CHUNK, GMLP_CHUNK, GMLP_GROUPS, GMLP_GROUP_DIM)
    w = w_s * jnp.tril(jnp.ones((GMLP_CHUNK, GMLP_CHUNK), w_s.dtype))
    s = jnp.einsum('gts,bcsgd->bctgd', w, vc) + b_s.T[None, None, :, :, None]
    return u * s.reshape(B, T, GMLP_WIDTH)

def setup_inputs(seed: int = 0) -> dict:
    key = jax.random.key(seed)
    ks = iter(jax.random.split(key, 40))
    L = DEPTH

    def w(shape, fan_in):
        return jax.random.normal(next(ks), shape, jnp.float32) * fan_in ** -0.5

    def gain(shape):
        return 1.0 + 0.02 * jax.random.normal(next(ks), shape, jnp.float32)

    def small(shape, s):
        return s * jax.random.normal(next(ks), shape, jnp.float32)

    return {
        "x": jax.random.normal(next(ks), (BATCH, SEQ, D_MODEL), jnp.float32),
        "mem": jax.random.normal(next(ks), (BATCH, MEM_TOKENS, D_MODEL), jnp.float32),
        "norm_mix": gain((L, D_MODEL)),
        "w_in": w((L, D_MODEL, IN_W), D_MODEL),
        "w_cmp_k1": w((L, CMP_BLOCK * HEAD_DIM, CMP_HIDDEN), CMP_BLOCK * HEAD_DIM),
        "w_cmp_k2": w((L, CMP_HIDDEN, HEAD_DIM), CMP_HIDDEN),
        "w_cmp_v1": w((L, CMP_BLOCK * HEAD_DIM, CMP_HIDDEN), CMP_BLOCK * HEAD_DIM),
        "w_cmp_v2": w((L, CMP_HIDDEN, HEAD_DIM), CMP_HIDDEN),
        "pe_cmp_k": small((L, CMP_BLOCK, HEAD_DIM), 0.1),
        "pe_cmp_v": small((L, CMP_BLOCK, HEAD_DIM), 0.1),
        "ln_sgu": gain((L, GMLP_WIDTH)),
        "w_spatial": w((L, GMLP_GROUPS, GMLP_CHUNK, GMLP_CHUNK), GMLP_CHUNK),
        "b_spatial": 1.0 + small((L, GMLP_GROUPS, GMLP_CHUNK), 0.1),
        "w_proj_a": w((L, NSA_W, D_MODEL), NSA_W),
        "w_proj_b": w((L, GMLP_WIDTH, D_MODEL), GMLP_WIDTH),
        "w_merge": w((L, D_MODEL, 2 * D_MODEL), D_MODEL),
        "b_merge": small((L, 2 * D_MODEL), 0.1),
        "w_out": w((L, D_MODEL, D_MODEL), D_MODEL),
        "norm_mem_q": gain((L, D_MODEL)),
        "norm_mem_kv": gain((L, D_MODEL)),
        "w_mq": w((L, D_MODEL, MEM_W), D_MODEL),
        "w_mkv": w((L, D_MODEL, 2 * MEM_W), D_MODEL),
        "w_mo": w((L, MEM_W, D_MODEL), MEM_W),
        "norm_ffn": gain((L, D_MODEL)),
        "w_gate_up": w((L, D_MODEL, 2 * D_FF), D_MODEL),
        "w_down": w((L, D_FF, D_MODEL), D_FF),
        "norm_final": gain((D_MODEL,)),
    }

def reference(x, mem, norm_mix, w_in, w_cmp_k1, w_cmp_k2, w_cmp_v1, w_cmp_v2, pe_cmp_k, pe_cmp_v,
              ln_sgu, w_spatial, b_spatial, w_proj_a, w_proj_b, w_merge, b_merge, w_out,
              norm_mem_q, norm_mem_kv, w_mq, w_mkv, w_mo, norm_ffn, w_gate_up, w_down, norm_final):
    B, T, _ = x.shape
    n_mem = mem.shape[1]
    h = x
    for l in range(DEPTH):
        xn = rmsnorm(h, norm_mix[l])
        proj = xn @ w_in[l]
        q, kvc, kvs, kvw, uv, g_raw = jnp.split(proj, SPLITS, axis=-1)
        q = q.reshape(B, T, N_HEADS_NSA, HEAD_DIM)
        kvc = kvc.reshape(B, T, 2, N_KV_GROUPS, HEAD_DIM)
        kvs = kvs.reshape(B, T, 2, N_KV_GROUPS, HEAD_DIM)
        kvw = kvw.reshape(B, T, 2, N_KV_GROUPS, HEAD_DIM)
        k_cmp = compress(kvc[:, :, 0], pe_cmp_k[l], w_cmp_k1[l], w_cmp_k2[l])
        v_cmp = compress(kvc[:, :, 1], pe_cmp_v[l], w_cmp_v1[l], w_cmp_v2[l])
        nsa_gates = jax.nn.sigmoid(g_raw.astype(jnp.float32)).reshape(B, T, N_HEADS_NSA, 3).astype(q.dtype)
        o_nsa = nsa_attention(q, k_cmp, v_cmp, kvs[:, :, 0], kvs[:, :, 1], kvw[:, :, 0], kvw[:, :, 1], nsa_gates)
        u, v = jnp.split(jax.nn.gelu(uv), 2, axis=-1)
        o_sgu = chunked_sgu(u, v, ln_sgu[l], w_spatial[l], b_spatial[l])
        mg = jax.nn.sigmoid((xn @ w_merge[l] + b_merge[l]).astype(jnp.float32)).astype(h.dtype)
        mg = mg.reshape(B, T, 2, D_MODEL)
        mixed = mg[:, :, 0] * (o_nsa @ w_proj_a[l]) + mg[:, :, 1] * (o_sgu @ w_proj_b[l])
        h = h + mixed @ w_out[l]
        hq = (rmsnorm(h, norm_mem_q[l]) @ w_mq[l]).reshape(B, T, MEM_HEADS, MEM_HEAD_DIM)
        mkv = (rmsnorm(mem, norm_mem_kv[l]) @ w_mkv[l]).reshape(B, n_mem, 2, MEM_HEADS, MEM_HEAD_DIM)
        s = jnp.einsum('bthd,bnhd->bhtn', hq, mkv[:, :, 0]).astype(jnp.float32) * MEM_HEAD_DIM ** -0.5
        p = jax.nn.softmax(s, axis=-1).astype(h.dtype)
        o = jnp.einsum('bhtn,bnhd->bthd', p, mkv[:, :, 1]).reshape(B, T, MEM_W)
        h = h + o @ w_mo[l]
        gate, up = jnp.split(rmsnorm(h, norm_ffn[l]) @ w_gate_up[l], 2, axis=-1)
        h = h + (jax.nn.silu(gate) * up) @ w_down[l]
    return rmsnorm(h, norm_final)


_drawn_inputs = setup_inputs


def setup_inputs(seed=0):
    import zlib

    import numpy as np

    out = dict(_drawn_inputs(seed))
    spreads = {}
    factors = {'norm_mix': 4.487,
     'pe_cmp_k': 8.0,
     'pe_cmp_v': 3.872,
     'ln_sgu': 8.0,
     'b_merge': 3.118,
     'norm_mem_q': 8.0,
     'norm_mem_kv': 8.0,
     'norm_ffn': 12.814,
     'norm_final': 7.881}
    for name, (base, spread) in spreads.items():
        noise = np.random.default_rng([zlib.crc32(name.encode()), seed]).standard_normal(out[name].shape)
        drawn = base * np.exp(spread * noise) if base else spread * noise
        out[name] = __import__('jax').numpy.asarray(drawn.astype(out[name].dtype))
    for name, factor in factors.items():
        out[name] = (out[name] * factor).astype(out[name].dtype)
    return out
```

```python
from contextlib import ExitStack

import numpy as np

P = 128
T = 512
D = 1024
KT = D // P
TB = T // P
HD = 64
PAIRS = 4
NCMP = 31
CJ = 16
MEM = 256
MB = MEM // P
MH = 4
FT = 2816 // P
SLOTS = 4
CW = KT * P

C_MEM, N_MEM = 0, 8
C_IN = C_MEM + N_MEM
N_IN = 7
C_ATT = C_IN + N_IN
N_ATT = 4 * PAIRS
C_MRG = C_ATT + N_ATT
N_MRG = 20
C_OUT = C_MRG + N_MRG
C_MQ = C_OUT + KT
C_MO = C_MQ + MH
C_GU = C_MO + KT // 2
C_DN = C_GU + 2 * FT
NCHUNK = C_DN + 3 * KT

P_ATT = C_ATT
P_MRG = C_MRG
P_OUT = P_MRG + 28
P_MQ = P_OUT + KT
P_MO = P_MQ + MH
P_GU = P_MO + KT
P_DN = P_GU + 2 * FT
C_AB = [C_MRG + 4 + n for n in range(4)] + [C_MRG + 16 + n for n in range(4)]
P_AB = [P_MRG + 4 + 2 * n for n in range(4)] + [P_MRG + 20 + 2 * n for n in range(4)]
FREE_MQ = P_OUT
FREE_GU = FREE_MQ + MH

F_MEMRMS, F_XRMS, F_HID, F_CMP = 0, 1, 2, 3
F_ATT, F_PAIR = 4, 18
F_SGU = F_ATT + F_PAIR * PAIRS
F_QRMS = F_SGU + 4
F_CROSS = F_QRMS + 1
F_FRMS = F_CROSS + 2 * MH
F_ORMS = F_FRMS + 1
R_MEM, R_SLC, R_WIN, R_GATE = 0, 4, 5, 6
R_ATT, R_PAIR = 7, 16
R_CROSS = R_ATT + R_PAIR * PAIRS

KS, KW, VS, VW, KC_, VC_ = 0, 512, 1024, 1280, 1536, 1568
KVW = 1632

_cols = [("gmix", KT), ("gmem", KT), ("gq", KT), ("gf", KT), ("gfin", KT), ("bm", 2 * KT), ("lng", 4),
         ("slope", 8), ("valid", TB), ("eps", 1), ("eps4", 1), ("w2k", P), ("w2v", HD), ("pe", 64),
         ("ident", P), ("tri", P), ("tab", 640), ("ws", 4 * P)]
COL, NCOL = {}, 0
for _n, _w in _cols:
    COL[_n] = (NCOL, _w)
    NCOL += _w
NCOL += -NCOL % 8
MASKED = 1e32
SC_MEM = float(P) ** -0.5
GC, GA = 0.7978845608028654, 0.044715


def unit_off(qb):
    return P * qb * (qb + 1) // 2


def row_off(kb):
    return sum((TB - k) * P for k in range(kb))


class Steps:

    def __init__(self):
        self.base, self.k, self.turn = 0, 0, None

    def add(self):
        self.k += 1
        return 1

    def now(self):
        return self.base + self.k if self.turn is None else self.base + self.k + self.turn * self.per

    def enter(self, turn, per):
        self.base, self.k, self.turn, self.per = self.base + self.k, 0, turn, per

    def leave(self, turns):
        assert self.k == self.per, (self.k, self.per)
        self.base, self.k, self.turn = self.base + self.per * turns, 0, None


def build(nc, wpk, xT, memT, w1d, cst, bsp, out):
    import concourse.bass as bass
    from concourse import mybir

    F32, F32R = mybir.dt.float32, mybir.dt.float32r
    ALU, ACT, AX = mybir.AluOpType, mybir.ActivationFunctionType, mybir.AxisListType.X

    with ExitStack() as ctx:
        total = 52800
        arena = ctx.enter_context(nc.sbuf_tensor("arena", [P, total], F32))
        base = arena_base(nc, arena, total)

        def at(name, off, shape, dt=F32):
            n = int(np.prod(shape[1:]))
            assert off + n <= total, (name, off + n)
            return nc.alloc_sbuf_tensor_at(name, shape, dt, offset=base + 4 * off)

        def sem(name):
            return ctx.enter_context(nc.semaphore(name))

        o = 0
        WRAW = at("w_raw", o, [P, SLOTS, KT, P])
        WL = at("w_lo", o, [P, SLOTS, KT, P], F32R)
        o += SLOTS * CW
        WH = at("w_hi", o, [P, SLOTS, KT, P], F32R)
        o += SLOTS * CW
        XH = at("x_hi", o, [P, KT, T], F32R)
        OUTT = at("out_t", o, [P, KT, T])
        o += KT * T
        XL = at("x_lo", o, [P, KT, T], F32R)
        o += KT * T
        CST = at("cst", o, [P, NCOL])
        o += NCOL
        ONES = at("ones", o, [P, P]); o += P
        RS = at("rs", o, [P, T]); o += T
        RSM = at("rs_mem", o, [P, MEM]); o += MEM
        ACC = at("acc", o, [P, T]); o += T
        SQ = at("sq", o, [P, 2, T]); o += 2 * T
        Z = at("z", o, [P, 4, T]); o += 4 * T
        BH = at("bh", o, [P, 2 * KT]); o += 2 * KT
        BB = at("bb", o, [P, 4, P]); o += 4 * P
        GT = at("gt", o, [P, TB, 24]); o += TB * 24
        MN = at("mn", o, [P, 16]); o += 16
        DEN = at("den", o, [P, 16]); o += 16
        RD = at("rd", o, [P, 16]); o += 16
        MC = at("mc", o, [P, 2, TB]); o += 8
        DC = at("dc", o, [P, 2, TB]); o += 8
        RC = at("rc", o, [P, 2, TB]); o += 8
        HOLD = at("hold", o, [P, 16]); o += 16
        BN = at("bn", o, [P, TB, 6]); o += TB * 6
        BA = at("ba", o, [P, TB, 2]); o += TB * 2
        LS = at("ls", o, [P, TB]); o += 8
        z0 = o
        H = at("h", z0, [P, KT, T])
        U = at("u", z0, [P, 4, T])
        VT = at("v_tok", z0 + 2048, [P, TB, T])
        MK = at("mk", z0 + 4096, [P, MH, MEM])
        MV = at("mv", z0 + 5120, [P, MB, MH * P])
        z = z0 + 6144
        ONH = at("on_hi", z, [P, PAIRS, T], F32R)
        ONL = at("on_lo", z + 2048, [P, PAIRS, T], F32R)
        W1 = at("w1", z, [P, 2, CJ, P])
        OXH = at("ox_hi", z, [P, MH, T], F32R)
        OXL = at("ox_lo", z + 2048, [P, MH, T], F32R)
        SIG = at("sig", z + 4096, [P, 8, T])
        KC = at("kc", z + 4096, [P, 2, T])
        G = at("g", z + 5120, [P, 2, CJ, 2 * NCMP])
        HZ = at("hz", z + 7168, [P, 2, 4 * NCMP])
        P2 = at("p2", z + 4096, [P, 2, TB, MEM])
        PT2 = at("pt2", z + 6144, [P, 2, MB, T])
        KV = at("kv", z + 8192, [P, 2, KVW])
        KVS = at("kvs", z + 11456, [P, KVW])
        Q = at("q", z + 13088, [P, T])
        PP = at("pp", z + 13600, [P, 2, 1280])
        PT = at("pt", z + 16160, [P, 2, 1280])
        PC = at("pc", z + 18720, [P, 2, TB, 32])
        PCT = at("pct", z + 18976, [NCMP, 2, T])
        DN = at("dn", z + 20000, [P, 2, 640])
        MRAW = at("mem_raw", z + 8192, [P, KT, MEM])
        MSQ = at("mem_sq", z + 10240, [P, KT, MEM])
        MHH = at("mem_hi", z + 13600, [P, KT, MEM], F32R)
        MHL = at("mem_lo", z + 15648, [P, KT, MEM], F32R)
        OSH = at("os_hi", z + 8192, [P, 4, T], F32R)
        OSL = at("os_lo", z + 10240, [P, 4, T], F32R)
        MXH = at("mix_hi", z + 12288, [P, KT, T], F32R)
        MXL = at("mix_lo", z + 16384, [P, KT, T], F32R)
        HQ = at("hq", z + 20480, [P, 2, T])
        HH = at("hid_hi", z, [P, FT, T], F32R)
        HL = at("hid_lo", z + FT * T, [P, FT, T], F32R)

        def cc(name, a=0, b=None):
            c, w = COL[name]
            return CST[:, c + a:c + (w if b is None else b)]

        IDENT = cc("ident")

        LB = [ctx.enter_context(nc.psum_tensor(f"lin{i}", [P, T], F32)) for i in range(2)]
        SB = [ctx.enter_context(nc.psum_tensor(f"score{i}", [P, T], F32)) for i in range(3)]
        RB = [ctx.enter_context(nc.psum_tensor(f"turn{i}", [P, T], F32)) for i in range(2)]
        OB = ctx.enter_context(nc.psum_tensor("heads", [P, T], F32))

        w_loaded = [sem(f"w_loaded{s}") for s in range(SLOTS)]
        hi_ready = sem("hi_ready")
        lo_ready = sem("lo_ready")
        chunk_used = sem("chunk_used")
        cst_loaded, mem_loaded = sem("cst_loaded"), sem("mem_loaded")
        x_loaded = [sem("x_loaded0"), sem("x_loaded1")]
        w1_loaded, bsp_loaded, h_loaded = sem("w1_loaded"), sem("bsp_loaded"), sem("h_loaded")
        ones_ready = sem("ones_ready")
        memhi_ready, memlo_ready, memsq_ready = sem("memhi_ready"), sem("memlo_ready"), sem("memsq_ready")
        xhi_ready, xlo_ready = sem("xhi_ready"), sem("xlo_ready")
        sq_ready, acc_ready = sem("sq_ready"), sem("acc_ready")
        h_ready = sem("h_ready")
        rms_ready = sem("rms_ready")
        panel_half = sem("panel_half")
        panel_free = sem("panel_free")
        s_done, s_free = sem("s_done"), sem("s_free")
        r_done, r_free = sem("r_done"), sem("r_free")
        o_done, o_free = sem("o_done"), sem("o_free")
        gelu_sq, gelu_arg, gelu_tanh, gelu_done = sem("gelu_sq"), sem("gelu_arg"), sem("gelu_tanh"), sem("gelu_done")
        g_ready = sem("g_ready")
        kv_staged, dn_staged = sem("kv_staged"), sem("dn_staged")
        cmp_arg, cmp_exp, cmp_ready = sem("cmp_arg"), sem("cmp_exp"), sem("cmp_ready")
        p_max, p_exp, p_ready = sem("p_max"), sem("p_exp"), sem("p_ready")
        sig_ready = sem("sig_ready")
        onhi_ready, onlo_ready = sem("onhi_ready"), sem("onlo_ready")
        ln_var, ln_std, vn_ready = sem("ln_var"), sem("ln_std"), sem("vn_ready")
        sgu_out, oshi_ready, oslo_ready = sem("sgu_out"), sem("oshi_ready"), sem("oslo_ready")
        mix_ready, mixhi_ready, mixlo_ready = sem("mix_ready"), sem("mixhi_ready"), sem("mixlo_ready")
        act_tanh = sem("act_tanh")
        hid_ready, hidhi_ready, hidlo_ready = sem("hid_ready"), sem("hidhi_ready"), sem("hidlo_ready")
        dve_step = sem("dve_step")
        gates_ready = sem("gates_ready")
        out_ready, out_stored = sem("out_ready"), sem("out_stored")

        block = ctx.enter_context(nc.Block())

        def chunk_slot(i):
            return i % SLOTS

        @block.sync
        def _(sp):
            def load(i, s):
                sp.dma_start(WRAW[:, s, :, :], wpk[i].rearrange("p (u c) -> p u c", u=KT)).then_inc(w_loaded[s], 16)

            for i in range(SLOTS):
                load(i, i)
            with sp.Fori(1, NCHUNK // SLOTS) as g:
                for s in range(SLOTS):
                    sp.wait_ge(chunk_used, g * SLOTS + (s + 1 - SLOTS))
                    sp.dma_start(WRAW[:, s, :, :], wpk[bass.ds(g * SLOTS + s, 1), :, :].rearrange(
                        "a p (u c) -> p (a u) c", u=KT)).then_inc(w_loaded[s], 16)
            for i in range(NCHUNK // SLOTS * SLOTS, NCHUNK):
                sp.wait_ge(chunk_used, i + 1 - SLOTS)
                load(i, i % SLOTS)
            for m in range(4):
                sp.wait_ge(out_ready, 2 * m + 2)
                sp.dma_start(out[:, 2 * m:2 * m + 2, :], OUTT[:, 2 * m:2 * m + 2, :]).then_inc(out_stored, 16)
            sp.wait_ge(out_stored, 64)

        @block.gpsimd
        def _(pool):
            pool.memset(ONES[:, :], 1.0 / D).then_inc(ones_ready, 1)

            def split(i, s):
                pool.wait_ge(hi_ready, i + 1)
                pool.tensor_tensor(WL[:, s, :, :], WRAW[:, s, :, :], WH[:, s, :, :].bitcast(F32),
                                   ALU.subtract).then_inc(lo_ready, 1)

            with pool.Fori(0, NCHUNK // SLOTS) as g:
                for s in range(SLOTS):
                    split(g * SLOTS + s, s)
            for i in range(NCHUNK // SLOTS * SLOTS, NCHUNK):
                split(i, i % SLOTS)

        @block.scalar
        def _(act):
            act.dma_start(CST[:, :], cst).then_inc(cst_loaded, 16)
            act.dma_start(MRAW[:, :, :], memT).then_inc(mem_loaded, 16)
            for m in range(2):
                act.dma_start(H[:, 4 * m:4 * m + 4, :], xT[:, 4 * m:4 * m + 4, :]).then_inc(x_loaded[m], 16)
            act.dma_start(W1[:, :, :, :], w1d).then_inc(w1_loaded, 16)
            act.dma_start(BB[:, :, :], bsp.partition_broadcast(P)).then_inc(bsp_loaded, 16)

            def w_hi(i, s=None, turn=None):
                s = i % SLOTS if s is None else s
                act.wait_ge(w_loaded[s], 16 * (i // SLOTS + 1) if turn is None else turn)
                act.activation(WH[:, s, :, :], WRAW[:, s, :, :], ACT.Copy).then_inc(hi_ready, 1)

            def root(n, width, eps_bank, dst):
                act.wait_ge(s_done, n + 1)
                act.activation(dst, eps_bank[:, 0:width], ACT.Sqrt, bias=cc("eps")).then_inc(rms_ready, 1)

            def x_tile(n, gain, count):
                act.activation(XH[:, n, :], H[:, n, :], ACT.Copy, scale=gain).then_inc(xhi_ready, 1)
                if count >= 2:
                    act.wait_ge(acc_ready, count - 1)
                act.activation(SQ[:, count % 2, :], H[:, n, :], ACT.Square).then_inc(sq_ready, 1)

            w_hi(0)
            act.wait_ge(cst_loaded, 16)
            act.wait_ge(mem_loaded, 16)
            for k in range(KT):
                act.activation(MHH[:, k, :], MRAW[:, k, :], ACT.Copy, scale=cc("gmem", k, k + 1)).then_inc(memhi_ready, 1)
            w_hi(1)
            act.activation(MSQ[:, :, :], MRAW[:, :, :], ACT.Square).then_inc(memsq_ready, 1)
            w_hi(2)
            root(F_MEMRMS, MEM, SB[F_MEMRMS % 3], RSM[:, :])
            for i in range(N_MEM):
                w_hi(i + 3)
                act.wait_ge(x_loaded[i // 4], 16)
                x_tile(i, cc("gmix", i, i + 1), i)
                if i > 4:
                    n = i - 5
                    act.wait_ge(r_done, R_MEM + n + 1)
                    act.activation(MV[:, :, n * P:(n + 1) * P], RB[(R_MEM + n) % 2][:, 0:MEM].rearrange(
                        "p (b c) -> p b c", b=MB), ACT.Copy).then_inc(r_free, 1)
            w_hi(11)
            act.wait_ge(r_done, R_MEM + 4)
            act.activation(MV[:, :, 3 * P:4 * P], RB[(R_MEM + 3) % 2][:, 0:MEM].rearrange(
                "p (b c) -> p b c", b=MB), ACT.Copy).then_inc(r_free, 1)
            root(F_XRMS, T, SB[F_XRMS % 3], RS[:, :])
            w_hi(12)
            w_hi(13)
            w_hi(14)
            act.wait_ge(s_free, F_HID + 1)
            act.activation(HZ[:, 1, :], HZ[:, 0, :], ACT.Square).then_inc(gelu_sq, 1)
            act.wait_ge(gelu_arg, 1)
            act.activation(HZ[:, 1, :], HZ[:, 1, :], ACT.Tanh, scale=GC).then_inc(gelu_tanh, 1)

            def turned_values(n, off):
                act.wait_ge(r_done, n + 1)
                for g in range(2):
                    ins = act.activation(KV[:, g, off:off + TB * HD].rearrange("p (b d) -> p b d", b=TB),
                                         RB[n % 2][:, :].rearrange("p (b g d) -> p g b d", b=TB, g=2)[:, g, :, :],
                                         ACT.Copy)
                ins.then_inc(r_free, 1)

            turned_values(R_SLC, VS)
            w_hi(15)
            turned_values(R_WIN, VW)
            w_hi(16)
            act.wait_ge(r_done, R_GATE + 1)
            act.activation(GT[:, :, :], RB[R_GATE % 2][:, 0:TB * 24].rearrange("p (b c) -> p b c", b=TB),
                           ACT.Tanh, scale=0.5).then_inc(r_free, 1)
            w_hi(17)

            with act.Fori(0, PAIRS) as c:
                pan, fil, tur = P_ATT + c * 4, F_ATT + c * F_PAIR, R_ATT + c * R_PAIR

                def ahead(k):
                    i = C_ATT + k + 3
                    w_hi(i, i % SLOTS, (i // SLOTS + 1) * 16 + c * 16)

                def exps(u):
                    for qb in range(TB):
                        act.wait_ge(s_free, fil + (2 + 4 * u + qb + 1))
                        w = (qb + 1) * P
                        sl = PP[:, u % 2, unit_off(qb):unit_off(qb) + w]
                        j = 4 * u + qb
                        ins = act.activation(sl, sl, ACT.Exp, bias=MN[:, j:j + 1], scale=-1.0,
                                             accum_out=DEN[:, j:j + 1])
                    ins.then_inc(p_exp, 1)

                def turned(u):
                    for f in range(3):
                        k = 2 + 3 * u + f + (2 if u >= 2 else 0)
                        act.wait_ge(r_done, tur + (k + 1))
                        bank = RB[(R_ATT + k) % 2]
                        pt = PT[:, u % 2, :]
                        if f == 0:
                            ins = act.activation(pt[:, 0:512], bank[:, 0:512], ACT.Copy)
                        elif f == 1:
                            act.activation(pt[:, row_off(1):row_off(1) + 384], bank[:, 0:384], ACT.Copy)
                            ins = act.activation(pt[:, row_off(3):row_off(3) + 128], bank[:, 384:512], ACT.Copy)
                        else:
                            ins = act.activation(pt[:, row_off(2):row_off(2) + 256], bank[:, 0:256], ACT.Copy)
                        ins.then_inc(r_free, 1)

                ahead(0)
                act.wait_ge(o_free, c + 1)
                act.wait_ge(gates_ready, 1)
                act.activation(KVS[:, :], KV[:, bass.ds(c // 2, 1), :].rearrange("p a n -> p (a n)"), ACT.Copy).then_inc(kv_staged, 1)
                for e in range(2):
                    sc, _ = COL["slope"]
                    ins = act.activation(DN[:, e, :], cc("tab"), ACT.Copy, scale=CST[:, bass.ds(c * 2 + (sc + e), 1)])
                ins.then_inc(dn_staged, 1)
                ahead(1)
                for e in range(2):
                    act.wait_ge(cmp_arg, c * 2 + (e + 1))
                    act.activation(PC[:, e, :, 0:NCMP], PC[:, e, :, 0:NCMP], ACT.Exp, scale=-1.0).then_inc(cmp_exp, 1)
                exps(0)
                act.wait_ge(panel_free, pan + 2)
                act.activation(Z[:, 1, :], Z[:, 0, :], ACT.Square).then_inc(gelu_sq, 1)
                ahead(2)
                act.wait_ge(gelu_arg, c * 2 + 2)
                act.activation(Z[:, 1, :], Z[:, 1, :], ACT.Tanh, scale=GC).then_inc(gelu_tanh, 1)
                act.wait_ge(panel_free, pan + 3)
                act.activation(Z[:, 3, :], Z[:, 2, :], ACT.Square).then_inc(gelu_sq, 1)
                exps(1)
                for e in range(2):
                    act.wait_ge(r_done, tur + (e + 1))
                    act.activation(PCT[:, e, :], RB[(R_ATT + e) % 2][0:NCMP, :], ACT.Copy).then_inc(r_free, 1)
                turned(0)
                act.wait_ge(gelu_arg, c * 2 + 3)
                act.activation(Z[:, 3, :], Z[:, 3, :], ACT.Tanh, scale=GC).then_inc(gelu_tanh, 1)
                exps(2)
                turned(1)
                ahead(3)
                for a in range(2):
                    k = 8 + a
                    act.wait_ge(r_done, tur + (k + 1))
                    act.activation(VT[:, 2 * a:2 * a + 2, bass.ds(c * P, P)],
                                   RB[(R_ATT + k) % 2][:, 0:2 * P].rearrange("p (b d) -> p b d", b=2),
                                   ACT.Copy).then_inc(r_free, 1)
                exps(3)
                act.wait_ge(panel_free, pan + 4)
                sg = SIG[:, bass.ds(c, 1), :].rearrange("p a n -> p (a n)")
                act.activation(sg, sg, ACT.Tanh, scale=0.5, bias=BH[:, bass.ds(c, 1)]).then_inc(sig_ready, 1)
                turned(2)
                turned(3)
                act.wait_ge(o_done, c + 1)
                act.activation(ONH[:, bass.ds(c, 1), :].rearrange("p a n -> p (a n)"), OB[:, :], ACT.Copy).then_inc(onhi_ready, 1)

            act.wait_ge(ln_var, 1)
            act.activation(LS[:, :], BA[:, :, 1:2].rearrange("p b a -> p (b a)"), ACT.Sqrt, bias=cc("eps4")).then_inc(ln_std, 1)

            def gate_tile(sig, pan, chunk, col):
                act.wait_ge(panel_free, pan + 1)
                act.activation(SIG[:, sig, :], SIG[:, sig, :], ACT.Tanh, scale=0.5,
                               bias=BH[:, col:col + 1]).then_inc(sig_ready, 1)
                w_hi(chunk + 3)

            gate_tile(4, P_MRG, C_MRG, KT)
            gate_tile(5, P_MRG + 1, C_MRG + 1, KT + 1)
            for g in range(4):
                act.wait_ge(sgu_out, g + 1)
                act.activation(OSH[:, g, :], Z[:, 2 + g % 2, :], ACT.Copy).then_inc(oshi_ready, 1)
            gate_tile(6, P_MRG + 2, C_MRG + 2, KT + 2)
            gate_tile(7, P_MRG + 3, C_MRG + 3, KT + 3)
            for half in range(2):
                for k in range(4):
                    n = 4 * half + k
                    act.wait_ge(mix_ready, n + 1)
                    act.activation(MXH[:, n, :], Z[:, 2 * (k % 2), :], ACT.Copy, scale=0.5).then_inc(mixhi_ready, 1)
                    w_hi(C_MRG + (4 if half == 0 else 16) + k + 3)
                if half == 0:
                    act.wait_ge(oslo_ready, 4)
                    act.dma_start(H[:, :, :], xT).then_inc(h_loaded, 16)
                    for k in range(4):
                        gate_tile(k, P_MRG + 12 + k, C_MRG + 8 + k, 4 + k)
                    for k in range(4):
                        gate_tile(4 + k, P_MRG + 16 + k, C_MRG + 12 + k, KT + 4 + k)

            with act.Fori(0, 2) as r:
                for k in range(4):
                    n = r * 4 + k
                    act.wait_ge(h_ready, n + 1)
                    act.wait_ge(acc_ready, n + (KT - 1))
                    hn = H[:, bass.ds(n, 1), :].rearrange("p a n -> p (a n)")
                    act.activation(XH[:, bass.ds(n, 1), :].rearrange("p a n -> p (a n)"), hn, ACT.Copy,
                                   scale=CST[:, bass.ds(n + COL["gq"][0], 1)]).then_inc(xhi_ready, 1)
                    act.activation(SQ[:, k % 2, :], hn, ACT.Square).then_inc(sq_ready, 1)
                    i = C_OUT + 3 + k
                    w_hi(i, i % SLOTS, r * 16 + (i // SLOTS + 1) * 16)
            root(F_QRMS, T, SB[F_QRMS % 3], RS[:, :])

            def cross_exp(n):
                for qb in range(TB):
                    if qb % 2 == 0:
                        act.wait_ge(p_max, 2 * n + qb // 2 + 1)
                    j = 4 * (n % 2) + qb
                    bank = SB[(F_CROSS + 2 * n + qb // 2) % 3]
                    ins = act.activation(P2[:, n % 2, qb, :], bank[:, (qb % 2) * MEM:(qb % 2 + 1) * MEM], ACT.Exp,
                                         bias=MN[:, j:j + 1], scale=-1.0, accum_out=DEN[:, j:j + 1])
                    if qb % 2:
                        ins.then_inc(s_free, 1)

            def cross_turned(n):
                for b in range(MB):
                    k = R_CROSS + 2 * n + b
                    act.wait_ge(r_done, k + 1)
                    act.activation(PT2[:, n % 2, b, :], RB[k % 2][:, :], ACT.Copy).then_inc(r_free, 1)

            def cross_o(n):
                act.wait_ge(o_done, PAIRS + n + 1)
                act.activation(OXH[:, n, :], OB[:, :], ACT.Copy).then_inc(onhi_ready, 1)

            for n in range(MH):
                cross_exp(n)
                w_hi(C_MQ + n + 3)
                if n:
                    cross_turned(n - 1)
                    cross_o(n - 1)
            cross_turned(3)
            cross_o(3)
            for k in range(KT):
                n = k
                act.wait_ge(h_ready, KT + n + 1)
                act.activation(XH[:, n, :], H[:, n, :], ACT.Copy, scale=cc("gf", n, n + 1)).then_inc(xhi_ready, 1)
                act.wait_ge(acc_ready, 2 * KT + n - 1)
                act.activation(SQ[:, k % 2, :], H[:, n, :], ACT.Square).then_inc(sq_ready, 1)
                if k % 2:
                    w_hi(C_MO + k // 2 + 3)
            root(F_FRMS, T, SB[F_FRMS % 3], RS[:, :])
            with act.Fori(0, FT // 2) as r:
                for k in range(2):
                    j = r * 2 + k
                    act.wait_ge(panel_free, r * 4 + (FREE_GU + 2 * k + 1))
                    act.activation(Z[:, 2 * k + 1, :], Z[:, 2 * k, :], ACT.Tanh, scale=0.5).then_inc(act_tanh, 1)
                    for m in range(2):
                        i = C_GU + 3 + 2 * k + m
                        w_hi(i, i % SLOTS, (i // SLOTS + 1) * 16 + r * 16)
                    act.wait_ge(hid_ready, j + 1)
                    act.activation(HH[:, bass.ds(j, 1), :].rearrange("p a n -> p (a n)"), Z[:, 2 * k, :], ACT.Copy,
                                   scale=0.5).then_inc(hidhi_ready, 1)
            for n in range(KT):
                for m in range(3):
                    if C_DN + 3 * n + m + 3 < NCHUNK:
                        w_hi(C_DN + 3 * n + m + 3)
                act.wait_ge(h_ready, 2 * KT + n + 1)
                act.wait_ge(acc_ready, 3 * KT + n - 1)
                act.activation(SQ[:, n % 2, :], H[:, n, :], ACT.Square).then_inc(sq_ready, 1)
            root(F_ORMS, T, SB[F_ORMS % 3], RS[:, :])

        @block.vector
        def _(dve):
            st = Steps()

            def chain():
                dve.wait_ge(dve_step, st.now())

            def x_lo(n, gain, count):
                dve.wait_ge(xhi_ready, count + 1)
                dve.scalar_tensor_tensor(XL[:, n, :], H[:, n, :], gain, XH[:, n, :].bitcast(F32),
                                         ALU.mult, ALU.subtract).then_inc(xlo_ready, 1)

            def add_square(count, first, k2):
                dve.wait_ge(sq_ready, count + 1)
                if first:
                    dve.tensor_copy(ACC[:, :], SQ[:, k2, :]).then_inc(acc_ready, 1)
                else:
                    dve.wait_ge(acc_ready, count)
                    dve.tensor_tensor(ACC[:, :], ACC[:, :], SQ[:, k2, :], ALU.add).then_inc(acc_ready, 1)

            def inverse(n_root, dst):
                dve.wait_ge(rms_ready, n_root)
                dve.reciprocal(dst, dst).then_inc(s_free, 1)

            def times_rms(p, dst, w=T, rs=None, lo=0, hi=P, dlo=None):
                rs = RS if rs is None else rs
                return dve.tensor_tensor(dst, LB[p % 2][lo:hi, 0:w], rs[lo:hi, 0:w], ALU.mult)

            dve.wait_ge(cst_loaded, 16)
            for g in range(4):
                w = CST[:, COL["ws"][0] + g * P:COL["ws"][0] + (g + 1) * P]
                dve.tensor_tensor(w, w, cc("tri"), ALU.mult)
            dve.tensor_scalar(BH[:, :], cc("bm"), 0.5, None, ALU.mult).then_inc(o_free, 1)
            dve.wait_ge(mem_loaded, 16)
            for k in range(KT):
                dve.wait_ge(memhi_ready, k + 1)
                dve.scalar_tensor_tensor(MHL[:, k, :], MRAW[:, k, :], cc("gmem", k, k + 1), MHH[:, k, :].bitcast(F32),
                                         ALU.mult, ALU.subtract).then_inc(memlo_ready, 1)
            inverse(1, RSM[:, :])
            for i in range(N_MEM):
                dve.wait_ge(x_loaded[i // 4], 16)
                x_lo(i, cc("gmix", i, i + 1), i)
                add_square(i, i == 0, i % 2)
                dve.wait_ge(s_free, 1)
                dve.wait_ge(chunk_used, i + 1)
                if i < MH:
                    times_rms(i, MK[:, i, :], MEM, RSM).then_inc(panel_free, 1)
                else:
                    if i >= MH + 2:
                        dve.wait_ge(r_done, R_MEM + i - MH - 1)
                    times_rms(i, Z[:, i % 2, 0:MEM], MEM, RSM).then_inc(panel_free, 1)
            inverse(2, RS[:, :])
            dve.wait_ge(memlo_ready, KT)
            dve.memset(KV[:, :, KC_:KVW], 0.0).then_inc(dve_step, st.add())
            dve.wait_ge(s_free, F_XRMS + 1)
            for s in range(2):
                dve.wait_ge(chunk_used, C_IN + s + 1)
                times_rms(C_IN + s, KC[:, s, :]).then_inc(panel_free, 1)
                dve.wait_ge(panel_free, C_IN + s + 1)
                pe, _ = COL["pe"]
                for g in range(2):
                    for par in range(2):
                        for a in range(2):
                            src = KC[g * HD:(g + 1) * HD, s, :].rearrange(
                                "p (m b r) -> p r b m", b=8, r=2)[:, par, :, a:a + NCMP]
                            pv = CST[g * HD:(g + 1) * HD, pe + (s * 2 + par) * CJ + 8 * a:pe + (s * 2 + par) * CJ + 8 * a + 8]
                            dst = G[par * HD:(par + 1) * HD, s, 8 * a:8 * a + 8, g * NCMP:(g + 1) * NCMP]
                            ins = dve.tensor_tensor(dst, src, pv.unsqueeze(2).broadcast_to((HD, 8, NCMP)), ALU.add)
                ins.then_inc(g_ready, 1)

            def keys_in(p, off):
                dve.wait_ge(chunk_used, p + 1)
                for g in range(2):
                    for half in range(2):
                        ins = dve.tensor_tensor(KV[half * HD:(half + 1) * HD, g, off:off + T],
                                                LB[p % 2][g * HD:(g + 1) * HD, :], RS[g * HD:(g + 1) * HD, :], ALU.mult)
                ins.then_inc(panel_free, 1)

            keys_in(C_IN + 2, KS)
            dve.wait_ge(chunk_used, C_IN + 4)
            dve.wait_ge(r_done, R_MEM + 4)
            times_rms(C_IN + 3, Z[:, 2, :]).then_inc(panel_free, 1)
            dve.wait_ge(s_done, F_HID + 1)
            dve.tensor_copy(HZ[:, 0, :], SB[F_HID % 3][:, 0:4 * NCMP]).then_inc(s_free, 1)
            dve.wait_ge(gelu_sq, 1)
            dve.tensor_scalar(HZ[:, 1, :], HZ[:, 1, :], GA, 1.0, ALU.mult, ALU.add).then_inc(dve_step, st.add())
            chain()
            dve.tensor_tensor(HZ[:, 1, :], HZ[:, 1, :], HZ[:, 0, :], ALU.mult).then_inc(gelu_arg, 1)
            dve.wait_ge(gelu_tanh, 1)
            dve.scalar_tensor_tensor(HZ[:, 1, :], HZ[:, 1, :], 1.0, HZ[:, 0, :], ALU.add, ALU.mult).then_inc(gelu_done, 1)
            keys_in(C_IN + 4, KW)
            dve.wait_ge(s_done, F_CMP + 1)
            for g in range(2):
                dve.tensor_scalar(KV[:, g, KC_:KC_ + NCMP], SB[F_CMP % 3][:, g * NCMP:(g + 1) * NCMP], 0.5, None, ALU.mult)
                ins = dve.tensor_scalar(KV[0:NCMP, g, VC_:VC_ + HD], SB[F_CMP % 3][0:NCMP, P + g * HD:P + (g + 1) * HD],
                                        0.5, None, ALU.mult)
            ins.then_inc(s_free, 1)
            dve.wait_ge(chunk_used, C_IN + 6)
            times_rms(C_IN + 5, Z[:, 3, :]).then_inc(panel_free, 1)
            dve.wait_ge(chunk_used, C_IN + 7)
            times_rms(C_IN + 6, Z[:, 0, :]).then_inc(panel_free, 1)
            dve.wait_ge(r_free, R_GATE + 1)
            dve.tensor_scalar(GT[:, :, :], GT[:, :, :], 0.5, 0.5, ALU.mult, ALU.add).then_inc(gates_ready, 1)

            with dve.Fori(0, PAIRS) as c:
                st.enter(c, 20)
                pan, fil = P_ATT + c * 4, F_ATT + c * F_PAIR

                def scores(u):
                    e = u // 2
                    for qb in range(TB):
                        k = 2 + 4 * u + qb
                        w = (qb + 1) * P
                        j = 4 * u + qb
                        dve.wait_ge(s_done, fil + (k + 1))
                        dve.memset(HOLD[:, j:j + 1], 0.0)
                        dve.tensor_tensor_reduce(PP[:, u % 2, unit_off(qb):unit_off(qb) + w],
                                                 SB[(F_ATT + k) % 3][:, 0:w], DN[:, e, 384 - P * qb:512], 1.0, 3e38,
                                                 ALU.add, ALU.min, MN[:, j:j + 1]).then_inc(s_free, 1)

                def weigh(u):
                    e, br = u // 2, u % 2
                    dve.wait_ge(p_exp, c * 4 + (u + 1))
                    dve.reciprocal(RD[:, 4 * u:4 * u + 4], DEN[:, 4 * u:4 * u + 4]).then_inc(dve_step, st.add())
                    chain()
                    gate = GT[:, :, bass.ds(c * 6 + (3 * e + 1 + br), 1)].rearrange("p b a -> p (b a)")
                    dve.tensor_tensor(RD[:, 4 * u:4 * u + 4], RD[:, 4 * u:4 * u + 4], gate, ALU.mult).then_inc(dve_step, st.add())
                    chain()
                    for qb in range(TB):
                        sl = PP[:, u % 2, unit_off(qb):unit_off(qb) + (qb + 1) * P]
                        ins = dve.tensor_scalar(sl, sl, RD[:, 4 * u + qb:4 * u + qb + 1], None, ALU.mult)
                    ins.then_inc(p_ready, 1)

                def gelu_a(n, z):
                    dve.wait_ge(gelu_sq, n)
                    dve.tensor_scalar(Z[:, z + 1, :], Z[:, z + 1, :], GA, 1.0, ALU.mult, ALU.add).then_inc(dve_step, st.add())
                    chain()
                    dve.tensor_tensor(Z[:, z + 1, :], Z[:, z + 1, :], Z[:, z, :], ALU.mult).then_inc(gelu_arg, 1)

                dve.wait_ge(chunk_used, C_ATT + 1 + c * 4)
                dve.scalar_tensor_tensor(Q[:, :], LB[P_ATT % 2][:, :], -(float(HD) ** -0.5), RS[:, :],
                                         ALU.mult, ALU.mult).then_inc(panel_free, 1)
                dve.wait_ge(chunk_used, C_ATT + 2 + c * 4)
                times_rms(P_ATT + 1, Z[:, 0, :]).then_inc(panel_free, 1)
                dve.wait_ge(dn_staged, c + 1)
                for e in range(2):
                    dve.wait_ge(s_done, fil + (e + 1))
                    pc = PC[:, e, :, 0:NCMP]
                    dve.tensor_tensor(pc, SB[(F_ATT + e) % 3][:, 0:P].rearrange("p (b i) -> p b i", b=TB)[:, :, 0:NCMP],
                                      DN[:, e, 512:640].rearrange("p (b i) -> p b i", b=TB)[:, :, 0:NCMP],
                                      ALU.add).then_inc(s_free, 1)
                    dve.wait_ge(s_free, fil + (e + 1))
                    dve.tensor_reduce(MC[:, e, :], pc, AX, ALU.min).then_inc(dve_step, st.add())
                    chain()
                    dve.tensor_tensor(pc, pc, MC[:, e, :].unsqueeze(2).broadcast_to((P, TB, NCMP)), ALU.subtract).then_inc(cmp_arg, 1)
                scores(0)
                gelu_a(c * 2 + 2, 0)
                for e in range(2):
                    dve.wait_ge(cmp_exp, c * 2 + (e + 1))
                    pc = PC[:, e, :, 0:NCMP]
                    dve.tensor_reduce(DC[:, e, :], pc, AX, ALU.add).then_inc(dve_step, st.add())
                    chain()
                    dve.reciprocal(RC[:, e, :], DC[:, e, :]).then_inc(dve_step, st.add())
                    chain()
                    gate = GT[:, :, bass.ds(c * 6 + 3 * e, 1)].rearrange("p b a -> p (b a)")
                    dve.tensor_tensor(RC[:, e, :], RC[:, e, :], gate, ALU.mult).then_inc(dve_step, st.add())
                    chain()
                    dve.tensor_tensor(RC[:, e, :], RC[:, e, :], cc("valid"), ALU.mult).then_inc(dve_step, st.add())
                    chain()
                    dve.tensor_tensor(pc, pc, RC[:, e, :].unsqueeze(2).broadcast_to((P, TB, NCMP)), ALU.mult).then_inc(cmp_ready, 1)
                dve.wait_ge(gelu_tanh, c * 2 + 2)
                dve.scalar_tensor_tensor(U[:, bass.ds(c, 1), :].rearrange("p a n -> p (a n)"), Z[:, 1, :], 1.0, Z[:, 0, :],
                                         ALU.add, ALU.mult).then_inc(gelu_done, 1)
                weigh(0)
                dve.wait_ge(chunk_used, C_ATT + 3 + c * 4)
                times_rms(P_ATT + 2, Z[:, 2, :]).then_inc(panel_free, 1)
                scores(1)
                gelu_a(c * 2 + 3, 2)
                weigh(1)
                scores(2)
                dve.wait_ge(gelu_tanh, c * 2 + 3)
                dve.scalar_tensor_tensor(Z[:, 3, :], Z[:, 3, :], 1.0, Z[:, 2, :], ALU.add, ALU.mult).then_inc(gelu_done, 1)
                weigh(2)
                scores(3)
                dve.wait_ge(chunk_used, C_ATT + 4 + c * 4)
                times_rms(P_ATT + 3, SIG[:, bass.ds(c, 1), :].rearrange("p a n -> p (a n)")).then_inc(panel_free, 1)
                weigh(3)
                dve.wait_ge(onhi_ready, c + 1)
                dve.tensor_tensor(ONL[:, bass.ds(c, 1), :].rearrange("p a n -> p (a n)"), OB[:, :],
                                  ONH[:, bass.ds(c, 1), :].rearrange("p a n -> p (a n)").bitcast(F32),
                                  ALU.subtract).then_inc(o_free, 1)
            st.leave(PAIRS)

            dve.wait_ge(r_free, R_CROSS)
            for b in range(TB):
                ins = dve.bn_stats(BN[:, b, :], VT[:, b, :])
            ins.then_inc(dve_step, st.add())
            chain()
            for b in range(TB):
                ins = dve.bn_aggr(BA[:, b, :], BN[:, b, :])
            ins.then_inc(ln_var, 1)
            dve.wait_ge(ln_std, 1)
            dve.reciprocal(LS[:, :], LS[:, :]).then_inc(dve_step, st.add())
            chain()
            for b in range(TB):
                dve.tensor_scalar(VT[:, b, :], VT[:, b, :], BA[:, b, 0:1], LS[:, b:b + 1], ALU.subtract,
                                  ALU.mult).then_inc(vn_ready, 1)

            def gate_in(sig, pan, chunk):
                dve.wait_ge(chunk_used, chunk + 1)
                times_rms(pan, SIG[:, sig, :]).then_inc(panel_free, 1)

            gate_in(4, P_MRG, C_MRG)
            gate_in(5, P_MRG + 1, C_MRG + 1)
            dve.wait_ge(bsp_loaded, 16)
            for g in range(4):
                n = F_SGU + g
                dve.wait_ge(s_done, n + 1)
                dve.scalar_tensor_tensor(Z[:, 0, :].rearrange("p (b t) -> p b t", b=TB), SB[n % 3][:, :].rearrange("p (b t) -> p b t", b=TB),
                                         cc("lng", g, g + 1), BB[:, g, :].unsqueeze(1).broadcast_to((P, TB, P)),
                                         ALU.mult, ALU.add).then_inc(s_free, 1)
                dve.wait_ge(s_free, n + 1)
                if g >= 2:
                    dve.wait_ge(oshi_ready, g - 1)
                dve.scalar_tensor_tensor(Z[:, 2 + g % 2, :], Z[:, 0, :], 0.5, U[:, g, :], ALU.mult, ALU.mult).then_inc(sgu_out, 1)
                dve.wait_ge(oshi_ready, g + 1)
                dve.tensor_tensor(OSL[:, g, :], Z[:, 2 + g % 2, :], OSH[:, g, :].bitcast(F32), ALU.subtract).then_inc(oslo_ready, 1)
            gate_in(6, P_MRG + 2, C_MRG + 2)
            gate_in(7, P_MRG + 3, C_MRG + 3)
            for half in range(2):
                for k in range(4):
                    n = 4 * half + k
                    pan = P_AB[n]
                    dve.wait_ge(sig_ready, PAIRS + 4 + 8 * half)
                    dve.wait_ge(panel_half, n + 1)
                    dve.scalar_tensor_tensor(Z[:, 2 * (k % 2), :], SIG[:, k, :], 1.0, LB[pan % 2][:, :], ALU.add, ALU.mult).then_inc(panel_free, 1)
                    dve.wait_ge(chunk_used, C_AB[n] + 1)
                    dve.scalar_tensor_tensor(Z[:, 2 * (k % 2) + 1, :], SIG[:, 4 + k, :], 1.0, LB[(pan + 1) % 2][:, :], ALU.add, ALU.mult).then_inc(panel_free, 1)
                    dve.wait_ge(panel_free, pan + 2)
                    dve.tensor_tensor(Z[:, 2 * (k % 2), :], Z[:, 2 * (k % 2), :], Z[:, 2 * (k % 2) + 1, :], ALU.add).then_inc(mix_ready, 1)
                    dve.wait_ge(mixhi_ready, n + 1)
                    dve.scalar_tensor_tensor(MXL[:, n, :], Z[:, 2 * (k % 2), :], 0.5, MXH[:, n, :].bitcast(F32),
                                             ALU.mult, ALU.subtract).then_inc(mixlo_ready, 1)
                if half == 0:
                    for k in range(4):
                        gate_in(k, P_MRG + 12 + k, C_MRG + 8 + k)
                    for k in range(4):
                        gate_in(4 + k, P_MRG + 16 + k, C_MRG + 12 + k)

            def clear_sum():
                dve.memset(ACC[:, :], 0.0).then_inc(dve_step, st.add())
                chain()

            clear_sum()
            dve.wait_ge(h_loaded, 16)
            with dve.Fori(0, 2) as r:
                for k in range(4):
                    n = r * 4 + k
                    hn = H[:, bass.ds(n, 1), :].rearrange("p a n -> p (a n)")
                    dve.wait_ge(chunk_used, n + (C_OUT + 1))
                    dve.tensor_tensor(hn, hn, LB[(P_OUT + k) % 2][:, :], ALU.add).then_inc(h_ready, 1)
                    dve.wait_ge(h_ready, n + 1)
                    dve.wait_ge(xhi_ready, n + (KT + 1))
                    dve.scalar_tensor_tensor(XL[:, bass.ds(n, 1), :].rearrange("p a n -> p (a n)"), hn,
                                             CST[:, bass.ds(n + COL["gq"][0], 1)],
                                             XH[:, bass.ds(n, 1), :].rearrange("p a n -> p (a n)").bitcast(F32),
                                             ALU.mult, ALU.subtract).then_inc(xlo_ready, 1)
                    dve.wait_ge(sq_ready, n + (KT + 1))
                    dve.wait_ge(acc_ready, n + KT)
                    dve.tensor_tensor(ACC[:, :], ACC[:, :], SQ[:, k % 2, :], ALU.add).then_inc(acc_ready, 1)

            inverse(3, RS[:, :])
            dve.wait_ge(s_free, F_QRMS + 1)
            def cross_q(n):
                dve.wait_ge(chunk_used, C_MQ + n + 1)
                dve.scalar_tensor_tensor(HQ[:, n % 2, :], LB[(P_MQ + n) % 2][:, :], -SC_MEM, RS[:, :],
                                         ALU.mult, ALU.mult).then_inc(panel_free, 1)

            def cross_max(n):
                for f in range(2):
                    k = F_CROSS + 2 * n + f
                    dve.wait_ge(s_done, k + 1)
                    j = 4 * (n % 2) + 2 * f
                    dve.tensor_reduce(MN[:, j:j + 2], SB[k % 3][:, :].rearrange("p (b m) -> p b m", b=2), AX,
                                      ALU.min).then_inc(p_max, 1)

            def cross_weigh(n):
                dve.wait_ge(s_free, F_CROSS + 2 * n + 2)
                j = 4 * (n % 2)
                dve.reciprocal(RD[:, j:j + 4], DEN[:, j:j + 4]).then_inc(dve_step, st.add())
                chain()
                for qb in range(TB):
                    ins = dve.tensor_scalar(P2[:, n % 2, qb, :], P2[:, n % 2, qb, :], RD[:, j + qb:j + qb + 1], None, ALU.mult)
                ins.then_inc(p_ready, 1)

            def cross_o_lo(n):
                dve.wait_ge(onhi_ready, PAIRS + n + 1)
                dve.tensor_tensor(OXL[:, n, :], OB[:, :], OXH[:, n, :].bitcast(F32), ALU.subtract).then_inc(o_free, 1)

            cross_q(0)
            for n in range(MH):
                cross_max(n)
                if n < 3:
                    cross_q(n + 1)
                cross_weigh(n)
                if n:
                    cross_o_lo(n - 1)
            cross_o_lo(3)
            clear_sum()
            for n in range(KT):
                if n % 2 == 0:
                    dve.wait_ge(panel_half, KT + n // 2 + 1)
                else:
                    dve.wait_ge(chunk_used, C_MO + n // 2 + 1)
                dve.tensor_tensor(H[:, n, :], H[:, n, :], LB[(P_MO + n) % 2][:, :], ALU.add).then_inc(h_ready, 1)
                dve.wait_ge(xhi_ready, 2 * KT + n + 1)
                dve.scalar_tensor_tensor(XL[:, n, :], H[:, n, :], cc("gf", n, n + 1), XH[:, n, :].bitcast(F32),
                                         ALU.mult, ALU.subtract).then_inc(xlo_ready, 1)
                add_square(2 * KT + n, False, n % 2)
            inverse(4, RS[:, :])
            dve.wait_ge(s_free, F_FRMS + 1)
            st_g = FREE_GU
            with dve.Fori(0, FT // 2) as r:
                st.enter(r, 2)
                for k in range(2):
                    j = r * 2 + k
                    zg, zt, zu = Z[:, 2 * k, :], Z[:, 2 * k + 1, :], SQ[:, k, :]
                    dve.wait_ge(chunk_used, r * 4 + (C_GU + 2 * k + 1))
                    times_rms(P_GU + 2 * k, zg).then_inc(panel_free, 1)
                    dve.wait_ge(act_tanh, j + 1)
                    dve.scalar_tensor_tensor(zt, zt, 1.0, zg, ALU.add, ALU.mult).then_inc(dve_step, st.add())
                    dve.wait_ge(chunk_used, r * 4 + (C_GU + 2 * k + 2))
                    times_rms(P_GU + 2 * k + 1, zu).then_inc(panel_free, 1)
                    chain()
                    dve.wait_ge(panel_free, r * 4 + (FREE_GU + 2 * k + 2))
                    dve.tensor_tensor(zg, zt, zu, ALU.mult).then_inc(hid_ready, 1)
                    dve.wait_ge(hidhi_ready, j + 1)
                    dve.scalar_tensor_tensor(HL[:, bass.ds(j, 1), :].rearrange("p a n -> p (a n)"), zg, 0.5,
                                             HH[:, bass.ds(j, 1), :].rearrange("p a n -> p (a n)").bitcast(F32),
                                             ALU.mult, ALU.subtract).then_inc(hidlo_ready, 1)
            st.leave(FT // 2)
            clear_sum()
            for n in range(KT):
                dve.wait_ge(chunk_used, C_DN + 3 * n + 3)
                dve.tensor_tensor(H[:, n, :], H[:, n, :], LB[(P_DN + n) % 2][:, :], ALU.add).then_inc(h_ready, 1)
                add_square(3 * KT + n, False, n % 2)
            inverse(5, RS[:, :])
            dve.wait_ge(s_free, F_ORMS + 1)
            for n in range(KT):
                dve.scalar_tensor_tensor(OUTT[:, n, :], H[:, n, :], cc("gfin", n, n + 1), RS[:, :],
                                         ALU.mult, ALU.mult).then_inc(out_ready, 1)

        @block.tensor
        def _(pe):
            def bank_free(p):
                q = p - 2
                if q < 0:
                    return None, 0
                if q < P_OUT:
                    return panel_free, q + 1
                if q < P_MQ:
                    return h_ready, q - P_OUT + 1
                if q < P_MO:
                    return panel_free, FREE_MQ + q - P_MQ + 1
                if q < P_GU:
                    return h_ready, KT + q - P_MO + 1
                if q < P_DN:
                    return panel_free, FREE_GU + q - P_GU + 1
                return h_ready, 2 * KT + q - P_DN + 1

            def panel(i, bank, units, w=T, shift=None, first=True, last=True, done=None):
                s = i % SLOTS
                pe.wait_ge(lo_ready, i + 1 if shift is None else shift + (i + 1))
                for m, (u, hi, lo) in enumerate(units):
                    end = last and m == len(units) - 1
                    dst = LB[bank][:, 0:w]
                    pe.matmul(dst, WH[:, s, u, :], hi, start=first and m == 0, stop=False)
                    pe.matmul(dst, WH[:, s, u, :], lo, start=False, stop=False)
                    ins = pe.matmul(dst, WL[:, s, u, :], hi, start=False, stop=end)
                ins.then_inc(chunk_used if done is None else done, 1)

            def free(p):
                s, v = bank_free(p)
                if s is not None:
                    pe.wait_ge(s, v)

            X = [(k, XH[:, k, :], XL[:, k, :]) for k in range(KT)]

            def s_bank(n, turn=None):
                if n >= 3:
                    pe.wait_ge(s_free, n - 2 if turn is None else turn * F_PAIR + (n - 2))
                return SB[n % 3]

            def r_bank(n, turn=None):
                if n >= 2:
                    pe.wait_ge(r_free, n - 1 if turn is None else turn * R_PAIR + (n - 1))
                return RB[n % 2]

            def mean_square(n, count):
                pe.wait_ge(acc_ready, count)
                pe.matmul(s_bank(n)[:, :], ONES[:, :], ACC[:, :], start=True, stop=True).then_inc(s_done, 1)

            M = [(k, MHH[:, k, :], MHL[:, k, :]) for k in range(KT)]
            pe.wait_ge(ones_ready, 1)

            def memory_turn(n):
                pe.wait_ge(panel_free, MH + n + 1)
                bank = r_bank(R_MEM + n)
                for b in range(MB):
                    ins = pe.transpose(bank[:, b * P:(b + 1) * P], Z[:, n % 2, b * P:(b + 1) * P], IDENT)
                ins.then_inc(r_done, 1)

            for i in range(N_MEM):
                if i == 0:
                    pe.wait_ge(memlo_ready, KT)
                free(i)
                panel(C_MEM + i, i % 2, M, MEM)
                if i == 0:
                    pe.wait_ge(memsq_ready, 1)
                    for k in range(KT):
                        ins = pe.matmul(SB[F_MEMRMS][:, 0:MEM], ONES[:, :], MSQ[:, k, :], start=k == 0, stop=k == KT - 1)
                    ins.then_inc(s_done, 1)
                if i > MH:
                    memory_turn(i - MH - 1)
            mean_square(F_XRMS, KT)
            pe.wait_ge(xlo_ready, KT)

            def turn_values(n, p, z):
                pe.wait_ge(panel_free, p + 1)
                bank = r_bank(n)
                for b in range(TB):
                    ins = pe.transpose(bank[:, b * P:(b + 1) * P], Z[:, z, b * P:(b + 1) * P], IDENT)
                ins.then_inc(r_done, 1)

            for j in range(N_IN):
                i = C_IN + j
                free(i)
                panel(i, i % 2, X)
                if j == 0:
                    memory_turn(3)
                if j == 3:
                    pe.wait_ge(w1_loaded, 16)
                    pe.wait_ge(g_ready, 2)
                    bank = s_bank(F_HID)
                    for s in range(2):
                        for u in range(CJ):
                            ins = pe.matmul(bank[:, s * 2 * NCMP:(s + 1) * 2 * NCMP], W1[:, s, u, :], G[:, s, u, :],
                                            start=u == 0, stop=u == CJ - 1)
                    ins.then_inc(s_done, 1)
                if j == 4:
                    turn_values(R_SLC, C_IN + 3, 2)
                    pe.wait_ge(gelu_done, 1)
                    bank = s_bank(F_CMP)
                    pe.matmul(bank[:, 0:2 * NCMP], cc("w2k"), HZ[:, 1, 0:2 * NCMP], start=True, stop=True)
                    for g in range(2):
                        a = (2 + g) * NCMP
                        ins = pe.matmul(bank[0:NCMP, P + g * HD:P + (g + 1) * HD], HZ[:, 1, a:a + NCMP], cc("w2v"),
                                        start=True, stop=True)
                    ins.then_inc(s_done, 1)
            turn_values(R_WIN, C_IN + 5, 3)
            pe.wait_ge(panel_free, C_IN + 7)
            bank = r_bank(R_GATE)
            for b in range(TB):
                ins = pe.transpose(bank[:, b * 24:(b + 1) * 24], Z[0:24, 0, b * P:(b + 1) * P], IDENT[0:24, 0:24])
            ins.then_inc(r_done, 1)

            with pe.Fori(0, PAIRS) as c:
                def att_panel(k):
                    p = P_ATT + k
                    pe.wait_ge(panel_free, c * 4 + (p - 1))
                    panel(C_ATT + k, p % 2, X, shift=c * 4)

                def scores(u):
                    e, off = u // 2, (KS, KW)[u % 2]
                    for qb in range(TB):
                        bank = s_bank(F_ATT + 2 + 4 * u + qb, c)
                        w = (qb + 1) * P
                        pe.matmul(bank[:, 0:w], Q[e * HD:(e + 1) * HD, qb * P:(qb + 1) * P],
                                  KVS[e * HD:(e + 1) * HD, off:off + w], start=True, stop=True).then_inc(s_done, 1)

                def turn(u):
                    for f, kbs in enumerate(((0,), (1, 3), (2,))):
                        k = 2 + 3 * u + f + (2 if u >= 2 else 0)
                        bank = r_bank(R_ATT + k, c)
                        if f == 0:
                            pe.wait_ge(p_ready, c * 4 + (u + 1))
                        at_ = 0
                        for kb in kbs:
                            for qb in range(kb, TB):
                                ins = pe.transpose(bank[:, at_:at_ + P], PP[:, u % 2, unit_off(qb) + kb * P:unit_off(qb) + (kb + 1) * P], IDENT)
                                at_ += P
                        ins.then_inc(r_done, 1)

                def values(u):
                    e, off = u // 2, (VS, VW)[u % 2]
                    for f, kbs in enumerate(((0,), (1, 3), (2,))):
                        k = R_ATT + 2 + 3 * u + f + (2 if u >= 2 else 0)
                        pe.wait_ge(r_free, c * R_PAIR + (k + 1))
                        for kb in kbs:
                            ins = pe.matmul(OB[e * HD:(e + 1) * HD, kb * P:T], KVS[:, off + kb * HD:off + (kb + 1) * HD],
                                            PT[:, u % 2, row_off(kb):row_off(kb) + (TB - kb) * P],
                                            start=False, stop=u % 2 == 1 and kb == 2, skip_group_check=True)
                    if u == 3:
                        ins.then_inc(o_done, 1)

                att_panel(0)
                att_panel(1)
                pe.wait_ge(panel_free, c * 4 + (P_ATT + 1))
                pe.wait_ge(kv_staged, c + 1)
                for e in range(2):
                    bank = s_bank(F_ATT + e, c)
                    for qb in range(TB):
                        ins = pe.matmul(bank[:, qb * 32:qb * 32 + NCMP], Q[e * HD:(e + 1) * HD, qb * P:(qb + 1) * P],
                                        KVS[e * HD:(e + 1) * HD, KC_:KC_ + NCMP], start=True, stop=True)
                    ins.then_inc(s_done, 1)
                scores(0)
                att_panel(2)
                scores(1)
                for e in range(2):
                    pe.wait_ge(cmp_ready, c * 2 + (e + 1))
                    bank = r_bank(R_ATT + e, c)
                    for qb in range(TB):
                        ins = pe.transpose(bank[0:NCMP, qb * P:(qb + 1) * P], PC[:, e, qb, 0:NCMP], IDENT)
                    ins.then_inc(r_done, 1)
                turn(0)
                for e in range(2):
                    pe.wait_ge(r_free, c * R_PAIR + (R_ATT + e + 1))
                    pe.matmul(OB[e * HD:(e + 1) * HD, :], KVS[0:NCMP, VC_:VC_ + HD], PCT[:, e, :], start=True, stop=False,
                              skip_group_check=True)
                values(0)
                scores(2)
                turn(1)
                values(1)
                pe.wait_ge(gelu_done, c * 2 + 3)
                for a in range(2):
                    bank = r_bank(R_ATT + 8 + a, c)
                    for b in range(2):
                        tb = 2 * a + b
                        ins = pe.transpose(bank[:, b * P:(b + 1) * P], Z[:, 3, tb * P:(tb + 1) * P], IDENT)
                    ins.then_inc(r_done, 1)
                scores(3)
                att_panel(3)
                turn(2)
                values(2)
                turn(3)
                values(3)

            def x_panel(i, p):
                free(p)
                panel(i, p % 2, X)

            def two_panels(n):
                free(P_AB[n])
                panel(C_AB[n], P_AB[n] % 2, [(k, ONH[:, k, :], ONL[:, k, :]) for k in range(4)], done=panel_half)
                free(P_AB[n] + 1)
                panel(C_AB[n], (P_AB[n] + 1) % 2, [(4 + k, OSH[:, k, :], OSL[:, k, :]) for k in range(4)])

            for k in range(4):
                x_panel(C_MRG + k, P_MRG + k)
                if k == 1:
                    pe.wait_ge(vn_ready, TB)
                    for g in range(4):
                        bank = s_bank(F_SGU + g)
                        ws, _ = COL["ws"]
                        for b in range(TB):
                            ins = pe.matmul(bank[:, b * P:(b + 1) * P], VT[:, b, g * P:(g + 1) * P],
                                            CST[:, ws + g * P:ws + (g + 1) * P], start=True, stop=True)
                        ins.then_inc(s_done, 1)
            pe.wait_ge(o_free, PAIRS + 1)
            pe.wait_ge(oslo_ready, 4)
            for n in range(4):
                two_panels(n)
            for k in range(8):
                x_panel(C_MRG + 8 + k, P_MRG + 12 + k)
            for n in range(4, 8):
                two_panels(n)
            MX = [(k, MXH[:, k, :], MXL[:, k, :]) for k in range(KT)]
            pe.wait_ge(mixlo_ready, KT)
            for j in range(KT):
                free(P_OUT + j)
                panel(C_OUT + j, (P_OUT + j) % 2, MX)

            def cross_scores(n):
                pe.wait_ge(panel_free, FREE_MQ + n + 1)
                for f in range(2):
                    bank = s_bank(F_CROSS + 2 * n + f)
                    for b in range(2):
                        qb = 2 * f + b
                        ins = pe.matmul(bank[:, b * MEM:(b + 1) * MEM], HQ[:, n % 2, qb * P:(qb + 1) * P], MK[:, n, :],
                                        start=True, stop=True)
                    ins.then_inc(s_done, 1)

            def cross_turn(n):
                pe.wait_ge(p_ready, 16 + n + 1)
                for b in range(MB):
                    bank = r_bank(R_CROSS + 2 * n + b)
                    for qb in range(TB):
                        ins = pe.transpose(bank[:, qb * P:(qb + 1) * P], P2[:, n % 2, qb, b * P:(b + 1) * P], IDENT)
                    ins.then_inc(r_done, 1)

            def cross_values(n):
                pe.wait_ge(o_free, PAIRS + n + 1)
                for b in range(MB):
                    pe.wait_ge(r_free, R_CROSS + 2 * n + b + 1)
                    ins = pe.matmul(OB[:, :], MV[:, b, n * P:(n + 1) * P], PT2[:, n % 2, b, :], start=b == 0, stop=b == MB - 1)
                ins.then_inc(o_done, 1)

            def mq_panel(n):
                free(P_MQ + n)
                panel(C_MQ + n, (P_MQ + n) % 2, X)

            pe.wait_ge(xlo_ready, 2 * KT)
            mq_panel(0)
            mean_square(F_QRMS, 2 * KT)
            mq_panel(1)
            cross_scores(0)
            mq_panel(2)
            cross_turn(0)
            cross_scores(1)
            cross_values(0)
            mq_panel(3)
            cross_turn(1)
            cross_scores(2)
            cross_values(1)
            cross_turn(2)
            cross_scores(3)
            cross_values(2)
            cross_turn(3)
            cross_values(3)
            pe.wait_ge(o_free, PAIRS + MH + 1)
            for m in range(KT // 2):
                for b in range(2):
                    free(P_MO + 2 * m + b)
                    panel(C_MO + m, (P_MO + b) % 2, [(4 * b + k, OXH[:, k, :], OXL[:, k, :]) for k in range(4)],
                          done=panel_half if b == 0 else None)
            pe.wait_ge(xlo_ready, 3 * KT)
            for j in range(2):
                free(P_GU + j)
                panel(C_GU + j, (P_GU + j) % 2, X)
                if j == 0:
                    mean_square(F_FRMS, 3 * KT)
            for j in range(2, 4):
                free(P_GU + j)
                panel(C_GU + j, (P_GU + j) % 2, X)
            with pe.Fori(1, FT // 2) as r:
                for j in range(4):
                    pe.wait_ge(panel_free, r * 4 + (FREE_GU + j - 1))
                    panel(C_GU + j, (P_GU + j) % 2, X, shift=r * 4)
            pe.wait_ge(hidlo_ready, FT)
            HID = [(k % KT, HH[:, k, :], HL[:, k, :]) for k in range(FT)]

            def down(n, shift=None):
                for m in range(3):
                    panel(C_DN + 3 * n + m, (P_DN + n) % 2, HID[KT * m:KT * (m + 1)], shift=shift,
                          first=m == 0, last=m == 2)

            for n in range(2):
                free(P_DN + n)
                down(n)
            for n in range(2, KT):
                free(P_DN + n)
                down(n)
            mean_square(F_ORMS, 4 * KT)


def arena_base(nc, arena, total):
    return nc.sbuf_base - 4 * total


def kernel(**inputs):
    import concourse.bacc as bacc
    from concourse import mybir
    from concourse.bass_utils import run_bass_kernel_spmd

    f = {k: np.asarray(v) for k, v in inputs.items()}

    def tiles(w):
        k, n = w.shape
        return w.reshape(k // P, P, n // P, P).transpose(2, 1, 0, 3)

    w_in = f["w_in"][0]
    win = tiles(w_in[:, :2304])
    gates = np.zeros((D, P), w_in.dtype)
    gates[:, 0:24] = w_in[:, 2304:2328]
    mrg, mkv = tiles(f["w_merge"][0]), tiles(f["w_mkv"][0])
    pa, pb = tiles(f["w_proj_a"][0]), tiles(f["w_proj_b"][0])
    wo, mq, mo = tiles(f["w_out"][0]), tiles(f["w_mq"][0]), tiles(f["w_mo"][0])
    gu, dn = tiles(f["w_gate_up"][0]), tiles(f["w_down"][0])
    pack = np.zeros((NCHUNK, P, KT, P), w_in.dtype)
    at = 0

    def put(x, u0=0):
        nonlocal at
        pack[at, :, u0:u0 + x.shape[1]] = x
        at += 1

    for n in range(8):
        put(mkv[n])
    for n in range(4, 10):
        put(win[n])
    put(tiles(gates)[0])
    for c in range(PAIRS):
        put(win[c])
        put(win[10 + c])
        put(win[14 + c])
        put(mrg[c])
    for half in range(2):
        if half:
            for n in range(4, 8):
                put(mrg[n])
        for n in range(4 * half, 4 * half + 4):
            put(mrg[KT + n])
        for n in range(4 * half, 4 * half + 4):
            pack[at, :, 0:4] = pa[n]
            put(pb[n], 4)
    for n in range(8):
        put(wo[n])
    for n in range(MH):
        put(mq[n])
    for m in range(4):
        pack[at, :, 0:4] = mo[2 * m]
        put(mo[2 * m + 1], 4)
    for j in range(FT):
        put(gu[j])
        put(gu[FT + j])
    for n in range(KT):
        for m in range(3):
            put(dn[n][:, KT * m:KT * (m + 1)])
    assert at == NCHUNK

    cst = np.zeros((P, NCOL), w_in.dtype)

    def col(name, a):
        c, w = COL[name]
        cst[:a.shape[0], c:c + w] = a.reshape(a.shape[0], w)

    def by_tile(v):
        return v.reshape(-1, P).T

    col("gmix", by_tile(f["norm_mix"][0]))
    col("gmem", by_tile(f["norm_mem_kv"][0]))
    col("gq", by_tile(f["norm_mem_q"][0]))
    col("gf", by_tile(f["norm_ffn"][0]))
    col("gfin", by_tile(f["norm_final"]))
    col("bm", by_tile(f["b_merge"][0]))
    col("lng", by_tile(f["ln_sgu"][0]))
    col("slope", np.broadcast_to(2.0 ** -(np.arange(8) + 1.0), (P, 8)))
    p = np.arange(P)[:, None]
    col("valid", (np.arange(TB)[None] * P + p >= 31).astype(np.float32))
    col("eps", np.full((P, 1), 1e-6))
    col("eps4", np.full((P, 1), 4e-6))
    col("w2k", np.concatenate([f["w_cmp_k2"][0]] * 2, axis=1))
    col("w2v", f["w_cmp_v2"][0])
    pes = np.stack([f["pe_cmp_k"][0], f["pe_cmp_v"][0]]).reshape(2, CJ, 2, HD).transpose(3, 0, 2, 1).reshape(HD, 64)
    col("pe", np.concatenate([pes, pes]))
    col("ident", np.eye(P))
    col("tri", np.arange(P)[None] >= p)
    x = np.arange(T)[None]
    tab = np.where(384 + p - x >= 0, 384 + p - x, MASKED)
    qb, i = np.arange(TB)[:, None], np.arange(32)[None]
    dist = (P * qb + np.arange(P)[:, None, None] - (16 * i + 31)[None]).reshape(P, P)
    tabc = np.where((dist >= 0) & (np.arange(P)[None] % 32 < NCMP), dist, MASKED)
    col("tab", np.concatenate([tab, tabc], axis=1))
    col("ws", f["w_spatial"][0].transpose(2, 0, 1))

    w1 = np.stack([f["w_cmp_k1"][0], f["w_cmp_v1"][0]]).reshape(2, CJ, P, P).transpose(2, 0, 1, 3)
    arrays = {
        "wpk": pack.reshape(NCHUNK, P, CW),
        "xT": np.ascontiguousarray(f["x"][0].T.reshape(KT, P, T).transpose(1, 0, 2)),
        "memT": np.ascontiguousarray(f["mem"][0].T.reshape(KT, P, MEM).transpose(1, 0, 2)),
        "w1": np.ascontiguousarray(w1),
        "cst": cst,
        "bsp": np.ascontiguousarray(f["b_spatial"][0]),
    }
    nc = bacc.Bacc("TRN2", target_bir_lowering=False, num_devices=1)
    dt = mybir.dt.float32
    args = [nc.dram_tensor(n, a.shape, dt, kind="ExternalInput").ap() for n, a in arrays.items()]
    out = nc.dram_tensor("out", (P, KT, T), dt, kind="ExternalOutput").ap()
    build(nc, *args, out)
    got = run_bass_kernel_spmd(nc, [arrays], core_ids=[0]).results[0]["out"]
    return np.ascontiguousarray(got.transpose(1, 0, 2).reshape(D, T).T)[None]
```

```python
from contextlib import ExitStack

import numpy as np

P = 128
T = 512
D = 1024
KT = D // P
TB = T // P
HD = 64
PAIRS = 4
NCMP = 31
CJ = 16
MEM = 256
MB = MEM // P
MH = 4
FT = 2816 // P
SLOTS = 4
CW = KT * P

C_IN, N_IN = 0, 7
C_ATT = C_IN + N_IN
N_ATT = 4 * PAIRS
C_MRG = C_ATT + N_ATT
N_MRG = 20
C_OUT = C_MRG + N_MRG
CROSS = ("k0", "k1", "q0", "v0", "q1", "v1", "k2", "q2", "v2", "k3", "q3", "v3")
C_X = C_OUT + KT
C_MO = C_X + len(CROSS)
C_GU = C_MO + KT // 2
C_DN = C_GU + 2 * FT
NCHUNK = C_DN + 3 * KT

P_ATT = C_ATT
P_MRG = C_MRG
P_OUT = P_MRG + 28
P_X = P_OUT + KT
P_MO = P_X + len(CROSS)
P_GU = P_MO + KT
P_DN = P_GU + 2 * FT
C_AB = [C_MRG + 4 + n for n in range(4)] + [C_MRG + 16 + n for n in range(4)]
P_AB = [P_MRG + 4 + 2 * n for n in range(4)] + [P_MRG + 20 + 2 * n for n in range(4)]
FREE_X = P_OUT
FREE_GU = FREE_X + len(CROSS)

F_XRMS, F_HID, F_CMP = 0, 1, 2
F_ATT, F_PAIR = 3, 18
F_SGU = F_ATT + F_PAIR * PAIRS
F_MEMRMS = F_SGU + 4
F_QRMS = F_MEMRMS + 1
F_CROSS = F_QRMS + 1
F_FRMS = F_CROSS + 2 * MH
F_ORMS = F_FRMS + 1
R_SLC, R_WIN, R_GATE = 0, 1, 2
R_ATT, R_PAIR = 3, 16
R_X = R_ATT + R_PAIR * PAIRS
R_VT = [R_X + n for n in (0, 5, 6, 9)]
R_CT = [R_X + n for n in (1, 3, 7, 10)]

KS, KW, KC_ = 0, T, 2 * T
KEYW = KC_ + 32
VS, VW, VC_ = 0, 256, 512
KVW = VC_ + HD

_cols = [("gmix", KT), ("eps", 1), ("eps4", 1), ("gmem", KT), ("gq", KT), ("gf", KT), ("gfin", KT),
         ("bm", 2 * KT), ("lng", 4), ("slope", 8), ("valid", TB), ("w2k", P), ("w2v", HD), ("pe", 64),
         ("ident", P), ("tri", P), ("tab", 640), ("ws", 4 * P)]
COL, NCOL = {}, 0
for _n, _w in _cols:
    COL[_n] = (NCOL, _w)
    NCOL += _w
NCOL += -NCOL % 8
FEW = COL["w2k"][0]
MASKED = 1e32
SC_MEM = float(P) ** -0.5
GC, GA = 0.7978845608028654, 0.044715


def unit_off(qb):
    return P * qb * (qb + 1) // 2


def row_off(kb):
    return sum((TB - k) * P for k in range(kb))


TURNS = (0,), (1, 3), (2,)


def turn_fill(u, f):
    return 2 + 3 * u + f + (2 if u >= 2 else 0)


class Steps:

    def __init__(self):
        self.base, self.k, self.turn = 0, 0, None

    def add(self):
        self.k += 1
        return 1

    def now(self):
        return self.base + self.k if self.turn is None else self.base + self.k + self.turn * self.per

    def enter(self, turn, per):
        self.base, self.k, self.turn, self.per = self.base + self.k, 0, turn, per

    def leave(self, turns):
        assert self.k == self.per, (self.k, self.per)
        self.base, self.k, self.turn = self.base + self.per * turns, 0, None


def build(nc, wpk, xT, memT, w1d, cst, bsp, out):
    import concourse.bass as bass
    from concourse import mybir

    F32, F32R = mybir.dt.float32, mybir.dt.float32r
    ALU, ACT, AX = mybir.AluOpType, mybir.ActivationFunctionType, mybir.AxisListType.X

    with ExitStack() as ctx:
        total = 52800
        arena = ctx.enter_context(nc.sbuf_tensor("arena", [P, total], F32))
        base = arena_base(nc, arena, total)

        def at(name, off, shape, dt=F32):
            n = int(np.prod(shape[1:]))
            assert off + n <= total, (name, off + n)
            return nc.alloc_sbuf_tensor_at(name, shape, dt, offset=base + 4 * off)

        def sem(name):
            return ctx.enter_context(nc.semaphore(name))

        o = 0
        WRAW = at("w_raw", o, [P, SLOTS, KT, P])
        WL = at("w_lo", o, [P, SLOTS, KT, P], F32R)
        o += SLOTS * CW
        WH = at("w_hi", o, [P, SLOTS, KT, P], F32R)
        o += SLOTS * CW
        XH = at("x_hi", o, [P, KT, T], F32R)
        OUTT = at("out_t", o, [P, KT, T])
        o += KT * T
        XL = at("x_lo", o, [P, KT, T], F32R)
        o += KT * T
        CST = at("cst", o, [P, NCOL])
        o += NCOL
        ONES = at("ones", o, [P, P]); o += P
        RS = at("rs", o, [P, T]); o += T
        RSM = at("rs_mem", o, [P, MEM]); o += MEM
        ACC = at("acc", o, [P, T]); o += T
        SQ = at("sq", o, [P, 2, T]); o += 2 * T
        Z = at("z", o, [P, 4, T]); o += 4 * T
        BH = at("bh", o, [P, 2 * KT]); o += 2 * KT
        BB = at("bb", o, [P, 4, P]); o += 4 * P
        GT = at("gt", o, [P, TB, 24]); o += TB * 24
        MN = at("mn", o, [P, 16]); o += 16
        DEN = at("den", o, [P, 16]); o += 16
        RD = at("rd", o, [P, 16]); o += 16
        MC = at("mc", o, [P, 2, TB]); o += 8
        DC = at("dc", o, [P, 2, TB]); o += 8
        RC = at("rc", o, [P, 2, TB]); o += 8
        HOLD = at("hold", o, [P, 16]); o += 16
        BN = at("bn", o, [P, TB, 6]); o += TB * 6
        BA = at("ba", o, [P, TB, 2]); o += TB * 2
        LS = at("ls", o, [P, TB]); o += 8
        z0 = o
        H = at("h", z0, [P, KT, T])
        U = at("u", z0, [P, 4, T])
        VT = at("v_tok", z0 + 2048, [P, TB, T])
        MK = at("mk", z0 + 4096, [P, MH, MEM])
        MV = at("mv", z0 + 5120, [P, MB, MH * P])
        z = z0 + 6144
        ONH = at("on_hi", z, [P, PAIRS, T], F32R)
        ONL = at("on_lo", z + 2048, [P, PAIRS, T], F32R)
        W1 = at("w1", z, [P, 2, CJ, P])
        OXH = at("ox_hi", z, [P, MH, T], F32R)
        OXL = at("ox_lo", z + 2048, [P, MH, T], F32R)
        SIG = at("sig", z + 4096, [P, 8, T])
        P2 = at("p2", z + 4096, [P, 2, TB, MEM])
        PT2 = at("pt2", z + 6144, [P, 2, MB, T])
        KH = at("keys_hi", z + 6144, [P, 2, KEYW], F32R)
        KV = at("values", z + 8256, [P, 2, KVW])
        KVS = at("pair_values", z + 9408, [P, KVW])
        QS = at("q_split", z + 9984, [P, 2, T], F32R)
        KR = at("keys_raw", z + 11008, [P, 2, KEYW])
        KL = at("keys_lo", z + 11008, [P, 2, KEYW], F32R)
        Q = at("q", z + 13120, [P, T])
        G = at("g", z + 13632, [P, 2, CJ, 2 * NCMP])
        KC = at("kc", z + 16192, [P, 2, T])
        HZ = at("hz", z + 17216, [P, 2, 4 * NCMP])
        PP = at("pp", z + 13632, [P, 2, 1280])
        PT = at("pt", z + 16192, [P, 2, 1280])
        PC = at("pc", z + 18752, [P, 2, TB, 32])
        PCT = at("pct", z + 19008, [P, 2, T])
        DN = at("dn", z + 20032, [P, 2, 640])
        MRAW = at("mem_raw", z + 20480, [P, KT, MEM])
        MSQ = at("mem_sq", z + 4096, [P, KT, MEM])
        MSUM = at("mem_sum", z + 6144, [P, MEM])
        MHH = at("mem_hi", z + 8192, [P, KT, MEM], F32R)
        MHL = at("mem_lo", z + 10240, [P, KT, MEM], F32R)
        OSH = at("os_hi", z + 8192, [P, 4, T], F32R)
        OSL = at("os_lo", z + 10240, [P, 4, T], F32R)
        MXH = at("mix_hi", z + 12288, [P, KT, T], F32R)
        MXL = at("mix_lo", z + 16384, [P, KT, T], F32R)
        HQ = at("hq", z + 20480, [P, 2, T])
        HH = at("hid_hi", z, [P, FT, T], F32R)
        HL = at("hid_lo", z + FT * T, [P, FT, T], F32R)

        def cc(name, a=0, b=None):
            c, w = COL[name]
            return CST[:, c + a:c + (w if b is None else b)]

        IDENT = cc("ident")

        LB = [ctx.enter_context(nc.psum_tensor(f"lin{i}", [P, T], F32)) for i in range(2)]
        SB = [ctx.enter_context(nc.psum_tensor(f"score{i}", [P, T], F32)) for i in range(3)]
        RB = [ctx.enter_context(nc.psum_tensor(f"turn{i}", [P, T], F32)) for i in range(2)]
        OB = ctx.enter_context(nc.psum_tensor("heads", [P, T], F32))

        w_loaded = [sem(f"w_loaded{s}") for s in range(SLOTS)]
        hi_ready = sem("hi_ready")
        lo_ready = sem("lo_ready")
        chunk_used = sem("chunk_used")
        cst_loaded, mem_loaded = sem("cst_loaded"), sem("mem_loaded")
        tables_loaded = sem("tables_loaded")
        x_loaded = [sem(f"x_loaded{m}") for m in range(KT // 2)]
        w1_loaded, bsp_loaded, h_loaded = sem("w1_loaded"), sem("bsp_loaded"), sem("h_loaded")
        ones_ready = sem("ones_ready")
        memhi_ready, memlo_ready, memsq_ready = sem("memhi_ready"), sem("memlo_ready"), sem("memsq_ready")
        memsum_ready = sem("memsum_ready")
        xhi_ready, xlo_ready = sem("xhi_ready"), sem("xlo_ready")
        sq_ready, acc_ready = sem("sq_ready"), sem("acc_ready")
        h_ready = sem("h_ready")
        rms_ready = sem("rms_ready")
        panel_half = sem("panel_half")
        panel_free = sem("panel_free")
        s_done, s_free = sem("s_done"), sem("s_free")
        r_done, r_free = sem("r_done"), sem("r_free")
        o_done, o_free = sem("o_done"), sem("o_free")
        gelu_sq, gelu_arg, gelu_tanh, gelu_done = sem("gelu_sq"), sem("gelu_arg"), sem("gelu_tanh"), sem("gelu_done")
        g_ready = sem("g_ready")
        kv_staged, dn_staged = sem("kv_staged"), sem("dn_staged")
        keyhi_ready, keylo_ready = sem("keyhi_ready"), sem("keylo_ready")
        qhi_ready, q_ready = sem("qhi_ready"), sem("q_ready")
        cmp_arg, cmp_exp, cmp_ready = sem("cmp_arg"), sem("cmp_exp"), sem("cmp_ready")
        p_max, p_exp, p_ready = sem("p_max"), sem("p_exp"), sem("p_ready")
        sig_ready = sem("sig_ready")
        onhi_ready, onlo_ready = sem("onhi_ready"), sem("onlo_ready")
        ln_var, ln_std, vn_ready = sem("ln_var"), sem("ln_std"), sem("vn_ready")
        sgu_out, oshi_ready, oslo_ready = sem("sgu_out"), sem("oshi_ready"), sem("oslo_ready")
        mix_ready, mixhi_ready, mixlo_ready = sem("mix_ready"), sem("mixhi_ready"), sem("mixlo_ready")
        act_tanh = sem("act_tanh")
        hid_ready, hidhi_ready, hidlo_ready = sem("hid_ready"), sem("hidhi_ready"), sem("hidlo_ready")
        dve_step = sem("dve_step")
        gates_ready = sem("gates_ready")
        out_ready, out_stored = sem("out_ready"), sem("out_stored")

        block = ctx.enter_context(nc.Block())

        def chunk_slot(i):
            return i % SLOTS

        @block.sync
        def _(sp):
            def load(i, s):
                sp.dma_start(WRAW[:, s, :, :], wpk[i].rearrange("p (u c) -> p u c", u=KT)).then_inc(w_loaded[s], 16)

            for i in range(SLOTS):
                load(i, i)
            with sp.Fori(1, NCHUNK // SLOTS) as g:
                for s in range(SLOTS):
                    sp.wait_ge(chunk_used, g * SLOTS + (s + 1 - SLOTS))
                    sp.dma_start(WRAW[:, s, :, :], wpk[bass.ds(g * SLOTS + s, 1), :, :].rearrange(
                        "a p (u c) -> p (a u) c", u=KT)).then_inc(w_loaded[s], 16)
            for i in range(NCHUNK // SLOTS * SLOTS, NCHUNK):
                sp.wait_ge(chunk_used, i + 1 - SLOTS)
                load(i, i % SLOTS)
            for m in range(4):
                sp.wait_ge(out_ready, 2 * m + 2)
                sp.dma_start(out[:, 2 * m:2 * m + 2, :], OUTT[:, 2 * m:2 * m + 2, :]).then_inc(out_stored, 16)
            sp.wait_ge(out_stored, 64)

        @block.gpsimd
        def _(pool):
            pool.memset(ONES[:, :], 1.0 / D).then_inc(ones_ready, 1)
            pool.memset(PCT[:, :, :], 0.0).then_inc(ones_ready, 1)

            def split(i, s):
                pool.wait_ge(hi_ready, i + 1)
                pool.tensor_tensor(WL[:, s, :, :], WRAW[:, s, :, :], WH[:, s, :, :].bitcast(F32),
                                   ALU.subtract).then_inc(lo_ready, 1)

            with pool.Fori(0, NCHUNK // SLOTS) as g:
                for s in range(SLOTS):
                    split(g * SLOTS + s, s)
            for i in range(NCHUNK // SLOTS * SLOTS, NCHUNK):
                split(i, i % SLOTS)

        @block.scalar
        def _(act):
            act.dma_start(CST[:, 0:FEW], cst[:, 0:FEW]).then_inc(cst_loaded, 16)
            for m in range(KT // 2):
                act.dma_start(H[:, 2 * m:2 * m + 2, :], xT[:, 2 * m:2 * m + 2, :]).then_inc(x_loaded[m], 16)
            act.dma_start(CST[:, FEW:NCOL], cst[:, FEW:NCOL]).then_inc(tables_loaded, 16)
            act.dma_start(W1[:, :, :, :], w1d).then_inc(w1_loaded, 16)
            act.dma_start(BB[:, :, :], bsp.partition_broadcast(P)).then_inc(bsp_loaded, 16)

            def w_hi(i, s=None, turn=None):
                s = i % SLOTS if s is None else s
                act.wait_ge(w_loaded[s], 16 * (i // SLOTS + 1) if turn is None else turn)
                act.activation(WH[:, s, :, :], WRAW[:, s, :, :], ACT.Copy).then_inc(hi_ready, 1)

            def root(n, width, eps_bank, dst):
                act.wait_ge(s_done, n + 1)
                act.activation(dst, eps_bank[:, 0:width], ACT.Sqrt, bias=cc("eps")).then_inc(rms_ready, 1)

            def square(n):
                if n >= 2:
                    act.wait_ge(acc_ready, n - 1)
                act.activation(SQ[:, n % 2, :], H[:, n, :], ACT.Square).then_inc(sq_ready, 1)

            w_hi(0)
            act.wait_ge(cst_loaded, 16)
            for n in range(KT):
                act.wait_ge(x_loaded[n // 2], 16)
                act.activation(XH[:, n, :], H[:, n, :], ACT.Copy, scale=cc("gmix", n, n + 1)).then_inc(xhi_ready, 1)
                if n == 3:
                    w_hi(1)
                if n >= 4:
                    square(n - 4)
            w_hi(2)
            for n in range(4, KT):
                square(n)
            root(F_XRMS, T, SB[F_XRMS % 3], RS[:, :])
            for i in range(3, 7):
                w_hi(i)
            act.wait_ge(s_free, F_HID + 1)
            act.activation(HZ[:, 1, :], HZ[:, 0, :], ACT.Square).then_inc(gelu_sq, 1)
            act.wait_ge(gelu_arg, 1)
            act.activation(HZ[:, 1, :], HZ[:, 1, :], ACT.Tanh, scale=GC).then_inc(gelu_tanh, 1)

            def turned_values(n, off):
                act.wait_ge(r_done, n + 1)
                for g in range(2):
                    ins = act.activation(KV[:, g, off:off + TB * HD].rearrange("p (b d) -> p b d", b=TB),
                                         RB[n % 2][:, :].rearrange("p (b g d) -> p g b d", b=TB, g=2)[:, g, :, :],
                                         ACT.Copy)
                ins.then_inc(r_free, 1)

            def keys_hi(off, width):
                act.activation(KH[:, :, off:off + width], KR[:, :, off:off + width], ACT.Copy).then_inc(keyhi_ready, 1)

            turned_values(R_SLC, VS)
            act.wait_ge(panel_free, C_IN + 3)
            keys_hi(KS, T)
            w_hi(7)
            act.wait_ge(panel_free, C_IN + 5)
            keys_hi(KW, T)
            turned_values(R_WIN, VW)
            act.wait_ge(s_free, F_CMP + 1)
            keys_hi(KC_, 32)
            w_hi(8)
            act.wait_ge(r_done, R_GATE + 1)
            act.activation(GT[:, :, :], RB[R_GATE % 2][:, 0:TB * 24].rearrange("p (b c) -> p b c", b=TB),
                           ACT.Tanh, scale=0.5).then_inc(r_free, 1)
            w_hi(9)

            act.wait_ge(ones_ready, 2)
            with act.Fori(0, PAIRS) as c:
                pan, fil, tur = P_ATT + c * 4, F_ATT + c * F_PAIR, R_ATT + c * R_PAIR

                def ahead(k):
                    i = C_ATT + k + 3
                    w_hi(i, i % SLOTS, (i // SLOTS + 1) * 16 + c * 16)

                def exps(u):
                    for qb in range(TB):
                        act.wait_ge(s_free, fil + (2 + 4 * u + qb + 1))
                        w = (qb + 1) * P
                        sl = PP[:, u % 2, unit_off(qb):unit_off(qb) + w]
                        j = 4 * u + qb
                        ins = act.activation(sl, sl, ACT.Exp, bias=MN[:, j:j + 1], scale=-1.0,
                                             accum_out=DEN[:, j:j + 1])
                    ins.then_inc(p_exp, 1)

                def turned(u):
                    for f in range(3):
                        k = 2 + 3 * u + f + (2 if u >= 2 else 0)
                        act.wait_ge(r_done, tur + (k + 1))
                        bank = RB[(R_ATT + k) % 2]
                        pt = PT[:, u % 2, :]
                        if f == 0:
                            ins = act.activation(pt[:, 0:512], bank[:, 0:512], ACT.Copy)
                        elif f == 1:
                            act.activation(pt[:, row_off(1):row_off(1) + 384], bank[:, 0:384], ACT.Copy)
                            ins = act.activation(pt[:, row_off(3):row_off(3) + 128], bank[:, 384:512], ACT.Copy)
                        else:
                            ins = act.activation(pt[:, row_off(2):row_off(2) + 256], bank[:, 0:256], ACT.Copy)
                        ins.then_inc(r_free, 1)

                act.wait_ge(o_free, c + 1)
                act.wait_ge(gates_ready, 1)
                act.activation(KVS[:, :], KV[:, bass.ds(c // 2, 1), :].rearrange("p a n -> p (a n)"), ACT.Copy).then_inc(kv_staged, 1)
                for e in range(2):
                    sc, _ = COL["slope"]
                    ins = act.activation(DN[:, e, :], cc("tab"), ACT.Copy, scale=CST[:, bass.ds(c * 2 + (sc + e), 1)])
                ins.then_inc(dn_staged, 1)
                act.wait_ge(panel_free, pan + 1)
                for e in range(2):
                    act.activation(QS[e * HD:(e + 1) * HD, e, :], Q[e * HD:(e + 1) * HD, :], ACT.Copy).then_inc(qhi_ready, 1)
                ahead(0)
                for e in range(2):
                    act.wait_ge(cmp_arg, c * 2 + (e + 1))
                    act.activation(PC[:, e, :, 0:NCMP], PC[:, e, :, 0:NCMP], ACT.Exp, scale=-1.0).then_inc(cmp_exp, 1)
                ahead(1)
                exps(0)
                exps(1)
                act.wait_ge(panel_free, pan + 2)
                act.activation(Z[:, 1, :], Z[:, 0, :], ACT.Square).then_inc(gelu_sq, 1)
                for e in range(2):
                    act.wait_ge(r_done, tur + (e + 1))
                    act.activation(PCT[0:NCMP, e, :], RB[(R_ATT + e) % 2][0:NCMP, :], ACT.Copy).then_inc(r_free, 1)
                turned(0)
                ahead(2)
                act.wait_ge(gelu_arg, c * 2 + 2)
                act.activation(Z[:, 1, :], Z[:, 1, :], ACT.Tanh, scale=GC).then_inc(gelu_tanh, 1)
                act.wait_ge(panel_free, pan + 3)
                act.activation(Z[:, 3, :], Z[:, 2, :], ACT.Square).then_inc(gelu_sq, 1)
                exps(2)
                turned(1)
                act.wait_ge(gelu_arg, c * 2 + 3)
                act.activation(Z[:, 3, :], Z[:, 3, :], ACT.Tanh, scale=GC).then_inc(gelu_tanh, 1)
                ahead(3)
                exps(3)
                for a in range(2):
                    k = 8 + a
                    act.wait_ge(r_done, tur + (k + 1))
                    act.activation(VT[:, 2 * a:2 * a + 2, bass.ds(c * P, P)],
                                   RB[(R_ATT + k) % 2][:, 0:2 * P].rearrange("p (b d) -> p b d", b=2),
                                   ACT.Copy).then_inc(r_free, 1)
                turned(2)
                act.wait_ge(panel_free, pan + 4)
                sg = SIG[:, bass.ds(c, 1), :].rearrange("p a n -> p (a n)")
                act.activation(sg, sg, ACT.Tanh, scale=0.5, bias=BH[:, bass.ds(c, 1)]).then_inc(sig_ready, 1)
                turned(3)
                act.wait_ge(o_done, c + 1)
                act.activation(ONH[:, bass.ds(c, 1), :].rearrange("p a n -> p (a n)"), OB[:, :], ACT.Copy).then_inc(onhi_ready, 1)

            act.wait_ge(ln_var, 1)
            act.activation(LS[:, :], BA[:, :, 1:2].rearrange("p b a -> p (b a)"), ACT.Sqrt, bias=cc("eps4")).then_inc(ln_std, 1)

            def gate_tile(sig, pan, chunk, col):
                act.wait_ge(panel_free, pan + 1)
                act.activation(SIG[:, sig, :], SIG[:, sig, :], ACT.Tanh, scale=0.5,
                               bias=BH[:, col:col + 1]).then_inc(sig_ready, 1)
                w_hi(chunk + 3)

            gate_tile(4, P_MRG, C_MRG, KT)
            gate_tile(5, P_MRG + 1, C_MRG + 1, KT + 1)
            for g in range(4):
                act.wait_ge(sgu_out, g + 1)
                act.activation(OSH[:, g, :], Z[:, 2 + g % 2, :], ACT.Copy).then_inc(oshi_ready, 1)
            gate_tile(6, P_MRG + 2, C_MRG + 2, KT + 2)
            gate_tile(7, P_MRG + 3, C_MRG + 3, KT + 3)
            for half in range(2):
                for k in range(4):
                    n = 4 * half + k
                    act.wait_ge(mix_ready, n + 1)
                    act.activation(MXH[:, n, :], Z[:, 2 * (k % 2), :], ACT.Copy, scale=0.5).then_inc(mixhi_ready, 1)
                    w_hi(C_MRG + (4 if half == 0 else 16) + k + 3)
                if half == 0:
                    act.wait_ge(oslo_ready, 4)
                    act.dma_start(H[:, :, :], xT).then_inc(h_loaded, 16)
                    act.dma_start(MRAW[:, :, :], memT).then_inc(mem_loaded, 16)
                    for k in range(4):
                        gate_tile(k, P_MRG + 12 + k, C_MRG + 8 + k, 4 + k)
                    for k in range(4):
                        gate_tile(4 + k, P_MRG + 16 + k, C_MRG + 12 + k, KT + 4 + k)

            act.wait_ge(mem_loaded, 16)
            act.activation(MSQ[:, :, :], MRAW[:, :, :], ACT.Square).then_inc(memsq_ready, 1)
            with act.Fori(0, 2) as r:
                for k in range(4):
                    n = r * 4 + k
                    act.wait_ge(h_ready, n + 1)
                    act.activation(MHH[:, bass.ds(n, 1), :].rearrange("p a n -> p (a n)"),
                                   MRAW[:, bass.ds(n, 1), :].rearrange("p a n -> p (a n)"), ACT.Copy,
                                   scale=CST[:, bass.ds(n + COL["gmem"][0], 1)]).then_inc(memhi_ready, 1)
                    act.wait_ge(acc_ready, n + (KT - 1))
                    hn = H[:, bass.ds(n, 1), :].rearrange("p a n -> p (a n)")
                    act.activation(XH[:, bass.ds(n, 1), :].rearrange("p a n -> p (a n)"), hn, ACT.Copy,
                                   scale=CST[:, bass.ds(n + COL["gq"][0], 1)]).then_inc(xhi_ready, 1)
                    act.activation(SQ[:, k % 2, :], hn, ACT.Square).then_inc(sq_ready, 1)
                    i = C_OUT + 3 + k
                    w_hi(i, i % SLOTS, r * 16 + (i // SLOTS + 1) * 16)
            root(F_MEMRMS, MEM, SB[F_MEMRMS % 3], RSM[:, :])
            w_hi(C_X + 3)
            root(F_QRMS, T, SB[F_QRMS % 3], RS[:, :])

            def cross_exp(n):
                for qb in range(TB):
                    if qb % 2 == 0:
                        act.wait_ge(p_max, 2 * n + qb // 2 + 1)
                    j = 4 * (n % 2) + qb
                    bank = SB[(F_CROSS + 2 * n + qb // 2) % 3]
                    ins = act.activation(P2[:, n % 2, qb, :], bank[:, (qb % 2) * MEM:(qb % 2 + 1) * MEM], ACT.Exp,
                                         bias=MN[:, j:j + 1], scale=-1.0, accum_out=DEN[:, j:j + 1])
                    if qb % 2:
                        ins.then_inc(s_free, 1)

            def cross_turned(n):
                for b in range(MB):
                    k = R_CT[n] + b
                    act.wait_ge(r_done, k + 1)
                    act.activation(PT2[:, n % 2, b, :], RB[k % 2][:, :], ACT.Copy).then_inc(r_free, 1)

            def cross_o(n):
                act.wait_ge(o_done, PAIRS + n + 1)
                act.activation(OXH[:, n, :], OB[:, :], ACT.Copy).then_inc(onhi_ready, 1)

            def memory_values(n):
                act.wait_ge(r_done, R_VT[n] + 1)
                act.activation(MV[:, :, n * P:(n + 1) * P], RB[R_VT[n] % 2][:, 0:MEM].rearrange(
                    "p (b c) -> p b c", b=MB), ACT.Copy).then_inc(r_free, 1)

            w_hi(C_X + 4)
            w_hi(C_X + 5)
            cross_exp(0)
            w_hi(C_X + 6)
            memory_values(0)
            w_hi(C_X + 7)
            cross_exp(1)
            cross_turned(0)
            w_hi(C_X + 8)
            w_hi(C_X + 9)
            cross_o(0)
            cross_turned(1)
            w_hi(C_X + 10)
            memory_values(1)
            cross_exp(2)
            cross_o(1)
            w_hi(C_X + 11)
            w_hi(C_MO)
            memory_values(2)
            cross_turned(2)
            w_hi(C_MO + 1)
            cross_exp(3)
            cross_o(2)
            memory_values(3)
            w_hi(C_MO + 2)
            cross_turned(3)
            cross_o(3)
            for k in range(KT):
                n = k
                act.wait_ge(h_ready, KT + n + 1)
                act.activation(XH[:, n, :], H[:, n, :], ACT.Copy, scale=cc("gf", n, n + 1)).then_inc(xhi_ready, 1)
                act.wait_ge(acc_ready, 2 * KT + n - 1)
                act.activation(SQ[:, k % 2, :], H[:, n, :], ACT.Square).then_inc(sq_ready, 1)
                if k % 2:
                    w_hi(C_MO + k // 2 + 3)
            root(F_FRMS, T, SB[F_FRMS % 3], RS[:, :])
            with act.Fori(0, FT // 2) as r:
                for k in range(2):
                    j = r * 2 + k
                    act.wait_ge(panel_free, r * 4 + (FREE_GU + 2 * k + 1))
                    act.activation(Z[:, 2 * k + 1, :], Z[:, 2 * k, :], ACT.Tanh, scale=0.5).then_inc(act_tanh, 1)
                    for m in range(2):
                        i = C_GU + 3 + 2 * k + m
                        w_hi(i, i % SLOTS, (i // SLOTS + 1) * 16 + r * 16)
                    act.wait_ge(hid_ready, j + 1)
                    act.activation(HH[:, bass.ds(j, 1), :].rearrange("p a n -> p (a n)"), Z[:, 2 * k, :], ACT.Copy,
                                   scale=0.5).then_inc(hidhi_ready, 1)
            for n in range(KT):
                for m in range(3):
                    if C_DN + 3 * n + m + 3 < NCHUNK:
                        w_hi(C_DN + 3 * n + m + 3)
                act.wait_ge(h_ready, 2 * KT + n + 1)
                act.wait_ge(acc_ready, 3 * KT + n - 1)
                act.activation(SQ[:, n % 2, :], H[:, n, :], ACT.Square).then_inc(sq_ready, 1)
            root(F_ORMS, T, SB[F_ORMS % 3], RS[:, :])

        @block.vector
        def _(dve):
            st = Steps()

            def chain():
                dve.wait_ge(dve_step, st.now())

            def x_lo(n, gain, count):
                dve.wait_ge(xhi_ready, count + 1)
                dve.scalar_tensor_tensor(XL[:, n, :], H[:, n, :], gain, XH[:, n, :].bitcast(F32),
                                         ALU.mult, ALU.subtract).then_inc(xlo_ready, 1)

            def add_square(count, first, k2):
                dve.wait_ge(sq_ready, count + 1)
                if first:
                    dve.tensor_copy(ACC[:, :], SQ[:, k2, :]).then_inc(acc_ready, 1)
                else:
                    dve.wait_ge(acc_ready, count)
                    dve.tensor_tensor(ACC[:, :], ACC[:, :], SQ[:, k2, :], ALU.add).then_inc(acc_ready, 1)

            def inverse(n_root, dst):
                dve.wait_ge(rms_ready, n_root)
                dve.reciprocal(dst, dst).then_inc(s_free, 1)

            def times_rms(p, dst, w=T, rs=None, lo=0, hi=P, dlo=None):
                rs = RS if rs is None else rs
                return dve.tensor_tensor(dst, LB[p % 2][lo:hi, 0:w], rs[lo:hi, 0:w], ALU.mult)

            dve.wait_ge(cst_loaded, 16)
            for n in range(KT):
                x_lo(n, cc("gmix", n, n + 1), n)
                if n >= 4:
                    add_square(n - 4, n == 4, n % 2)
            for n in range(4, KT):
                add_square(n, False, n % 2)
            dve.tensor_scalar(BH[:, :], cc("bm"), 0.5, None, ALU.mult).then_inc(o_free, 1)
            inverse(1, RS[:, :])
            dve.memset(KR[:, :, KC_:KEYW], 0.0).then_inc(dve_step, st.add())
            dve.memset(KV[:, :, VC_:KVW], 0.0).then_inc(dve_step, st.add())
            dve.wait_ge(s_free, F_XRMS + 1)
            for s in range(2):
                dve.wait_ge(chunk_used, C_IN + s + 1)
                times_rms(C_IN + s, KC[:, s, :]).then_inc(panel_free, 1)
                dve.wait_ge(panel_free, C_IN + s + 1)
                if s == 0:
                    dve.wait_ge(tables_loaded, 16)
                pe, _ = COL["pe"]
                for g in range(2):
                    for par in range(2):
                        for a in range(2):
                            src = KC[g * HD:(g + 1) * HD, s, :].rearrange(
                                "p (m b r) -> p r b m", b=8, r=2)[:, par, :, a:a + NCMP]
                            pv = CST[g * HD:(g + 1) * HD, pe + (s * 2 + par) * CJ + 8 * a:pe + (s * 2 + par) * CJ + 8 * a + 8]
                            dst = G[par * HD:(par + 1) * HD, s, 8 * a:8 * a + 8, g * NCMP:(g + 1) * NCMP]
                            ins = dve.tensor_tensor(dst, src, pv.unsqueeze(2).broadcast_to((HD, 8, NCMP)), ALU.add)
                ins.then_inc(g_ready, 1)

            def keys_in(p, off):
                dve.wait_ge(chunk_used, p + 1)
                for g in range(2):
                    for half in range(2):
                        ins = dve.tensor_tensor(KR[half * HD:(half + 1) * HD, g, off:off + T],
                                                LB[p % 2][g * HD:(g + 1) * HD, :], RS[g * HD:(g + 1) * HD, :], ALU.mult)
                ins.then_inc(panel_free, 1)

            def keys_lo(n, off, width):
                dve.wait_ge(keyhi_ready, n)
                dve.tensor_tensor(KL[:, :, off:off + width], KR[:, :, off:off + width],
                                  KH[:, :, off:off + width].bitcast(F32), ALU.subtract).then_inc(keylo_ready, 1)

            keys_in(C_IN + 2, KS)
            dve.wait_ge(chunk_used, C_IN + 4)
            times_rms(C_IN + 3, Z[:, 2, :]).then_inc(panel_free, 1)
            for g in range(4):
                w = CST[:, COL["ws"][0] + g * P:COL["ws"][0] + (g + 1) * P]
                dve.tensor_tensor(w, w, cc("tri"), ALU.mult)
            dve.wait_ge(s_done, F_HID + 1)
            dve.tensor_copy(HZ[:, 0, :], SB[F_HID % 3][:, 0:4 * NCMP]).then_inc(s_free, 1)
            dve.wait_ge(gelu_sq, 1)
            dve.tensor_scalar(HZ[:, 1, :], HZ[:, 1, :], GA, 1.0, ALU.mult, ALU.add).then_inc(dve_step, st.add())
            chain()
            dve.tensor_tensor(HZ[:, 1, :], HZ[:, 1, :], HZ[:, 0, :], ALU.mult).then_inc(gelu_arg, 1)
            dve.wait_ge(gelu_tanh, 1)
            dve.scalar_tensor_tensor(HZ[:, 1, :], HZ[:, 1, :], 1.0, HZ[:, 0, :], ALU.add, ALU.mult).then_inc(gelu_done, 1)
            keys_in(C_IN + 4, KW)
            dve.wait_ge(s_done, F_CMP + 1)
            for g in range(2):
                dve.tensor_scalar(KR[:, g, KC_:KC_ + NCMP], SB[F_CMP % 3][:, g * NCMP:(g + 1) * NCMP], 0.5, None, ALU.mult)
                ins = dve.tensor_scalar(KV[0:NCMP, g, VC_:VC_ + HD], SB[F_CMP % 3][0:NCMP, P + g * HD:P + (g + 1) * HD],
                                        0.5, None, ALU.mult)
            ins.then_inc(s_free, 1)
            dve.wait_ge(chunk_used, C_IN + 6)
            times_rms(C_IN + 5, Z[:, 3, :]).then_inc(panel_free, 1)
            dve.wait_ge(chunk_used, C_IN + 7)
            times_rms(C_IN + 6, Z[:, 0, :]).then_inc(panel_free, 1)
            keys_lo(1, KS, T)
            keys_lo(2, KW, T)
            keys_lo(3, KC_, 32)
            dve.wait_ge(r_free, R_GATE + 1)
            dve.tensor_scalar(GT[:, :, :], GT[:, :, :], 0.5, 0.5, ALU.mult, ALU.add).then_inc(gates_ready, 1)

            with dve.Fori(0, PAIRS) as c:
                st.enter(c, 20)
                pan, fil = P_ATT + c * 4, F_ATT + c * F_PAIR

                def scores(u):
                    e = u // 2
                    for qb in range(TB):
                        k = 2 + 4 * u + qb
                        w = (qb + 1) * P
                        j = 4 * u + qb
                        dve.wait_ge(s_done, fil + (k + 1))
                        dve.memset(HOLD[:, j:j + 1], 0.0)
                        dve.tensor_tensor_reduce(PP[:, u % 2, unit_off(qb):unit_off(qb) + w],
                                                 SB[(F_ATT + k) % 3][:, 0:w], DN[:, e, 384 - P * qb:512], 1.0, 3e38,
                                                 ALU.add, ALU.min, MN[:, j:j + 1]).then_inc(s_free, 1)

                def weigh(u):
                    e, br = u // 2, u % 2
                    dve.wait_ge(p_exp, c * 4 + (u + 1))
                    dve.reciprocal(RD[:, 4 * u:4 * u + 4], DEN[:, 4 * u:4 * u + 4]).then_inc(dve_step, st.add())
                    chain()
                    gate = GT[:, :, bass.ds(c * 6 + (3 * e + 1 + br), 1)].rearrange("p b a -> p (b a)")
                    dve.tensor_tensor(RD[:, 4 * u:4 * u + 4], RD[:, 4 * u:4 * u + 4], gate, ALU.mult).then_inc(dve_step, st.add())
                    chain()
                    for qb in range(TB):
                        sl = PP[:, u % 2, unit_off(qb):unit_off(qb) + (qb + 1) * P]
                        ins = dve.tensor_scalar(sl, sl, RD[:, 4 * u + qb:4 * u + qb + 1], None, ALU.mult)
                    ins.then_inc(p_ready, 1)

                def gelu_a(n, z):
                    dve.wait_ge(gelu_sq, n)
                    dve.tensor_scalar(Z[:, z + 1, :], Z[:, z + 1, :], GA, 1.0, ALU.mult, ALU.add).then_inc(dve_step, st.add())
                    chain()
                    dve.tensor_tensor(Z[:, z + 1, :], Z[:, z + 1, :], Z[:, z, :], ALU.mult).then_inc(gelu_arg, 1)

                dve.wait_ge(chunk_used, C_ATT + 1 + c * 4)
                dve.scalar_tensor_tensor(Q[:, :], LB[P_ATT % 2][:, :], -(float(HD) ** -0.5), RS[:, :],
                                         ALU.mult, ALU.mult).then_inc(panel_free, 1)
                for e in range(2):
                    own, other = slice(e * HD, (e + 1) * HD), slice((1 - e) * HD, (2 - e) * HD)
                    dve.wait_ge(qhi_ready, c * 2 + (e + 1))
                    dve.tensor_tensor(QS[other, e, :], Q[own, :], QS[own, e, :].bitcast(F32), ALU.subtract).then_inc(q_ready, 1)
                dve.wait_ge(dn_staged, c + 1)
                for e in range(2):
                    dve.wait_ge(s_done, fil + (e + 1))
                    pc = PC[:, e, :, 0:NCMP]
                    dve.tensor_tensor(pc, SB[(F_ATT + e) % 3][:, 0:P].rearrange("p (b i) -> p b i", b=TB)[:, :, 0:NCMP],
                                      DN[:, e, 512:640].rearrange("p (b i) -> p b i", b=TB)[:, :, 0:NCMP],
                                      ALU.add).then_inc(s_free, 1)
                    dve.wait_ge(s_free, fil + (e + 1))
                    dve.tensor_reduce(MC[:, e, :], pc, AX, ALU.min).then_inc(dve_step, st.add())
                    chain()
                    dve.tensor_tensor(pc, pc, MC[:, e, :].unsqueeze(2).broadcast_to((P, TB, NCMP)), ALU.subtract).then_inc(cmp_arg, 1)
                scores(0)
                scores(1)
                for e in range(2):
                    dve.wait_ge(cmp_exp, c * 2 + (e + 1))
                    pc = PC[:, e, :, 0:NCMP]
                    dve.tensor_reduce(DC[:, e, :], pc, AX, ALU.add).then_inc(dve_step, st.add())
                    chain()
                    dve.reciprocal(RC[:, e, :], DC[:, e, :]).then_inc(dve_step, st.add())
                    chain()
                    gate = GT[:, :, bass.ds(c * 6 + 3 * e, 1)].rearrange("p b a -> p (b a)")
                    dve.tensor_tensor(RC[:, e, :], RC[:, e, :], gate, ALU.mult).then_inc(dve_step, st.add())
                    chain()
                    dve.tensor_tensor(RC[:, e, :], RC[:, e, :], cc("valid"), ALU.mult).then_inc(dve_step, st.add())
                    chain()
                    dve.tensor_tensor(pc, pc, RC[:, e, :].unsqueeze(2).broadcast_to((P, TB, NCMP)), ALU.mult).then_inc(cmp_ready, 1)
                dve.wait_ge(chunk_used, C_ATT + 2 + c * 4)
                times_rms(P_ATT + 1, Z[:, 0, :]).then_inc(panel_free, 1)
                weigh(0)
                weigh(1)
                gelu_a(c * 2 + 2, 0)
                dve.wait_ge(chunk_used, C_ATT + 3 + c * 4)
                times_rms(P_ATT + 2, Z[:, 2, :]).then_inc(panel_free, 1)
                scores(2)
                dve.wait_ge(gelu_tanh, c * 2 + 2)
                dve.scalar_tensor_tensor(U[:, bass.ds(c, 1), :].rearrange("p a n -> p (a n)"), Z[:, 1, :], 1.0, Z[:, 0, :],
                                         ALU.add, ALU.mult).then_inc(gelu_done, 1)
                gelu_a(c * 2 + 3, 2)
                weigh(2)
                scores(3)
                dve.wait_ge(gelu_tanh, c * 2 + 3)
                dve.scalar_tensor_tensor(Z[:, 3, :], Z[:, 3, :], 1.0, Z[:, 2, :], ALU.add, ALU.mult).then_inc(gelu_done, 1)
                dve.wait_ge(chunk_used, C_ATT + 4 + c * 4)
                times_rms(P_ATT + 3, SIG[:, bass.ds(c, 1), :].rearrange("p a n -> p (a n)")).then_inc(panel_free, 1)
                weigh(3)
                dve.wait_ge(onhi_ready, c + 1)
                dve.tensor_tensor(ONL[:, bass.ds(c, 1), :].rearrange("p a n -> p (a n)"), OB[:, :],
                                  ONH[:, bass.ds(c, 1), :].rearrange("p a n -> p (a n)").bitcast(F32),
                                  ALU.subtract).then_inc(o_free, 1)
            st.leave(PAIRS)

            dve.wait_ge(r_free, R_X)
            for b in range(TB):
                ins = dve.bn_stats(BN[:, b, :], VT[:, b, :])
            ins.then_inc(dve_step, st.add())
            chain()
            for b in range(TB):
                ins = dve.bn_aggr(BA[:, b, :], BN[:, b, :])
            ins.then_inc(ln_var, 1)
            dve.wait_ge(ln_std, 1)
            dve.reciprocal(LS[:, :], LS[:, :]).then_inc(dve_step, st.add())
            chain()
            for b in range(TB):
                dve.tensor_scalar(VT[:, b, :], VT[:, b, :], BA[:, b, 0:1], LS[:, b:b + 1], ALU.subtract,
                                  ALU.mult).then_inc(vn_ready, 1)

            def gate_in(sig, pan, chunk):
                dve.wait_ge(chunk_used, chunk + 1)
                times_rms(pan, SIG[:, sig, :]).then_inc(panel_free, 1)

            gate_in(4, P_MRG, C_MRG)
            gate_in(5, P_MRG + 1, C_MRG + 1)
            dve.wait_ge(bsp_loaded, 16)
            for g in range(4):
                n = F_SGU + g
                dve.wait_ge(s_done, n + 1)
                dve.scalar_tensor_tensor(Z[:, 0, :].rearrange("p (b t) -> p b t", b=TB), SB[n % 3][:, :].rearrange("p (b t) -> p b t", b=TB),
                                         cc("lng", g, g + 1), BB[:, g, :].unsqueeze(1).broadcast_to((P, TB, P)),
                                         ALU.mult, ALU.add).then_inc(s_free, 1)
                dve.wait_ge(s_free, n + 1)
                if g >= 2:
                    dve.wait_ge(oshi_ready, g - 1)
                dve.scalar_tensor_tensor(Z[:, 2 + g % 2, :], Z[:, 0, :], 0.5, U[:, g, :], ALU.mult, ALU.mult).then_inc(sgu_out, 1)
                dve.wait_ge(oshi_ready, g + 1)
                dve.tensor_tensor(OSL[:, g, :], Z[:, 2 + g % 2, :], OSH[:, g, :].bitcast(F32), ALU.subtract).then_inc(oslo_ready, 1)
            gate_in(6, P_MRG + 2, C_MRG + 2)
            gate_in(7, P_MRG + 3, C_MRG + 3)
            for half in range(2):
                for k in range(4):
                    n = 4 * half + k
                    pan = P_AB[n]
                    dve.wait_ge(sig_ready, PAIRS + 4 + 8 * half)
                    dve.wait_ge(panel_half, n + 1)
                    dve.scalar_tensor_tensor(Z[:, 2 * (k % 2), :], SIG[:, k, :], 1.0, LB[pan % 2][:, :], ALU.add, ALU.mult).then_inc(panel_free, 1)
                    dve.wait_ge(chunk_used, C_AB[n] + 1)
                    dve.scalar_tensor_tensor(Z[:, 2 * (k % 2) + 1, :], SIG[:, 4 + k, :], 1.0, LB[(pan + 1) % 2][:, :], ALU.add, ALU.mult).then_inc(panel_free, 1)
                    dve.wait_ge(panel_free, pan + 2)
                    dve.tensor_tensor(Z[:, 2 * (k % 2), :], Z[:, 2 * (k % 2), :], Z[:, 2 * (k % 2) + 1, :], ALU.add).then_inc(mix_ready, 1)
                    dve.wait_ge(mixhi_ready, n + 1)
                    dve.scalar_tensor_tensor(MXL[:, n, :], Z[:, 2 * (k % 2), :], 0.5, MXH[:, n, :].bitcast(F32),
                                             ALU.mult, ALU.subtract).then_inc(mixlo_ready, 1)
                if half == 0:
                    for k in range(4):
                        gate_in(k, P_MRG + 12 + k, C_MRG + 8 + k)
                    for k in range(4):
                        gate_in(4 + k, P_MRG + 16 + k, C_MRG + 12 + k)

            def clear_sum():
                dve.memset(ACC[:, :], 0.0).then_inc(dve_step, st.add())
                chain()

            clear_sum()
            dve.wait_ge(h_loaded, 16)
            dve.wait_ge(memsq_ready, 1)
            dve.tensor_reduce(MSUM[:, :], MSQ[:, :, :].rearrange("p k t -> p t k"), AX, ALU.add).then_inc(memsum_ready, 1)
            with dve.Fori(0, 2) as r:
                for k in range(4):
                    n = r * 4 + k
                    hn = H[:, bass.ds(n, 1), :].rearrange("p a n -> p (a n)")
                    dve.wait_ge(chunk_used, n + (C_OUT + 1))
                    dve.tensor_tensor(hn, hn, LB[(P_OUT + k) % 2][:, :], ALU.add).then_inc(h_ready, 1)
                    dve.wait_ge(h_ready, n + 1)
                    dve.wait_ge(xhi_ready, n + (KT + 1))
                    dve.scalar_tensor_tensor(XL[:, bass.ds(n, 1), :].rearrange("p a n -> p (a n)"), hn,
                                             CST[:, bass.ds(n + COL["gq"][0], 1)],
                                             XH[:, bass.ds(n, 1), :].rearrange("p a n -> p (a n)").bitcast(F32),
                                             ALU.mult, ALU.subtract).then_inc(xlo_ready, 1)
                    dve.wait_ge(sq_ready, n + (KT + 1))
                    dve.wait_ge(acc_ready, n + KT)
                    dve.tensor_tensor(ACC[:, :], ACC[:, :], SQ[:, k % 2, :], ALU.add).then_inc(acc_ready, 1)
                    dve.wait_ge(memhi_ready, n + 1)
                    dve.scalar_tensor_tensor(MHL[:, bass.ds(n, 1), :].rearrange("p a n -> p (a n)"),
                                             MRAW[:, bass.ds(n, 1), :].rearrange("p a n -> p (a n)"),
                                             CST[:, bass.ds(n + COL["gmem"][0], 1)],
                                             MHH[:, bass.ds(n, 1), :].rearrange("p a n -> p (a n)").bitcast(F32),
                                             ALU.mult, ALU.subtract).then_inc(memlo_ready, 1)

            inverse(2, RSM[:, :])
            dve.wait_ge(s_free, F_MEMRMS + 1)
            def cross_q(n):
                j = CROSS.index(f"q{n}")
                dve.wait_ge(chunk_used, C_X + j + 1)
                dve.scalar_tensor_tensor(HQ[:, n % 2, :], LB[(P_X + j) % 2][:, :], -SC_MEM, RS[:, :],
                                         ALU.mult, ALU.mult).then_inc(panel_free, 1)

            def memory_key(n):
                j = CROSS.index(f"k{n}")
                dve.wait_ge(chunk_used, C_X + j + 1)
                times_rms(P_X + j, MK[:, n, :], MEM, RSM).then_inc(panel_free, 1)

            def memory_value(n):
                j = CROSS.index(f"v{n}")
                dve.wait_ge(chunk_used, C_X + j + 1)
                if n >= 2:
                    dve.wait_ge(r_done, R_VT[n - 2] + 1)
                times_rms(P_X + j, Z[:, n % 2, 0:MEM], MEM, RSM).then_inc(panel_free, 1)

            def cross_max(n):
                for f in range(2):
                    k = F_CROSS + 2 * n + f
                    dve.wait_ge(s_done, k + 1)
                    j = 4 * (n % 2) + 2 * f
                    dve.tensor_reduce(MN[:, j:j + 2], SB[k % 3][:, :].rearrange("p (b m) -> p b m", b=2), AX,
                                      ALU.min).then_inc(p_max, 1)

            def cross_weigh(n):
                dve.wait_ge(s_free, F_CROSS + 2 * n + 2)
                j = 4 * (n % 2)
                dve.reciprocal(RD[:, j:j + 4], DEN[:, j:j + 4]).then_inc(dve_step, st.add())
                chain()
                for qb in range(TB):
                    ins = dve.tensor_scalar(P2[:, n % 2, qb, :], P2[:, n % 2, qb, :], RD[:, j + qb:j + qb + 1], None, ALU.mult)
                ins.then_inc(p_ready, 1)

            def cross_o_lo(n):
                dve.wait_ge(onhi_ready, PAIRS + n + 1)
                dve.tensor_tensor(OXL[:, n, :], OB[:, :], OXH[:, n, :].bitcast(F32), ALU.subtract).then_inc(o_free, 1)

            memory_key(0)
            memory_key(1)
            inverse(3, RS[:, :])
            dve.wait_ge(s_free, F_QRMS + 1)
            cross_q(0)
            memory_value(0)
            cross_max(0)
            cross_weigh(0)
            cross_q(1)
            cross_max(1)
            memory_value(1)
            cross_weigh(1)
            memory_key(2)
            cross_o_lo(0)
            cross_q(2)
            cross_max(2)
            cross_o_lo(1)
            memory_value(2)
            cross_weigh(2)
            memory_key(3)
            cross_q(3)
            cross_max(3)
            cross_o_lo(2)
            memory_value(3)
            cross_weigh(3)
            cross_o_lo(3)
            clear_sum()
            for n in range(KT):
                if n % 2 == 0:
                    dve.wait_ge(panel_half, KT + n // 2 + 1)
                else:
                    dve.wait_ge(chunk_used, C_MO + n // 2 + 1)
                dve.tensor_tensor(H[:, n, :], H[:, n, :], LB[(P_MO + n) % 2][:, :], ALU.add).then_inc(h_ready, 1)
                dve.wait_ge(xhi_ready, 2 * KT + n + 1)
                dve.scalar_tensor_tensor(XL[:, n, :], H[:, n, :], cc("gf", n, n + 1), XH[:, n, :].bitcast(F32),
                                         ALU.mult, ALU.subtract).then_inc(xlo_ready, 1)
                add_square(2 * KT + n, False, n % 2)
            inverse(4, RS[:, :])
            dve.wait_ge(s_free, F_FRMS + 1)
            st_g = FREE_GU
            with dve.Fori(0, FT // 2) as r:
                st.enter(r, 2)
                for k in range(2):
                    j = r * 2 + k
                    zg, zt, zu = Z[:, 2 * k, :], Z[:, 2 * k + 1, :], SQ[:, k, :]
                    dve.wait_ge(chunk_used, r * 4 + (C_GU + 2 * k + 1))
                    times_rms(P_GU + 2 * k, zg).then_inc(panel_free, 1)
                    dve.wait_ge(act_tanh, j + 1)
                    dve.scalar_tensor_tensor(zt, zt, 1.0, zg, ALU.add, ALU.mult).then_inc(dve_step, st.add())
                    dve.wait_ge(chunk_used, r * 4 + (C_GU + 2 * k + 2))
                    times_rms(P_GU + 2 * k + 1, zu).then_inc(panel_free, 1)
                    chain()
                    dve.wait_ge(panel_free, r * 4 + (FREE_GU + 2 * k + 2))
                    dve.tensor_tensor(zg, zt, zu, ALU.mult).then_inc(hid_ready, 1)
                    dve.wait_ge(hidhi_ready, j + 1)
                    dve.scalar_tensor_tensor(HL[:, bass.ds(j, 1), :].rearrange("p a n -> p (a n)"), zg, 0.5,
                                             HH[:, bass.ds(j, 1), :].rearrange("p a n -> p (a n)").bitcast(F32),
                                             ALU.mult, ALU.subtract).then_inc(hidlo_ready, 1)
            st.leave(FT // 2)
            clear_sum()
            for n in range(KT):
                dve.wait_ge(chunk_used, C_DN + 3 * n + 3)
                dve.tensor_tensor(H[:, n, :], H[:, n, :], LB[(P_DN + n) % 2][:, :], ALU.add).then_inc(h_ready, 1)
                add_square(3 * KT + n, False, n % 2)
            inverse(5, RS[:, :])
            dve.wait_ge(s_free, F_ORMS + 1)
            for n in range(KT):
                dve.scalar_tensor_tensor(OUTT[:, n, :], H[:, n, :], cc("gfin", n, n + 1), RS[:, :],
                                         ALU.mult, ALU.mult).then_inc(out_ready, 1)

        @block.tensor
        def _(pe):
            def bank_free(p):
                q = p - 2
                if q < 0:
                    return None, 0
                if q < P_OUT:
                    return panel_free, q + 1
                if q < P_X:
                    return h_ready, q - P_OUT + 1
                if q < P_MO:
                    return panel_free, FREE_X + q - P_X + 1
                if q < P_GU:
                    return h_ready, KT + q - P_MO + 1
                if q < P_DN:
                    return panel_free, FREE_GU + q - P_GU + 1
                return h_ready, 2 * KT + q - P_DN + 1

            def panel(i, bank, units, w=T, shift=None, first=True, last=True, done=None, ready=None):
                s = i % SLOTS
                if shift is None:
                    pe.wait_ge(lo_ready, i + 1)
                else:
                    pe.wait_ge(lo_ready, shift + (i + 1))
                for m, (u, hi, lo) in enumerate(units):
                    if ready is not None:
                        pe.wait_ge(ready[0], ready[1] + m)
                    end = last and m == len(units) - 1
                    dst = LB[bank][:, 0:w]
                    pe.matmul(dst, WH[:, s, u, :], hi, start=first and m == 0, stop=False)
                    pe.matmul(dst, WH[:, s, u, :], lo, start=False, stop=False)
                    ins = pe.matmul(dst, WL[:, s, u, :], hi, start=False, stop=end)
                if last or units[-1][0] == KT - 1:
                    ins.then_inc(chunk_used if done is None else done, 1)

            def free(p):
                s, v = bank_free(p)
                if s is not None:
                    pe.wait_ge(s, v)

            X = [(k, XH[:, k, :], XL[:, k, :]) for k in range(KT)]

            def s_bank(n, turn=None):
                if n >= 3:
                    pe.wait_ge(s_free, n - 2 if turn is None else turn * F_PAIR + (n - 2))
                return SB[n % 3]

            def r_bank(n, turn=None):
                if n >= 2:
                    pe.wait_ge(r_free, n - 1 if turn is None else turn * R_PAIR + (n - 1))
                return RB[n % 2]

            def mean_square(n, count):
                pe.wait_ge(acc_ready, count)
                pe.matmul(s_bank(n)[:, :], ONES[:, :], ACC[:, :], start=True, stop=True).then_inc(s_done, 1)

            pe.wait_ge(ones_ready, 1)
            def turn_values(n, p, z):
                pe.wait_ge(panel_free, p + 1)
                bank = r_bank(n)
                for b in range(TB):
                    ins = pe.transpose(bank[:, b * P:(b + 1) * P], Z[:, z, b * P:(b + 1) * P], IDENT)
                ins.then_inc(r_done, 1)

            for j in range(N_IN):
                i = C_IN + j
                free(i)
                if j == 0:
                    panel(i, i % 2, X, ready=(xlo_ready, 1))
                elif j == 1:
                    panel(i, i % 2, X[0:4], last=False)
                    mean_square(F_XRMS, KT)
                    panel(i, i % 2, X[4:KT], first=False)
                else:
                    panel(i, i % 2, X)
                if j == 3:
                    pe.wait_ge(w1_loaded, 16)
                    pe.wait_ge(tables_loaded, 16)
                    pe.wait_ge(g_ready, 2)
                    bank = s_bank(F_HID)
                    for s in range(2):
                        for u in range(CJ):
                            ins = pe.matmul(bank[:, s * 2 * NCMP:(s + 1) * 2 * NCMP], W1[:, s, u, :], G[:, s, u, :],
                                            start=u == 0, stop=u == CJ - 1)
                    ins.then_inc(s_done, 1)
                if j == 4:
                    turn_values(R_SLC, C_IN + 3, 2)
                    pe.wait_ge(gelu_done, 1)
                    bank = s_bank(F_CMP)
                    pe.matmul(bank[:, 0:2 * NCMP], cc("w2k"), HZ[:, 1, 0:2 * NCMP], start=True, stop=True)
                    for g in range(2):
                        a = (2 + g) * NCMP
                        ins = pe.matmul(bank[0:NCMP, P + g * HD:P + (g + 1) * HD], HZ[:, 1, a:a + NCMP], cc("w2v"),
                                        start=True, stop=True)
                    ins.then_inc(s_done, 1)
            turn_values(R_WIN, C_IN + 5, 3)
            pe.wait_ge(panel_free, C_IN + 7)
            bank = r_bank(R_GATE)
            for b in range(TB):
                ins = pe.transpose(bank[:, b * 24:(b + 1) * 24], Z[0:24, 0, b * P:(b + 1) * P], IDENT[0:24, 0:24])
            ins.then_inc(r_done, 1)

            pe.wait_ge(keylo_ready, 3)
            with pe.Fori(0, PAIRS) as c:
                def part(k, a, b):
                    p = P_ATT + k
                    if a == 0:
                        pe.wait_ge(panel_free, c * 4 + (p - 1))
                    panel(C_ATT + k, p % 2, X[a:b], shift=c * 4, first=a == 0, last=b == KT)

                def query_key(dst, e, qb, off, w):
                    for m, keys in enumerate((KH, KL)):
                        ins = pe.matmul(dst, QS[:, e, qb * P:(qb + 1) * P],
                                        keys[:, bass.ds(c // 2, 1), off:off + w].rearrange("p a n -> p (a n)"),
                                        start=m == 0, stop=m == 1)
                    return ins

                def scores(u, qb):
                    bank = s_bank(F_ATT + 2 + 4 * u + qb, c)
                    w = (qb + 1) * P
                    query_key(bank[:, 0:w], u // 2, qb, (KS, KW)[u % 2], w).then_inc(s_done, 1)

                def turn(u, f):
                    bank = r_bank(R_ATT + turn_fill(u, f), c)
                    if f == 0:
                        pe.wait_ge(p_ready, c * 4 + (u + 1))
                    at_ = 0
                    for kb in TURNS[f]:
                        for qb in range(kb, TB):
                            ins = pe.transpose(bank[:, at_:at_ + P], PP[:, u % 2, unit_off(qb) + kb * P:unit_off(qb) + (kb + 1) * P], IDENT)
                            at_ += P
                    ins.then_inc(r_done, 1)

                def values(u):
                    e, off = u // 2, (VS, VW)[u % 2]
                    for f in range(3):
                        pe.wait_ge(r_free, c * R_PAIR + (R_ATT + turn_fill(u, f) + 1))
                        for kb in TURNS[f]:
                            ins = pe.matmul(OB[e * HD:(e + 1) * HD, kb * P:T], KVS[:, off + kb * HD:off + (kb + 1) * HD],
                                            PT[:, u % 2, row_off(kb):row_off(kb) + (TB - kb) * P],
                                            start=False, stop=u % 2 == 1 and kb == 2, skip_group_check=True)
                    if u == 3:
                        ins.then_inc(o_done, 1)

                q, u, v, a = range(4)
                part(q, 0, KT)
                part(u, 0, 5)
                for e in range(2):
                    pe.wait_ge(q_ready, c * 2 + (e + 1))
                    bank = s_bank(F_ATT + e, c)
                    for qb in range(TB):
                        ins = query_key(bank[:, qb * 32:(qb + 1) * 32], e, qb, KC_, 32)
                    ins.then_inc(s_done, 1)
                scores(0, 0)
                for qb in range(1, TB):
                    part(u, 4 + qb, 5 + qb)
                    scores(0, qb)
                for qb in range(TB):
                    part(v, qb, qb + 1)
                    scores(1, qb)
                part(v, 4, KT)
                for e in range(2):
                    pe.wait_ge(cmp_ready, c * 2 + (e + 1))
                    bank = r_bank(R_ATT + e, c)
                    for qb in range(TB):
                        ins = pe.transpose(bank[0:NCMP, qb * P:(qb + 1) * P], PC[:, e, qb, 0:NCMP], IDENT)
                    ins.then_inc(r_done, 1)
                turn(0, 0)
                turn(0, 1)
                pe.wait_ge(kv_staged, c + 1)
                for e in range(2):
                    pe.wait_ge(r_free, c * R_PAIR + (R_ATT + e + 1))
                    pe.matmul(OB[e * HD:(e + 1) * HD, :], KVS[:, VC_:VC_ + HD], PCT[:, e, :], start=True, stop=False,
                              skip_group_check=True)
                turn(0, 2)
                scores(2, 0)
                for qb in range(1, TB):
                    part(a, qb - 1, qb)
                    scores(2, qb)
                turn(1, 0)
                turn(1, 1)
                values(0)
                turn(1, 2)
                scores(3, 0)
                scores(3, 1)
                part(a, 3, 4)
                scores(3, 2)
                values(1)
                scores(3, 3)
                pe.wait_ge(gelu_done, c * 2 + 3)
                for m in range(2):
                    bank = r_bank(R_ATT + 8 + m, c)
                    for b in range(2):
                        tb = 2 * m + b
                        ins = pe.transpose(bank[:, b * P:(b + 1) * P], Z[:, 3, tb * P:(tb + 1) * P], IDENT)
                    ins.then_inc(r_done, 1)
                part(a, 4, 5)
                for f in range(3):
                    turn(2, f)
                part(a, 5, KT)
                values(2)
                for f in range(3):
                    turn(3, f)
                values(3)

            def x_panel(i, p):
                free(p)
                panel(i, p % 2, X)

            def two_panels(n):
                free(P_AB[n])
                panel(C_AB[n], P_AB[n] % 2, [(k, ONH[:, k, :], ONL[:, k, :]) for k in range(4)], done=panel_half)
                free(P_AB[n] + 1)
                panel(C_AB[n], (P_AB[n] + 1) % 2, [(4 + k, OSH[:, k, :], OSL[:, k, :]) for k in range(4)])

            for k in range(4):
                x_panel(C_MRG + k, P_MRG + k)
                if k == 1:
                    pe.wait_ge(vn_ready, TB)
                    for g in range(4):
                        bank = s_bank(F_SGU + g)
                        ws, _ = COL["ws"]
                        for b in range(TB):
                            ins = pe.matmul(bank[:, b * P:(b + 1) * P], VT[:, b, g * P:(g + 1) * P],
                                            CST[:, ws + g * P:ws + (g + 1) * P], start=True, stop=True)
                        ins.then_inc(s_done, 1)
            pe.wait_ge(o_free, PAIRS + 1)
            pe.wait_ge(oslo_ready, 4)
            for n in range(4):
                two_panels(n)
            for k in range(8):
                x_panel(C_MRG + 8 + k, P_MRG + 12 + k)
            for n in range(4, 8):
                two_panels(n)
            MX = [(k, MXH[:, k, :], MXL[:, k, :]) for k in range(KT)]
            for j in range(KT):
                free(P_OUT + j)
                panel(C_OUT + j, (P_OUT + j) % 2, MX, ready=(mixlo_ready, 1) if j == 0 else None)
                if j == KT - 2:
                    pe.wait_ge(memsum_ready, 1)
                    pe.matmul(s_bank(F_MEMRMS)[:, 0:MEM], ONES[:, :], MSUM[:, :], start=True, stop=True).then_inc(s_done, 1)

            def cross_scores(n):
                pe.wait_ge(panel_free, FREE_X + CROSS.index(f"q{n}") + 1)
                for f in range(2):
                    bank = s_bank(F_CROSS + 2 * n + f)
                    for b in range(2):
                        qb = 2 * f + b
                        ins = pe.matmul(bank[:, b * MEM:(b + 1) * MEM], HQ[:, n % 2, qb * P:(qb + 1) * P], MK[:, n, :],
                                        start=True, stop=True)
                    ins.then_inc(s_done, 1)

            def cross_turn(n):
                pe.wait_ge(p_ready, 16 + n + 1)
                for b in range(MB):
                    bank = r_bank(R_CT[n] + b)
                    for qb in range(TB):
                        ins = pe.transpose(bank[:, qb * P:(qb + 1) * P], P2[:, n % 2, qb, b * P:(b + 1) * P], IDENT)
                    ins.then_inc(r_done, 1)

            def cross_values(n):
                pe.wait_ge(o_free, PAIRS + n + 1)
                pe.wait_ge(r_free, R_VT[n] + 1)
                for b in range(MB):
                    pe.wait_ge(r_free, R_CT[n] + b + 1)
                    ins = pe.matmul(OB[:, :], MV[:, b, n * P:(n + 1) * P], PT2[:, n % 2, b, :], start=b == 0, stop=b == MB - 1)
                ins.then_inc(o_done, 1)

            M = [(k, MHH[:, k, :], MHL[:, k, :]) for k in range(KT)]

            def cross_panel(name, ready=None):
                j = CROSS.index(name)
                free(P_X + j)
                panel(C_X + j, (P_X + j) % 2, X if name[0] == "q" else M, T if name[0] == "q" else MEM, ready=ready)

            def memory_turn(n):
                pe.wait_ge(panel_free, FREE_X + CROSS.index(f"v{n}") + 1)
                bank = r_bank(R_VT[n])
                for b in range(MB):
                    ins = pe.transpose(bank[:, b * P:(b + 1) * P], Z[:, n % 2, b * P:(b + 1) * P], IDENT)
                ins.then_inc(r_done, 1)

            cross_panel("k0", ready=(memlo_ready, 1))
            cross_panel("k1")
            mean_square(F_QRMS, 2 * KT)
            cross_panel("q0", ready=(xlo_ready, KT + 1))
            cross_panel("v0")
            cross_scores(0)
            cross_panel("q1")
            memory_turn(0)
            cross_scores(1)
            cross_turn(0)
            cross_panel("v1")
            cross_panel("k2")
            cross_values(0)
            cross_turn(1)
            cross_panel("q2")
            memory_turn(1)
            cross_scores(2)
            cross_values(1)
            cross_panel("v2")
            cross_panel("k3")
            cross_panel("q3")
            memory_turn(2)
            cross_turn(2)
            cross_scores(3)
            cross_values(2)
            cross_panel("v3")
            memory_turn(3)
            cross_turn(3)
            cross_values(3)
            for m in range(KT // 2):
                for b in range(2):
                    free(P_MO + 2 * m + b)
                    panel(C_MO + m, (P_MO + b) % 2, [(4 * b + k, OXH[:, k, :], OXL[:, k, :]) for k in range(4)],
                          done=panel_half if b == 0 else None,
                          ready=(o_free, PAIRS + 2) if m == b == 0 else None)
            for j in range(2):
                free(P_GU + j)
                panel(C_GU + j, (P_GU + j) % 2, X, ready=(xlo_ready, 2 * KT + 1) if j == 0 else None)
                if j == 0:
                    mean_square(F_FRMS, 3 * KT)
            for j in range(2, 4):
                free(P_GU + j)
                panel(C_GU + j, (P_GU + j) % 2, X)
            with pe.Fori(1, FT // 2) as r:
                for j in range(4):
                    pe.wait_ge(panel_free, r * 4 + (FREE_GU + j - 1))
                    panel(C_GU + j, (P_GU + j) % 2, X, shift=r * 4)
            HID = [(k % KT, HH[:, k, :], HL[:, k, :]) for k in range(FT)]

            for n in range(KT):
                free(P_DN + n)
                for m in range(3):
                    panel(C_DN + 3 * n + m, (P_DN + n) % 2, HID[KT * m:KT * (m + 1)], first=m == 0, last=m == 2,
                          ready=(hidlo_ready, KT * m + 1) if n == 0 else None)
            mean_square(F_ORMS, 4 * KT)


def arena_base(nc, arena, total):
    return nc.sbuf_base - 4 * total


def kernel(**inputs):
    import concourse.bacc as bacc
    from concourse import mybir
    from concourse.bass_utils import run_bass_kernel_spmd

    f = {k: np.asarray(v) for k, v in inputs.items()}

    def tiles(w):
        k, n = w.shape
        return w.reshape(k // P, P, n // P, P).transpose(2, 1, 0, 3)

    w_in = f["w_in"][0]
    win = tiles(w_in[:, :2304])
    gates = np.zeros((D, P), w_in.dtype)
    gates[:, 0:24] = w_in[:, 2304:2328]
    mrg, mkv = tiles(f["w_merge"][0]), tiles(f["w_mkv"][0])
    pa, pb = tiles(f["w_proj_a"][0]), tiles(f["w_proj_b"][0])
    wo, mq, mo = tiles(f["w_out"][0]), tiles(f["w_mq"][0]), tiles(f["w_mo"][0])
    gu, dn = tiles(f["w_gate_up"][0]), tiles(f["w_down"][0])
    pack = np.zeros((NCHUNK, P, KT, P), w_in.dtype)
    at = 0

    def put(x, u0=0):
        nonlocal at
        pack[at, :, u0:u0 + x.shape[1]] = x
        at += 1

    for n in range(4, 10):
        put(win[n])
    put(tiles(gates)[0])
    for c in range(PAIRS):
        put(win[c])
        put(win[10 + c])
        put(win[14 + c])
        put(mrg[c])
    for half in range(2):
        if half:
            for n in range(4, 8):
                put(mrg[n])
        for n in range(4 * half, 4 * half + 4):
            put(mrg[KT + n])
        for n in range(4 * half, 4 * half + 4):
            pack[at, :, 0:4] = pa[n]
            put(pb[n], 4)
    for n in range(8):
        put(wo[n])
    for name in CROSS:
        n = int(name[1])
        put({"k": mkv[n], "v": mkv[MH + n], "q": mq[n]}[name[0]])
    for m in range(4):
        pack[at, :, 0:4] = mo[2 * m]
        put(mo[2 * m + 1], 4)
    for j in range(FT):
        put(gu[j])
        put(gu[FT + j])
    for n in range(KT):
        for m in range(3):
            put(dn[n][:, KT * m:KT * (m + 1)])
    assert at == NCHUNK

    cst = np.zeros((P, NCOL), w_in.dtype)

    def col(name, a):
        c, w = COL[name]
        cst[:a.shape[0], c:c + w] = a.reshape(a.shape[0], w)

    def by_tile(v):
        return v.reshape(-1, P).T

    col("gmix", by_tile(f["norm_mix"][0]))
    col("gmem", by_tile(f["norm_mem_kv"][0]))
    col("gq", by_tile(f["norm_mem_q"][0]))
    col("gf", by_tile(f["norm_ffn"][0]))
    col("gfin", by_tile(f["norm_final"]))
    col("bm", by_tile(f["b_merge"][0]))
    col("lng", by_tile(f["ln_sgu"][0]))
    col("slope", np.broadcast_to(2.0 ** -(np.arange(8) + 1.0), (P, 8)))
    p = np.arange(P)[:, None]
    col("valid", (np.arange(TB)[None] * P + p >= 31).astype(np.float32))
    col("eps", np.full((P, 1), 1e-6))
    col("eps4", np.full((P, 1), 4e-6))
    col("w2k", np.concatenate([f["w_cmp_k2"][0]] * 2, axis=1))
    col("w2v", f["w_cmp_v2"][0])
    pes = np.stack([f["pe_cmp_k"][0], f["pe_cmp_v"][0]]).reshape(2, CJ, 2, HD).transpose(3, 0, 2, 1).reshape(HD, 64)
    col("pe", np.concatenate([pes, pes]))
    col("ident", np.eye(P))
    col("tri", np.arange(P)[None] >= p)
    x = np.arange(T)[None]
    tab = np.where(384 + p - x >= 0, 384 + p - x, MASKED)
    qb, i = np.arange(TB)[:, None], np.arange(32)[None]
    dist = (P * qb + np.arange(P)[:, None, None] - (16 * i + 31)[None]).reshape(P, P)
    tabc = np.where((dist >= 0) & (np.arange(P)[None] % 32 < NCMP), dist, MASKED)
    col("tab", np.concatenate([tab, tabc], axis=1))
    col("ws", f["w_spatial"][0].transpose(2, 0, 1))

    w1 = np.stack([f["w_cmp_k1"][0], f["w_cmp_v1"][0]]).reshape(2, CJ, P, P).transpose(2, 0, 1, 3)
    arrays = {
        "wpk": pack.reshape(NCHUNK, P, CW),
        "xT": np.ascontiguousarray(f["x"][0].T.reshape(KT, P, T).transpose(1, 0, 2)),
        "memT": np.ascontiguousarray(f["mem"][0].T.reshape(KT, P, MEM).transpose(1, 0, 2)),
        "w1": np.ascontiguousarray(w1),
        "cst": cst,
        "bsp": np.ascontiguousarray(f["b_spatial"][0]),
    }
    nc = bacc.Bacc("TRN2", target_bir_lowering=False, num_devices=1)
    dt = mybir.dt.float32
    args = [nc.dram_tensor(n, a.shape, dt, kind="ExternalInput").ap() for n, a in arrays.items()]
    out = nc.dram_tensor("out", (P, KT, T), dt, kind="ExternalOutput").ap()
    build(nc, *args, out)
    got = run_bass_kernel_spmd(nc, [arrays], core_ids=[0]).results[0]["out"]
    return np.ascontiguousarray(got.transpose(1, 0, 2).reshape(D, T).T)[None]
```

```python
from contextlib import ExitStack

import numpy as np

P = 128
T = 512
D = 1024
KT = D // P
TB = T // P
HD = 64
PAIRS = 4
NCMP = 31
CJ = 16
MEM = 256
MB = MEM // P
MH = 4
FT = 2816 // P
SLOTS = 4
CW = KT * P

C_IN, N_IN = 0, 7
C_ATT = C_IN + N_IN
N_ATT = 4 * PAIRS
C_MRG = C_ATT + N_ATT
N_MRG = 20
C_OUT = C_MRG + N_MRG
CROSS = ("k0", "k1", "q0", "v0", "q1", "v1", "k2", "q2", "v2", "k3", "q3", "v3")
C_X = C_OUT + KT
C_MO = C_X + len(CROSS)
C_GU = C_MO + KT // 2
C_DN = C_GU + 2 * FT
NCHUNK = C_DN + 3 * KT

P_ATT = C_ATT
P_MRG = C_MRG
P_OUT = P_MRG + 28
P_X = P_OUT + KT
P_MO = P_X + len(CROSS)
P_GU = P_MO + KT
P_DN = P_GU + 2 * FT
C_AB = [C_MRG + 4 + n for n in range(4)] + [C_MRG + 16 + n for n in range(4)]
P_AB = [P_MRG + 4 + 2 * n for n in range(4)] + [P_MRG + 20 + 2 * n for n in range(4)]
FREE_X = P_OUT
FREE_GU = FREE_X + len(CROSS)

F_XRMS, F_HID, F_CMP = 0, 1, 2
F_ATT, F_PAIR = 3, 18
F_SGU = F_ATT + F_PAIR * PAIRS
F_MEMRMS = F_SGU + 4
F_QRMS = F_MEMRMS + 1
F_CROSS = F_QRMS + 1
F_FRMS = F_CROSS + 2 * MH
R_SLC, R_WIN, R_GATE = 0, 1, 2
R_ATT, R_PAIR = 3, 16
R_X = R_ATT + R_PAIR * PAIRS
R_VT = [R_X + n for n in (0, 5, 6, 9)]
R_CT = [R_X + n for n in (1, 3, 7, 10)]

KS, KW, KC_ = 0, T, 2 * T
KEYW = KC_ + 32
VS, VW, VC_ = 0, 256, 512
KVW = VC_ + HD

_cols = [("gmix", KT), ("eps", 1), ("eps4", 1), ("gmem", KT), ("gq", KT), ("gf", KT), ("gfin", KT),
         ("bm", 2 * KT), ("lng", 4), ("slope", 8), ("valid", TB), ("w2k", P), ("w2v", HD), ("pe", 64),
         ("ident", P), ("tri", P), ("tab", 640), ("ws", 4 * P)]
COL, NCOL = {}, 0
for _n, _w in _cols:
    COL[_n] = (NCOL, _w)
    NCOL += _w
NCOL += -NCOL % 8
FEW = COL["w2k"][0]
WARM = 13
MASKED = 1e32
SC_MEM = float(P) ** -0.5
GC, GA = 0.7978845608028654, 0.044715


def unit_off(qb):
    return P * qb * (qb + 1) // 2


def row_off(kb):
    return sum((TB - k) * P for k in range(kb))


TURNS = (0,), (1, 3), (2,)


def turn_fill(u, f):
    return 2 + 3 * u + f + (2 if u >= 2 else 0)


class Steps:

    def __init__(self):
        self.base, self.k, self.turn = 0, 0, None

    def add(self):
        self.k += 1
        return 1

    def now(self):
        return self.base + self.k if self.turn is None else self.base + self.k + self.turn * self.per

    def enter(self, turn, per):
        self.base, self.k, self.turn, self.per = self.base + self.k, 0, turn, per

    def leave(self, turns):
        assert self.k == self.per, (self.k, self.per)
        self.base, self.k, self.turn = self.base + self.per * turns, 0, None


def build(nc, wpk, xT, memT, w1d, cst, bsp, out):
    import concourse.bass as bass
    from concourse import mybir

    F32, F32R = mybir.dt.float32, mybir.dt.float32r
    ALU, ACT, AX = mybir.AluOpType, mybir.ActivationFunctionType, mybir.AxisListType.X

    with ExitStack() as ctx:
        total = 52800
        arena = ctx.enter_context(nc.sbuf_tensor("arena", [P, total], F32))
        base = arena_base(nc, arena, total)

        def at(name, off, shape, dt=F32):
            n = int(np.prod(shape[1:]))
            assert off + n <= total, (name, off + n)
            return nc.alloc_sbuf_tensor_at(name, shape, dt, offset=base + 4 * off)

        def sem(name):
            return ctx.enter_context(nc.semaphore(name))

        o = 0
        WRAW = at("w_raw", o, [P, SLOTS, KT, P])
        WL = at("w_lo", o, [P, SLOTS, KT, P], F32R)
        o += SLOTS * CW
        WH = at("w_hi", o, [P, SLOTS, KT, P], F32R)
        o += SLOTS * CW
        XH = at("x_hi", o, [P, KT, T], F32R)
        HG = at("h_gain", o, [P, KT, T])
        o += KT * T
        XL = at("x_lo", o, [P, KT, T], F32R)
        OUTK = at("out_tok", o, [P, TB, D])
        o += KT * T
        CST = at("cst", o, [P, NCOL])
        o += NCOL
        ONES = at("ones", o, [P, P]); o += P
        RS = at("rs", o, [P, T]); o += T
        RSM = at("rs_mem", o, [P, MEM]); o += MEM
        ACC = at("acc", o, [P, T]); o += T
        SQ = at("sq", o, [P, 2, T]); o += 2 * T
        Z = at("z", o, [P, 4, T]); o += 4 * T
        BH = at("bh", o, [P, 2 * KT]); o += 2 * KT
        BB = at("bb", o, [P, 4, P]); o += 4 * P
        GT = at("gt", o, [P, TB, 24]); o += TB * 24
        MN = at("mn", o, [P, 16]); o += 16
        DEN = at("den", o, [P, 16]); o += 16
        RD = at("rd", o, [P, 16]); o += 16
        MC = at("mc", o, [P, 2, TB]); o += 8
        DC = at("dc", o, [P, 2, TB]); o += 8
        RC = at("rc", o, [P, 2, TB]); o += 8
        HOLD = at("hold", o, [P, 16]); o += 16
        BN = at("bn", o, [P, TB, 6]); o += TB * 6
        BA = at("ba", o, [P, TB, 2]); o += TB * 2
        LS = at("ls", o, [P, TB]); o += 8
        RF = at("r_final", o, [P, TB]); o += 8
        z0 = o
        H = at("h", z0, [P, KT, T])
        U = at("u", z0, [P, 4, T])
        VT = at("v_tok", z0 + 2048, [P, TB, T])
        MK = at("mk", z0 + 4096, [P, MH, MEM])
        MV = at("mv", z0 + 5120, [P, MB, MH * P])
        z = z0 + 6144
        ONH = at("on_hi", z, [P, PAIRS, T], F32R)
        ONL = at("on_lo", z + 2048, [P, PAIRS, T], F32R)
        W1 = at("w1", z, [P, 2, CJ, P])
        OXH = at("ox_hi", z, [P, MH, T], F32R)
        OXL = at("ox_lo", z + 2048, [P, MH, T], F32R)
        SIG = at("sig", z + 4096, [P, 8, T])
        P2 = at("p2", z + 4096, [P, 2, TB, MEM])
        PT2 = at("pt2", z + 6144, [P, 2, MB, T])
        KH = at("keys_hi", z + 6144, [P, 2, KEYW], F32R)
        KV = at("values", z + 8256, [P, 2, KVW])
        KVS = at("pair_values", z + 9408, [P, VC_])
        QS = at("q_split", z + 9984, [P, 2, T], F32R)
        KR = at("keys_raw", z + 11008, [P, 2, KEYW])
        KL = at("keys_lo", z + 11008, [P, 2, KEYW], F32R)
        Q = at("q", z + 13120, [P, T])
        G = at("g", z + 13632, [P, 2, CJ, 2 * NCMP])
        KC = at("kc", z + 16192, [P, 2, T])
        HZ = at("hz", z + 17216, [P, 2, 4 * NCMP])
        PP = at("pp", z + 13632, [P, 2, 1280])
        PT = at("pt", z + 16192, [P, 2, 1280])
        PC = at("pc", z + 18752, [P, 2, TB, 32])
        PCT = at("pct", z + 19008, [P, 2, T], F32R)
        PCS = at("pc_split", z + 21312, [P, 2, TB, 96], F32R)
        VCR = at("cmp_values", z + 22080, [P, 2, HD], F32R)
        VCS = at("pair_cmp_values", z + 22208, [P, 3 * HD], F32R)
        DN = at("dn", z + 20032, [P, 2, 640])
        MRAW = at("mem_raw", z + 20480, [P, KT, MEM])
        MSQ = at("mem_sq", z0 + 4096, [P, KT, MEM])
        MSUM = SQ[:, 0, 0:MEM]
        MHH = at("mem_hi", z + 8192, [P, KT, MEM], F32R)
        MHL = at("mem_lo", z + 10240, [P, KT, MEM], F32R)
        OSH = at("os_hi", z + 8192, [P, 4, T], F32R)
        OSL = at("os_lo", z + 10240, [P, 4, T], F32R)
        MXH = at("mix_hi", z + 12288, [P, KT, T], F32R)
        MXL = at("mix_lo", z + 16384, [P, KT, T], F32R)
        HQ = at("hq", z + 20480, [P, 2, T])
        HH = at("hid_hi", z, [P, FT, T], F32R)
        HL = at("hid_lo", z + FT * T, [P, FT, T], F32R)

        def cc(name, a=0, b=None):
            c, w = COL[name]
            return CST[:, c + a:c + (w if b is None else b)]

        IDENT = cc("ident")

        def tile_of(x, n):
            return x[:, bass.ds(n, 1), :].rearrange("p a n -> p (a n)")


        LB = [ctx.enter_context(nc.psum_tensor(f"lin{i}", [P, T], F32)) for i in range(2)]
        SB = [ctx.enter_context(nc.psum_tensor(f"score{i}", [P, T], F32)) for i in range(3)]
        RB = [ctx.enter_context(nc.psum_tensor(f"turn{i}", [P, T], F32)) for i in range(2)]
        OB = ctx.enter_context(nc.psum_tensor("heads", [P, T], F32))
        FB = SB + RB[:1]
        LB.append(RB[1])

        w_loaded = [sem(f"w_loaded{s}") for s in range(SLOTS)]
        hi_ready = sem("hi_ready")
        lo_ready = sem("lo_ready")
        chunk_used = sem("chunk_used")
        cst_loaded, mem_loaded = sem("cst_loaded"), sem("mem_loaded")
        tables_loaded = sem("tables_loaded")
        x_loaded = [sem(f"x_loaded{m}") for m in range(KT // 2)]
        w1_loaded, bsp_loaded, h_loaded = sem("w1_loaded"), sem("bsp_loaded"), sem("h_loaded")
        ones_ready = sem("ones_ready")
        memhi_ready, memlo_ready, memsq_ready = sem("memhi_ready"), sem("memlo_ready"), sem("memsq_ready")
        memsum_ready = sem("memsum_ready")
        scaled_ready = sem("scaled_ready")
        final_turned, final_copied = sem("final_turned"), sem("final_copied")
        last_turned = sem("last_turned")
        mean_done, root_done, rf_ready = sem("mean_done"), sem("root_done"), sem("rf_ready")
        xhi_ready, xlo_ready = sem("xhi_ready"), sem("xlo_ready")
        sq_ready, acc_ready = sem("sq_ready"), sem("acc_ready")
        h_ready = sem("h_ready")
        rms_ready = sem("rms_ready")
        panel_half = sem("panel_half")
        panel_free = sem("panel_free")
        s_done, s_free = sem("s_done"), sem("s_free")
        r_done, r_free = sem("r_done"), sem("r_free")
        o_done, o_free = sem("o_done"), sem("o_free")
        gelu_sq, gelu_arg, gelu_tanh, gelu_done = sem("gelu_sq"), sem("gelu_arg"), sem("gelu_tanh"), sem("gelu_done")
        g_ready = sem("g_ready")
        kv_staged, dn_staged = sem("kv_staged"), sem("dn_staged")
        keyhi_ready, keylo_ready = sem("keyhi_ready"), sem("keylo_ready")
        qhi_ready, q_ready = sem("qhi_ready"), sem("q_ready")
        cmp_arg, cmp_exp, cmp_ready = sem("cmp_arg"), sem("cmp_exp"), sem("cmp_ready")
        cmp_prob, cmp_hi = sem("cmp_prob"), sem("cmp_hi")
        vchi_ready = sem("vchi_ready")
        p_max, p_exp, p_ready = sem("p_max"), sem("p_exp"), sem("p_ready")
        sig_ready = sem("sig_ready")
        onhi_ready = sem("onhi_ready")
        ln_var, ln_std, vn_ready = sem("ln_var"), sem("ln_std"), sem("vn_ready")
        sgu_out, oshi_ready, oslo_ready = sem("sgu_out"), sem("oshi_ready"), sem("oslo_ready")
        mix_ready, mixhi_ready, mixlo_ready = sem("mix_ready"), sem("mixhi_ready"), sem("mixlo_ready")
        act_tanh = sem("act_tanh")
        hid_ready, hidhi_ready, hidlo_ready = sem("hid_ready"), sem("hidhi_ready"), sem("hidlo_ready")
        dve_step = sem("dve_step")
        gates_ready = sem("gates_ready")
        first_out, last_out = sem("first_out"), sem("last_out")
        out_stored = sem("out_stored")

        block = ctx.enter_context(nc.Block())

        @block.sync
        def _(sp):
            def load(i, s):
                sp.dma_start(WRAW[:, s, :, :], wpk[i].rearrange("p (u c) -> p u c", u=KT)).then_inc(w_loaded[s], 16)

            def load_x(m):
                sp.dma_start(H[:, 2 * m:2 * m + 2, :], xT[:, 2 * m:2 * m + 2, :]).then_inc(x_loaded[m], 16)

            load_x(0)
            load(0, 0)
            load_x(1)
            load(1, 1)
            load_x(2)
            load_x(3)
            load(2, 2)
            load(3, 3)
            with sp.Fori(1, NCHUNK // SLOTS) as g:
                for s in range(SLOTS):
                    sp.wait_ge(chunk_used, g * SLOTS + (s + 1 - SLOTS))
                    sp.dma_start(WRAW[:, s, :, :], wpk[bass.ds(g * SLOTS + s, 1), :, :].rearrange(
                        "a p (u c) -> p (a u) c", u=KT)).then_inc(w_loaded[s], 16)
            for i in range(NCHUNK // SLOTS * SLOTS, NCHUNK):
                sp.wait_ge(chunk_used, i + 1 - SLOTS)
                load(i, i % SLOTS)
            for b in range(TB):
                sp.wait_ge(first_out, b + 1)
                sp.wait_ge(last_out, b + 1)
                sp.dma_start(out[b * P:(b + 1) * P, :], OUTK[:, b, :]).then_inc(out_stored, 16)
            sp.wait_ge(out_stored, 64)

        @block.gpsimd
        def _(pool):
            pool.memset(ONES[:, :], 1.0 / D).then_inc(ones_ready, 1)
            for zeros in (PCT[:, :, :], PCS[:, :, :, :], VCR[:, :, :], VCS[:, :]):
                pool.memset(zeros.bitcast(F32), 0.0).then_inc(ones_ready, 1)

            def split(i, s):
                pool.wait_ge(hi_ready, i + 1)
                pool.tensor_tensor(WL[:, s, :, :], WRAW[:, s, :, :], WH[:, s, :, :].bitcast(F32),
                                   ALU.subtract).then_inc(lo_ready, 1)

            with pool.Fori(0, NCHUNK // SLOTS) as g:
                for s in range(SLOTS):
                    split(g * SLOTS + s, s)
            for i in range(NCHUNK // SLOTS * SLOTS, NCHUNK):
                split(i, i % SLOTS)

        @block.scalar
        def _(act):
            act.dma_start(CST[:, 0:FEW], cst[:, 0:FEW]).then_inc(cst_loaded, 16)

            def w_hi(i, s=None, turn=None):
                s = i % SLOTS if s is None else s
                act.wait_ge(w_loaded[s], 16 * (i // SLOTS + 1) if turn is None else turn)
                act.activation(WH[:, s, :, :], WRAW[:, s, :, :], ACT.Copy).then_inc(hi_ready, 1)

            def root(n, width, eps_bank, dst):
                act.wait_ge(s_done, n + 1)
                act.activation(dst, eps_bank[:, 0:width], ACT.Sqrt, bias=cc("eps")).then_inc(rms_ready, 1)

            def square(n):
                if n >= 4:
                    act.wait_ge(acc_ready, n - 3)
                act.activation(Z[:, n % 4, :], H[:, n, :], ACT.Square).then_inc(sq_ready, 1)

            act.wait_ge(ones_ready, 1)
            act.activation(LS[:, 0:1], ONES[:, 0:1], ACT.Sqrt)
            act.wait_ge(cst_loaded, 16)
            for n in range(KT):
                if n == 1:
                    w_hi(0)
                act.wait_ge(x_loaded[n // 2], 16)
                act.activation(XH[:, n, :], H[:, n, :], ACT.Copy, scale=cc("gmix", n, n + 1)).then_inc(xhi_ready, 1)
                if n == 1:
                    act.dma_start(CST[:, FEW:NCOL], cst[:, FEW:NCOL]).then_inc(tables_loaded, 16)
                    act.dma_start(W1[:, :, :, :], w1d).then_inc(w1_loaded, 16)
                    act.dma_start(BB[:, :, :], bsp.partition_broadcast(P)).then_inc(bsp_loaded, 16)
                if n == 3:
                    w_hi(1)
                if n >= 4:
                    square(n - 4)
            for n in range(4, KT):
                square(n)
            w_hi(2)
            root(F_XRMS, T, SB[F_XRMS % 3], RS[:, :])
            for i in range(3, 7):
                w_hi(i)
            act.wait_ge(s_free, F_HID + 1)
            act.activation(HZ[:, 1, :], HZ[:, 0, :], ACT.Square).then_inc(gelu_sq, 1)
            act.wait_ge(gelu_arg, 1)
            act.activation(HZ[:, 1, :], HZ[:, 1, :], ACT.Tanh, scale=GC).then_inc(gelu_tanh, 1)

            def turned_values(n, off):
                act.wait_ge(r_done, n + 1)
                for g in range(2):
                    ins = act.activation(KV[:, g, off:off + TB * HD].rearrange("p (b d) -> p b d", b=TB),
                                         RB[n % 2][:, :].rearrange("p (b g d) -> p g b d", b=TB, g=2)[:, g, :, :],
                                         ACT.Copy)
                ins.then_inc(r_free, 1)

            def keys_hi(off, width):
                act.activation(KH[:, :, off:off + width], KR[:, :, off:off + width], ACT.Copy).then_inc(keyhi_ready, 1)

            act.wait_ge(panel_free, C_IN + 3)
            keys_hi(KS, T)
            w_hi(7)
            turned_values(R_SLC, VS)
            act.wait_ge(s_free, F_CMP + 1)
            keys_hi(KC_, 32)
            act.wait_ge(ones_ready, 5)
            for part in range(2):
                ins = act.activation(VCR[part * 32:(part + 1) * 32, :, :], KV[0:32, :, VC_:KVW], ACT.Copy)
            ins.then_inc(vchi_ready, 1)
            w_hi(8)
            turned_values(R_WIN, VW)
            w_hi(9)
            act.wait_ge(r_done, R_GATE + 1)
            act.activation(GT[:, :, :], RB[R_GATE % 2][:, 0:TB * 24].rearrange("p (b c) -> p b c", b=TB),
                           ACT.Tanh, scale=0.5).then_inc(r_free, 1)
            act.wait_ge(panel_free, C_IN + 7)
            keys_hi(KW, T)

            with act.Fori(0, PAIRS) as c:
                pan, fil, tur = P_ATT + c * 4, F_ATT + c * F_PAIR, R_ATT + c * R_PAIR

                def ahead(k):
                    i = C_ATT + k + 3
                    w_hi(i, i % SLOTS, (i // SLOTS + 1) * 16 + c * 16)

                def exps(u):
                    for qb in range(TB):
                        act.wait_ge(s_free, fil + (2 + 4 * u + qb + 1))
                        w = (qb + 1) * P
                        sl = PP[:, u % 2, unit_off(qb):unit_off(qb) + w]
                        j = 4 * u + qb
                        ins = act.activation(sl, sl, ACT.Exp, bias=MN[:, j:j + 1], scale=-1.0,
                                             accum_out=DEN[:, j:j + 1])
                    ins.then_inc(p_exp, 1)

                def turned(u):
                    for f in range(3):
                        k = 2 + 3 * u + f + (2 if u >= 2 else 0)
                        act.wait_ge(r_done, tur + (k + 1))
                        bank = RB[(R_ATT + k) % 2]
                        pt = PT[:, u % 2, :]
                        if f == 0:
                            ins = act.activation(pt[:, 0:512], bank[:, 0:512], ACT.Copy)
                        elif f == 1:
                            act.activation(pt[:, row_off(1):row_off(1) + 384], bank[:, 0:384], ACT.Copy)
                            ins = act.activation(pt[:, row_off(3):row_off(3) + 128], bank[:, 384:512], ACT.Copy)
                        else:
                            ins = act.activation(pt[:, row_off(2):row_off(2) + 256], bank[:, 0:256], ACT.Copy)
                        ins.then_inc(r_free, 1)

                act.wait_ge(o_free, c + 1)
                act.wait_ge(gates_ready, 1)
                act.activation(VCS[:, HD:2 * HD], tile_of(VCR, c // 2).bitcast(F32), ACT.Copy)
                act.activation(KVS[:, :], KV[:, bass.ds(c // 2, 1), 0:VC_].rearrange("p a n -> p (a n)"),
                               ACT.Copy).then_inc(kv_staged, 1)
                for e in range(2):
                    sc, _ = COL["slope"]
                    ins = act.activation(DN[:, e, :], cc("tab"), ACT.Copy, scale=CST[:, bass.ds(c * 2 + (sc + e), 1)])
                ins.then_inc(dn_staged, 1)
                act.wait_ge(panel_free, pan + 1)
                for e in range(2):
                    act.activation(QS[e * HD:(e + 1) * HD, e, :], Q[e * HD:(e + 1) * HD, :],
                                   ACT.Copy).then_inc(qhi_ready, 1)
                ahead(0)
                for e in range(2):
                    act.wait_ge(cmp_arg, c * 2 + (e + 1))
                    act.activation(PC[:, e, :, 0:NCMP], PC[:, e, :, 0:NCMP], ACT.Exp, scale=-1.0).then_inc(cmp_exp, 1)
                ahead(1)
                def cmp_round(e):
                    act.wait_ge(cmp_prob, c * 2 + (e + 1))
                    for at_ in (0, 64):
                        ins = act.activation(PCS[:, e, :, at_:at_ + NCMP], PC[:, e, :, 0:NCMP], ACT.Copy)
                    ins.then_inc(cmp_hi, 1)

                exps(0)
                cmp_round(0)
                exps(1)
                cmp_round(1)
                act.wait_ge(panel_free, pan + 2)
                act.activation(Z[:, 1, :], Z[:, 0, :], ACT.Square).then_inc(gelu_sq, 1)
                for e in range(2):
                    act.wait_ge(r_done, tur + (e + 1))
                    act.activation(PCT[0:96, e, :], RB[(R_ATT + e) % 2][0:96, :], ACT.Copy).then_inc(r_free, 1)
                turned(0)
                ahead(2)
                act.wait_ge(gelu_arg, c * 2 + 2)
                act.activation(Z[:, 1, :], Z[:, 1, :], ACT.Tanh, scale=GC).then_inc(gelu_tanh, 1)
                act.wait_ge(panel_free, pan + 3)
                act.activation(Z[:, 3, :], Z[:, 2, :], ACT.Square).then_inc(gelu_sq, 1)
                exps(2)
                turned(1)
                act.wait_ge(gelu_arg, c * 2 + 3)
                act.activation(Z[:, 3, :], Z[:, 3, :], ACT.Tanh, scale=GC).then_inc(gelu_tanh, 1)
                ahead(3)
                exps(3)
                for a in range(2):
                    k = 8 + a
                    act.wait_ge(r_done, tur + (k + 1))
                    act.activation(VT[:, 2 * a:2 * a + 2, bass.ds(c * P, P)],
                                   RB[(R_ATT + k) % 2][:, 0:2 * P].rearrange("p (b d) -> p b d", b=2),
                                   ACT.Copy).then_inc(r_free, 1)
                turned(2)
                turned(3)
                act.wait_ge(o_done, c + 1)
                act.activation(tile_of(ONH, c), OB[:, :], ACT.Copy).then_inc(onhi_ready, 1)
                act.wait_ge(panel_free, pan + 4)
                sg = tile_of(SIG, c)
                act.activation(sg, sg, ACT.Tanh, scale=0.5, bias=BH[:, bass.ds(c, 1)]).then_inc(sig_ready, 1)

            act.wait_ge(ln_var, 1)
            act.activation(LS[:, :], BA[:, :, 1:2].rearrange("p b a -> p (b a)"), ACT.Sqrt,
                           bias=cc("eps4")).then_inc(ln_std, 1)

            def gate_tile(sig, pan, chunk, col):
                act.wait_ge(panel_free, pan + 1)
                act.activation(SIG[:, sig, :], SIG[:, sig, :], ACT.Tanh, scale=0.5,
                               bias=BH[:, col:col + 1]).then_inc(sig_ready, 1)
                w_hi(chunk + 3)

            gate_tile(4, P_MRG, C_MRG, KT)
            gate_tile(5, P_MRG + 1, C_MRG + 1, KT + 1)
            for g in range(4):
                act.wait_ge(sgu_out, g + 1)
                act.activation(OSH[:, g, :], Z[:, 2 + g % 2, :], ACT.Copy).then_inc(oshi_ready, 1)
            gate_tile(6, P_MRG + 2, C_MRG + 2, KT + 2)
            gate_tile(7, P_MRG + 3, C_MRG + 3, KT + 3)
            for half in range(2):
                for k in range(4):
                    n = 4 * half + k
                    act.wait_ge(mix_ready, n + 1)
                    act.activation(MXH[:, n, :], Z[:, 2 * (k % 2), :], ACT.Copy, scale=0.5).then_inc(mixhi_ready, 1)
                    w_hi(C_MRG + (4 if half == 0 else 16) + k + 3)
                if half == 0:
                    act.wait_ge(oslo_ready, 4)
                    act.dma_start(H[:, :, :], xT).then_inc(h_loaded, 16)
                    act.dma_start(MRAW[:, :, :], memT).then_inc(mem_loaded, 16)
                    for k in range(4):
                        gate_tile(k, P_MRG + 12 + k, C_MRG + 8 + k, 4 + k)
                    act.wait_ge(mem_loaded, 16)
                    act.activation(MSQ[:, :, :], MRAW[:, :, :], ACT.Square).then_inc(memsq_ready, 1)
                    for k in range(4):
                        gate_tile(4 + k, P_MRG + 16 + k, C_MRG + 12 + k, KT + 4 + k)
                        if k == 2:
                            root(F_MEMRMS, MEM, SB[F_MEMRMS % 3], RSM[:, :])

            with act.Fori(0, 2) as r:
                for k in range(4):
                    n = r * 4 + k
                    act.activation(tile_of(MHH, n),
                                   tile_of(MRAW, n), ACT.Copy,
                                   scale=CST[:, bass.ds(n + COL["gmem"][0], 1)]).then_inc(memhi_ready, 1)
                    act.wait_ge(h_ready, n + 1)
                    act.wait_ge(acc_ready, n + (KT - 1))
                    hn = tile_of(H, n)
                    act.activation(tile_of(XH, n), hn, ACT.Copy,
                                   scale=CST[:, bass.ds(n + COL["gq"][0], 1)]).then_inc(xhi_ready, 1)
                    act.activation(SQ[:, k % 2, :], hn, ACT.Square).then_inc(sq_ready, 1)
                    i = C_OUT + 3 + k
                    w_hi(i, i % SLOTS, r * 16 + (i // SLOTS + 1) * 16)
            w_hi(C_X + 3)
            root(F_QRMS, T, SB[F_QRMS % 3], RS[:, :])

            def cross_exp(n):
                for qb in range(TB):
                    if qb % 2 == 0:
                        act.wait_ge(p_max, 2 * n + qb // 2 + 1)
                    j = 4 * (n % 2) + qb
                    bank = SB[(F_CROSS + 2 * n + qb // 2) % 3]
                    ins = act.activation(P2[:, n % 2, qb, :], bank[:, (qb % 2) * MEM:(qb % 2 + 1) * MEM], ACT.Exp,
                                         bias=MN[:, j:j + 1], scale=-1.0, accum_out=DEN[:, j:j + 1])
                    if qb % 2:
                        ins.then_inc(s_free, 1)

            def cross_turned(n):
                for b in range(MB):
                    k = R_CT[n] + b
                    act.wait_ge(r_done, k + 1)
                    act.activation(PT2[:, n % 2, b, :], RB[k % 2][:, :], ACT.Copy).then_inc(r_free, 1)

            def cross_o(n):
                act.wait_ge(o_done, PAIRS + n + 1)
                act.activation(OXH[:, n, :], OB[:, :], ACT.Copy).then_inc(onhi_ready, 1)

            def memory_values(n):
                act.wait_ge(r_done, R_VT[n] + 1)
                act.activation(MV[:, :, n * P:(n + 1) * P], RB[R_VT[n] % 2][:, 0:MEM].rearrange(
                    "p (b c) -> p b c", b=MB), ACT.Copy).then_inc(r_free, 1)

            w_hi(C_X + 4)
            w_hi(C_X + 5)
            cross_exp(0)
            w_hi(C_X + 6)
            memory_values(0)
            w_hi(C_X + 7)
            cross_turned(0)
            cross_exp(1)
            w_hi(C_X + 8)
            w_hi(C_X + 9)
            cross_o(0)
            cross_turned(1)
            w_hi(C_X + 10)
            memory_values(1)
            cross_exp(2)
            cross_o(1)
            w_hi(C_X + 11)
            w_hi(C_MO)
            memory_values(2)
            w_hi(C_MO + 1)
            cross_exp(3)
            cross_turned(2)
            cross_o(2)
            memory_values(3)
            w_hi(C_MO + 2)
            cross_turned(3)
            cross_o(3)
            for k in range(KT):
                n = k
                act.wait_ge(h_ready, KT + n + 1)
                act.activation(XH[:, n, :], H[:, n, :], ACT.Copy, scale=cc("gf", n, n + 1)).then_inc(xhi_ready, 1)
                act.wait_ge(acc_ready, 2 * KT + n - 1)
                act.activation(SQ[:, k % 2, :], H[:, n, :], ACT.Square).then_inc(sq_ready, 1)
                if k % 2:
                    w_hi(C_MO + k // 2 + 3)
            root(F_FRMS, T, SB[F_FRMS % 3], RS[:, :])
            with act.Fori(0, FT // 2) as r:
                for k in range(2):
                    j = r * 2 + k
                    act.wait_ge(panel_free, r * 4 + (FREE_GU + 2 * k + 1))
                    act.activation(Z[:, 2 * k + 1, :], Z[:, 2 * k, :], ACT.Tanh, scale=0.5).then_inc(act_tanh, 1)
                    for m in range(2):
                        i = C_GU + 3 + 2 * k + m
                        w_hi(i, i % SLOTS, (i // SLOTS + 1) * 16 + r * 16)
                    act.wait_ge(hid_ready, j + 1)
                    act.activation(tile_of(HH, j), Z[:, 2 * k, :], ACT.Copy,
                                   scale=0.5).then_inc(hidhi_ready, 1)
            for n in range(KT):
                for m in range(3):
                    if C_DN + 3 * n + m + 3 < NCHUNK:
                        w_hi(C_DN + 3 * n + m + 3)
                if n == KT - 1:
                    act.activation(LS[:, 0:1], ONES[:, 0:1], ACT.Sqrt)
                act.wait_ge(h_ready, 2 * KT + n + 1)
                act.wait_ge(acc_ready, 3 * KT + n - 1)
                act.activation(SQ[:, n % 2, :], H[:, n, :], ACT.Square).then_inc(sq_ready, 1)
                if n == 5:
                    act.wait_ge(final_turned, 1)
                    for b in range(TB):
                        ins = act.activation(OUTK[:, b, 0:T], FB[b][:, :], ACT.Copy)
                    ins.then_inc(final_copied, 1)
            act.wait_ge(mean_done, 1)
            act.activation(RF[:, :], OB[:, 0:TB], ACT.Sqrt, bias=cc("eps")).then_inc(root_done, 1)
            act.wait_ge(last_turned, 1)
            act.wait_ge(rf_ready, 1)
            for b in range(TB):
                act.activation(OUTK[:, b, T:D], FB[b][:, :], ACT.Copy, scale=RF[:, b:b + 1]).then_inc(last_out, 1)

        @block.vector
        def _(dve):
            st = Steps()

            def chain():
                dve.wait_ge(dve_step, st.now())

            def x_lo(n, gain, count):
                dve.wait_ge(xhi_ready, count + 1)
                dve.scalar_tensor_tensor(XL[:, n, :], H[:, n, :], gain, XH[:, n, :].bitcast(F32),
                                         ALU.mult, ALU.subtract).then_inc(xlo_ready, 1)

            def add_square(count, square):
                dve.wait_ge(sq_ready, count + 1)
                if count == 0:
                    dve.tensor_copy(ACC[:, :], square).then_inc(acc_ready, 1)
                else:
                    dve.wait_ge(acc_ready, count)
                    dve.tensor_tensor(ACC[:, :], ACC[:, :], square, ALU.add).then_inc(acc_ready, 1)

            def inverse(n_root, dst):
                dve.wait_ge(rms_ready, n_root)
                dve.reciprocal(dst, dst).then_inc(s_free, 1)

            def times_rms(p, dst, w=T, rs=None, lo=0, hi=P, dlo=None):
                rs = RS if rs is None else rs
                return dve.tensor_tensor(dst, LB[p % 2][lo:hi, 0:w], rs[lo:hi, 0:w], ALU.mult)

            dve.wait_ge(cst_loaded, 16)
            for n in range(KT):
                x_lo(n, cc("gmix", n, n + 1), n)
                if n >= 4:
                    add_square(n - 4, Z[:, n % 4, :])
            for n in range(4, KT):
                add_square(n, Z[:, n % 4, :])
            dve.tensor_scalar(BH[:, :], cc("bm"), 0.5, None, ALU.mult).then_inc(o_free, 1)
            inverse(1, RS[:, :])
            dve.memset(KR[:, :, KC_:KEYW], 0.0).then_inc(dve_step, st.add())
            dve.memset(KV[:, :, VC_:KVW], 0.0).then_inc(dve_step, st.add())
            dve.wait_ge(s_free, F_XRMS + 1)
            for s in range(2):
                dve.wait_ge(chunk_used, C_IN + s + 1)
                times_rms(C_IN + s, KC[:, s, :]).then_inc(panel_free, 1)
            for s in range(2):
                dve.wait_ge(panel_free, C_IN + s + 1)
                if s == 0:
                    dve.wait_ge(tables_loaded, 16)
                pe, _ = COL["pe"]
                for g in range(2):
                    for par in range(2):
                        for a in range(2):
                            src = KC[g * HD:(g + 1) * HD, s, :].rearrange(
                                "p (m b r) -> p r b m", b=8, r=2)[:, par, :, a:a + NCMP]
                            p0 = pe + (s * 2 + par) * CJ + 8 * a
                            pv = CST[g * HD:(g + 1) * HD, p0:p0 + 8]
                            dst = G[par * HD:(par + 1) * HD, s, 8 * a:8 * a + 8, g * NCMP:(g + 1) * NCMP]
                            ins = dve.tensor_tensor(dst, src, pv.unsqueeze(2).broadcast_to((HD, 8, NCMP)), ALU.add)
                ins.then_inc(g_ready, 1)

            def keys_in(p, off, bank):
                dve.wait_ge(chunk_used, p + 1)
                for g in range(2):
                    for half in range(2):
                        ins = dve.tensor_tensor(KR[half * HD:(half + 1) * HD, g, off:off + T],
                                                LB[bank][g * HD:(g + 1) * HD, :], RS[g * HD:(g + 1) * HD, :], ALU.mult)
                ins.then_inc(panel_free, 1)

            def keys_lo(n, off, width):
                dve.wait_ge(keyhi_ready, n)
                dve.tensor_tensor(KL[:, :, off:off + width], KR[:, :, off:off + width],
                                  KH[:, :, off:off + width].bitcast(F32), ALU.subtract).then_inc(keylo_ready, 1)

            keys_in(C_IN + 2, KS, 2)
            dve.wait_ge(chunk_used, C_IN + 4)
            times_rms(C_IN + 3, Z[:, 2, :]).then_inc(panel_free, 1)
            for g in range(4):
                w = CST[:, COL["ws"][0] + g * P:COL["ws"][0] + (g + 1) * P]
                dve.tensor_tensor(w, w, cc("tri"), ALU.mult)
            dve.wait_ge(s_done, F_HID + 1)
            dve.tensor_copy(HZ[:, 0, :], SB[F_HID % 3][:, 0:4 * NCMP]).then_inc(s_free, 1)
            dve.wait_ge(gelu_sq, 1)
            dve.tensor_scalar(HZ[:, 1, :], HZ[:, 1, :], GA, 1.0, ALU.mult, ALU.add).then_inc(dve_step, st.add())
            chain()
            dve.tensor_tensor(HZ[:, 1, :], HZ[:, 1, :], HZ[:, 0, :], ALU.mult).then_inc(gelu_arg, 1)
            dve.wait_ge(gelu_tanh, 1)
            dve.scalar_tensor_tensor(HZ[:, 1, :], HZ[:, 1, :], 1.0, HZ[:, 0, :], ALU.add,
                                     ALU.mult).then_inc(gelu_done, 1)
            dve.wait_ge(chunk_used, C_IN + 5)
            times_rms(C_IN + 4, Z[:, 3, :]).then_inc(panel_free, 1)
            dve.wait_ge(s_done, F_CMP + 1)
            for g in range(2):
                dve.tensor_scalar(KR[:, g, KC_:KC_ + NCMP], SB[F_CMP % 3][:, g * NCMP:(g + 1) * NCMP], 0.5, None,
                                  ALU.mult)
                ins = dve.tensor_scalar(KV[0:NCMP, g, VC_:VC_ + HD],
                                        SB[F_CMP % 3][0:NCMP, P + g * HD:P + (g + 1) * HD],
                                        0.5, None, ALU.mult)
            ins.then_inc(s_free, 1)
            dve.wait_ge(chunk_used, C_IN + 6)
            times_rms(C_IN + 5, Z[:, 0, :]).then_inc(panel_free, 1)
            keys_lo(1, KS, T)
            keys_lo(2, KC_, 32)
            dve.wait_ge(vchi_ready, 1)
            dve.tensor_tensor(VCR[64:96, :, :], KV[0:32, :, VC_:KVW], VCR[0:32, :, :].bitcast(F32), ALU.subtract)
            dve.wait_ge(r_free, R_GATE + 1)
            dve.tensor_scalar(GT[:, :, :], GT[:, :, :], 0.5, 0.5, ALU.mult, ALU.add).then_inc(gates_ready, 1)
            keys_in(C_IN + 6, KW, (C_IN + 6) % 2)
            keys_lo(3, KW, T)

            with dve.Fori(0, PAIRS) as c:
                st.enter(c, 20)
                pan, fil = P_ATT + c * 4, F_ATT + c * F_PAIR

                def scores(u, qb0, qb1):
                    e = u // 2
                    for qb in range(qb0, qb1):
                        k = 2 + 4 * u + qb
                        w = (qb + 1) * P
                        j = 4 * u + qb
                        dve.wait_ge(s_done, fil + (k + 1))
                        dve.memset(HOLD[:, j:j + 1], 0.0)
                        dve.tensor_tensor_reduce(PP[:, u % 2, unit_off(qb):unit_off(qb) + w],
                                                 SB[(F_ATT + k) % 3][:, 0:w], DN[:, e, 384 - P * qb:512], 1.0, 3e38,
                                                 ALU.add, ALU.min, MN[:, j:j + 1]).then_inc(s_free, 1)

                def weigh(u):
                    e, br = u // 2, u % 2
                    dve.wait_ge(p_exp, c * 4 + (u + 1))
                    dve.reciprocal(RD[:, 4 * u:4 * u + 4], DEN[:, 4 * u:4 * u + 4]).then_inc(dve_step, st.add())
                    chain()
                    gate = GT[:, :, bass.ds(c * 6 + (3 * e + 1 + br), 1)].rearrange("p b a -> p (b a)")
                    dve.tensor_tensor(RD[:, 4 * u:4 * u + 4], RD[:, 4 * u:4 * u + 4], gate,
                                      ALU.mult).then_inc(dve_step, st.add())
                    chain()
                    for qb in range(TB):
                        sl = PP[:, u % 2, unit_off(qb):unit_off(qb) + (qb + 1) * P]
                        ins = dve.tensor_scalar(sl, sl, RD[:, 4 * u + qb:4 * u + qb + 1], None, ALU.mult)
                    ins.then_inc(p_ready, 1)

                def gelu_a(n, z):
                    dve.wait_ge(gelu_sq, n)
                    dve.tensor_scalar(Z[:, z + 1, :], Z[:, z + 1, :], GA, 1.0, ALU.mult, ALU.add).then_inc(dve_step, st.add())
                    chain()
                    dve.tensor_tensor(Z[:, z + 1, :], Z[:, z + 1, :], Z[:, z, :], ALU.mult).then_inc(gelu_arg, 1)

                dve.wait_ge(chunk_used, C_ATT + 1 + c * 4)
                dve.scalar_tensor_tensor(Q[:, :], LB[P_ATT % 2][:, :], -(float(HD) ** -0.5), RS[:, :],
                                         ALU.mult, ALU.mult).then_inc(panel_free, 1)
                for e in range(2):
                    own, other = slice(e * HD, (e + 1) * HD), slice((1 - e) * HD, (2 - e) * HD)
                    dve.wait_ge(qhi_ready, c * 2 + (e + 1))
                    dve.tensor_tensor(QS[other, e, :], Q[own, :], QS[own, e, :].bitcast(F32),
                                      ALU.subtract).then_inc(q_ready, 1)
                dve.wait_ge(dn_staged, c + 1)
                for e in range(2):
                    dve.wait_ge(s_done, fil + (e + 1))
                    pc = PC[:, e, :, 0:NCMP]
                    dve.tensor_tensor(pc,
                                      SB[(F_ATT + e) % 3][:, 0:P].rearrange("p (b i) -> p b i", b=TB)[:, :, 0:NCMP],
                                      DN[:, e, 512:640].rearrange("p (b i) -> p b i", b=TB)[:, :, 0:NCMP],
                                      ALU.add).then_inc(s_free, 1)
                    dve.wait_ge(s_free, fil + (e + 1))
                    dve.tensor_reduce(MC[:, e, :], pc, AX, ALU.min).then_inc(dve_step, st.add())
                    chain()
                    dve.tensor_tensor(pc, pc, MC[:, e, :].unsqueeze(2).broadcast_to((P, TB, NCMP)),
                                      ALU.subtract).then_inc(cmp_arg, 1)
                def cmp_weigh(e):
                    dve.wait_ge(cmp_exp, c * 2 + (e + 1))
                    pc = PC[:, e, :, 0:NCMP]
                    dve.tensor_reduce(DC[:, e, :], pc, AX, ALU.add).then_inc(dve_step, st.add())
                    chain()
                    dve.reciprocal(RC[:, e, :], DC[:, e, :]).then_inc(dve_step, st.add())
                    chain()
                    gate = GT[:, :, bass.ds(c * 6 + 3 * e, 1)].rearrange("p b a -> p (b a)")
                    dve.tensor_tensor(RC[:, e, :], RC[:, e, :], gate, ALU.mult).then_inc(dve_step, st.add())
                    chain()
                    dve.tensor_tensor(RC[:, e, :], RC[:, e, :], cc("valid"), ALU.mult).then_inc(dve_step, st.add())
                    chain()
                    dve.tensor_tensor(pc, pc, RC[:, e, :].unsqueeze(2).broadcast_to((P, TB, NCMP)),
                                      ALU.mult).then_inc(cmp_prob, 1)

                def cmp_lo(e):
                    dve.wait_ge(cmp_hi, c * 2 + (e + 1))
                    dve.tensor_tensor(PCS[:, e, :, 32:32 + NCMP], PC[:, e, :, 0:NCMP],
                                      PCS[:, e, :, 0:NCMP].bitcast(F32),
                                      ALU.subtract).then_inc(cmp_ready, 1)

                scores(0, 0, 2)
                cmp_weigh(0)
                scores(0, 2, TB)
                scores(1, 0, 2)
                cmp_weigh(1)
                scores(1, 2, TB)
                cmp_lo(0)
                weigh(0)
                cmp_lo(1)
                dve.wait_ge(chunk_used, C_ATT + 2 + c * 4)
                times_rms(P_ATT + 1, Z[:, 0, :]).then_inc(panel_free, 1)
                weigh(1)
                gelu_a(c * 2 + 2, 0)
                dve.wait_ge(chunk_used, C_ATT + 3 + c * 4)
                times_rms(P_ATT + 2, Z[:, 2, :]).then_inc(panel_free, 1)
                scores(2, 0, TB)
                dve.wait_ge(gelu_tanh, c * 2 + 2)
                dve.scalar_tensor_tensor(tile_of(U, c), Z[:, 1, :], 1.0, Z[:, 0, :],
                                         ALU.add, ALU.mult).then_inc(gelu_done, 1)
                gelu_a(c * 2 + 3, 2)
                weigh(2)
                scores(3, 0, 3)
                dve.wait_ge(gelu_tanh, c * 2 + 3)
                dve.scalar_tensor_tensor(Z[:, 3, :], Z[:, 3, :], 1.0, Z[:, 2, :], ALU.add,
                                         ALU.mult).then_inc(gelu_done, 1)
                scores(3, 3, TB)
                weigh(3)
                dve.wait_ge(chunk_used, C_ATT + 4 + c * 4)
                times_rms(P_ATT + 3, tile_of(SIG, c)).then_inc(panel_free, 1)
                dve.wait_ge(onhi_ready, c + 1)
                dve.tensor_tensor(tile_of(ONL, c), OB[:, :],
                                  tile_of(ONH, c).bitcast(F32),
                                  ALU.subtract).then_inc(o_free, 1)
            st.leave(PAIRS)

            dve.wait_ge(r_free, R_X)
            for b in range(TB):
                ins = dve.bn_stats(BN[:, b, :], VT[:, b, :])
            ins.then_inc(dve_step, st.add())
            chain()
            for b in range(TB):
                ins = dve.bn_aggr(BA[:, b, :], BN[:, b, :])
            ins.then_inc(ln_var, 1)
            dve.wait_ge(ln_std, 1)
            dve.reciprocal(LS[:, :], LS[:, :]).then_inc(dve_step, st.add())
            chain()
            for b in range(TB):
                dve.tensor_scalar(VT[:, b, :], VT[:, b, :], BA[:, b, 0:1], LS[:, b:b + 1], ALU.subtract,
                                  ALU.mult).then_inc(vn_ready, 1)

            def gate_in(sig, pan, chunk):
                dve.wait_ge(chunk_used, chunk + 1)
                times_rms(pan, SIG[:, sig, :]).then_inc(panel_free, 1)

            gate_in(4, P_MRG, C_MRG)
            gate_in(5, P_MRG + 1, C_MRG + 1)
            dve.wait_ge(bsp_loaded, 16)
            for g in range(4):
                n = F_SGU + g
                dve.wait_ge(s_done, n + 1)
                dve.scalar_tensor_tensor(Z[:, 0, :].rearrange("p (b t) -> p b t", b=TB),
                                         SB[n % 3][:, :].rearrange("p (b t) -> p b t", b=TB),
                                         cc("lng", g, g + 1), BB[:, g, :].unsqueeze(1).broadcast_to((P, TB, P)),
                                         ALU.mult, ALU.add).then_inc(s_free, 1)
                dve.wait_ge(s_free, n + 1)
                if g >= 2:
                    dve.wait_ge(oshi_ready, g - 1)
                dve.scalar_tensor_tensor(Z[:, 2 + g % 2, :], Z[:, 0, :], 0.5, U[:, g, :], ALU.mult,
                                         ALU.mult).then_inc(sgu_out, 1)
                dve.wait_ge(oshi_ready, g + 1)
                dve.tensor_tensor(OSL[:, g, :], Z[:, 2 + g % 2, :], OSH[:, g, :].bitcast(F32),
                                  ALU.subtract).then_inc(oslo_ready, 1)
            gate_in(6, P_MRG + 2, C_MRG + 2)
            gate_in(7, P_MRG + 3, C_MRG + 3)
            for half in range(2):
                for k in range(4):
                    n = 4 * half + k
                    pan = P_AB[n]
                    dve.wait_ge(sig_ready, PAIRS + 4 + 8 * half)
                    dve.wait_ge(panel_half, n + 1)
                    dve.scalar_tensor_tensor(Z[:, 2 * (k % 2), :], SIG[:, k, :], 1.0, LB[pan % 2][:, :], ALU.add,
                                             ALU.mult).then_inc(panel_free, 1)
                    dve.wait_ge(chunk_used, C_AB[n] + 1)
                    dve.scalar_tensor_tensor(Z[:, 2 * (k % 2) + 1, :], SIG[:, 4 + k, :], 1.0,
                                             LB[(pan + 1) % 2][:, :], ALU.add, ALU.mult).then_inc(panel_free, 1)
                    dve.wait_ge(panel_free, pan + 2)
                    dve.tensor_tensor(Z[:, 2 * (k % 2), :], Z[:, 2 * (k % 2), :], Z[:, 2 * (k % 2) + 1, :],
                                      ALU.add).then_inc(mix_ready, 1)
                    dve.wait_ge(mixhi_ready, n + 1)
                    dve.scalar_tensor_tensor(MXL[:, n, :], Z[:, 2 * (k % 2), :], 0.5, MXH[:, n, :].bitcast(F32),
                                             ALU.mult, ALU.subtract).then_inc(mixlo_ready, 1)
                if half == 0:
                    for k in range(4):
                        gate_in(k, P_MRG + 12 + k, C_MRG + 8 + k)
                    dve.wait_ge(memsq_ready, 1)
                    dve.tensor_reduce(MSUM, MSQ[:, :, :].rearrange("p k t -> p t k"), AX,
                                      ALU.add).then_inc(memsum_ready, 1)
                    for k in range(4):
                        gate_in(4 + k, P_MRG + 16 + k, C_MRG + 12 + k)
                        if k == 2:
                            inverse(2, RSM[:, :])

            def clear_sum():
                dve.memset(ACC[:, :], 0.0).then_inc(dve_step, st.add())
                chain()

            clear_sum()
            dve.wait_ge(h_loaded, 16)
            dve.wait_ge(s_free, F_MEMRMS + 1)
            with dve.Fori(0, 2) as r:
                for k in range(4):
                    n = r * 4 + k
                    hn = tile_of(H, n)
                    dve.wait_ge(memhi_ready, n + 1)
                    dve.scalar_tensor_tensor(tile_of(MHL, n),
                                             tile_of(MRAW, n),
                                             CST[:, bass.ds(n + COL["gmem"][0], 1)],
                                             tile_of(MHH, n).bitcast(F32),
                                             ALU.mult, ALU.subtract).then_inc(memlo_ready, 1)
                    dve.wait_ge(chunk_used, n + (C_OUT + 1))
                    dve.tensor_tensor(hn, hn, LB[(P_OUT + k) % 2][:, :], ALU.add).then_inc(h_ready, 1)
                    dve.wait_ge(h_ready, n + 1)
                    dve.wait_ge(xhi_ready, n + (KT + 1))
                    dve.scalar_tensor_tensor(tile_of(XL, n), hn,
                                             CST[:, bass.ds(n + COL["gq"][0], 1)],
                                             tile_of(XH, n).bitcast(F32),
                                             ALU.mult, ALU.subtract).then_inc(xlo_ready, 1)
                    dve.wait_ge(sq_ready, n + (KT + 1))
                    dve.wait_ge(acc_ready, n + KT)
                    dve.tensor_tensor(ACC[:, :], ACC[:, :], SQ[:, k % 2, :], ALU.add).then_inc(acc_ready, 1)

            def cross_q(n):
                j = CROSS.index(f"q{n}")
                dve.wait_ge(chunk_used, C_X + j + 1)
                dve.scalar_tensor_tensor(HQ[:, n % 2, :], LB[(P_X + j) % 2][:, :], -SC_MEM, RS[:, :],
                                         ALU.mult, ALU.mult).then_inc(panel_free, 1)

            def memory_key(n):
                j = CROSS.index(f"k{n}")
                dve.wait_ge(chunk_used, C_X + j + 1)
                times_rms(P_X + j, MK[:, n, :], MEM, RSM).then_inc(panel_free, 1)

            def memory_value(n):
                j = CROSS.index(f"v{n}")
                dve.wait_ge(chunk_used, C_X + j + 1)
                if n >= 2:
                    dve.wait_ge(r_done, R_VT[n - 2] + 1)
                times_rms(P_X + j, Z[:, n % 2, 0:MEM], MEM, RSM).then_inc(panel_free, 1)

            def cross_max(n):
                for f in range(2):
                    k = F_CROSS + 2 * n + f
                    dve.wait_ge(s_done, k + 1)
                    j = 4 * (n % 2) + 2 * f
                    dve.tensor_reduce(MN[:, j:j + 2], SB[k % 3][:, :].rearrange("p (b m) -> p b m", b=2), AX,
                                      ALU.min).then_inc(p_max, 1)

            def cross_weigh(n):
                dve.wait_ge(s_free, F_CROSS + 2 * n + 2)
                j = 4 * (n % 2)
                dve.reciprocal(RD[:, j:j + 4], DEN[:, j:j + 4]).then_inc(dve_step, st.add())
                chain()
                for qb in range(TB):
                    ins = dve.tensor_scalar(P2[:, n % 2, qb, :], P2[:, n % 2, qb, :], RD[:, j + qb:j + qb + 1],
                                            None, ALU.mult)
                ins.then_inc(p_ready, 1)

            def cross_o_lo(n):
                dve.wait_ge(onhi_ready, PAIRS + n + 1)
                dve.tensor_tensor(OXL[:, n, :], OB[:, :], OXH[:, n, :].bitcast(F32), ALU.subtract).then_inc(o_free, 1)

            memory_key(0)
            memory_key(1)
            inverse(3, RS[:, :])
            dve.wait_ge(s_free, F_QRMS + 1)
            cross_q(0)
            clear_sum()
            memory_value(0)
            cross_max(0)
            cross_weigh(0)
            cross_q(1)
            cross_max(1)
            memory_value(1)
            cross_weigh(1)
            memory_key(2)
            cross_o_lo(0)
            cross_q(2)
            memory_value(2)
            cross_max(2)
            cross_o_lo(1)
            cross_weigh(2)
            memory_key(3)
            cross_q(3)
            cross_max(3)
            cross_weigh(3)
            memory_value(3)
            cross_o_lo(2)
            cross_o_lo(3)
            for n in range(KT):
                if n % 2 == 0:
                    dve.wait_ge(panel_half, KT + n // 2 + 1)
                else:
                    dve.wait_ge(chunk_used, C_MO + n // 2 + 1)
                dve.tensor_tensor(H[:, n, :], H[:, n, :], LB[(P_MO + n) % 2][:, :], ALU.add).then_inc(h_ready, 1)
                dve.wait_ge(xhi_ready, 2 * KT + n + 1)
                dve.scalar_tensor_tensor(XL[:, n, :], H[:, n, :], cc("gf", n, n + 1), XH[:, n, :].bitcast(F32),
                                         ALU.mult, ALU.subtract).then_inc(xlo_ready, 1)
                add_square(2 * KT + n, SQ[:, n % 2, :])
            inverse(4, RS[:, :])
            dve.wait_ge(s_free, F_FRMS + 1)
            with dve.Fori(0, FT // 2) as r:
                st.enter(r, 2)
                for k in range(2):
                    j = r * 2 + k
                    zg, zt, zu = Z[:, 2 * k, :], Z[:, 2 * k + 1, :], SQ[:, k, :]
                    dve.wait_ge(chunk_used, r * 4 + (C_GU + 2 * k + 1))
                    times_rms(P_GU + 2 * k, zg).then_inc(panel_free, 1)
                    dve.wait_ge(act_tanh, j + 1)
                    dve.scalar_tensor_tensor(zt, zt, 1.0, zg, ALU.add, ALU.mult).then_inc(dve_step, st.add())
                    dve.wait_ge(chunk_used, r * 4 + (C_GU + 2 * k + 2))
                    times_rms(P_GU + 2 * k + 1, zu).then_inc(panel_free, 1)
                    chain()
                    dve.wait_ge(panel_free, r * 4 + (FREE_GU + 2 * k + 2))
                    dve.tensor_tensor(zg, zt, zu, ALU.mult).then_inc(hid_ready, 1)
                    dve.wait_ge(hidhi_ready, j + 1)
                    dve.scalar_tensor_tensor(tile_of(HL, j), zg, 0.5,
                                             tile_of(HH, j).bitcast(F32),
                                             ALU.mult, ALU.subtract).then_inc(hidlo_ready, 1)
            st.leave(FT // 2)
            clear_sum()
            for n in range(KT):
                dve.wait_ge(chunk_used, C_DN + 3 * n + 3)
                dve.tensor_tensor(H[:, n, :], H[:, n, :], LB[(P_DN + n) % 2][:, :], ALU.add).then_inc(h_ready, 1)
                dve.wait_ge(h_ready, 2 * KT + n + 1)
                dve.tensor_scalar(HG[:, n, :], H[:, n, :], cc("gfin", n, n + 1), None,
                                  ALU.mult).then_inc(scaled_ready, 1)
                if n < KT - 1:
                    add_square(3 * KT + n, SQ[:, n % 2, :])
            dve.wait_ge(root_done, 1)
            dve.reciprocal(RF[:, :], RF[:, :]).then_inc(rf_ready, 1)
            dve.wait_ge(rf_ready, 1)
            dve.wait_ge(final_copied, 1)
            for b in range(TB):
                dve.tensor_scalar(OUTK[:, b, 0:T], OUTK[:, b, 0:T], RF[:, b:b + 1], None,
                                  ALU.mult).then_inc(first_out, 1)

        @block.tensor
        def _(pe):
            def bank_free(p):
                q = p - 2
                if q < 0:
                    return None, 0
                if q < P_OUT:
                    return panel_free, q + 1
                if q < P_X:
                    return h_ready, q - P_OUT + 1
                if q < P_MO:
                    return panel_free, FREE_X + q - P_X + 1
                if q < P_GU:
                    return h_ready, KT + q - P_MO + 1
                if q < P_DN:
                    return panel_free, FREE_GU + q - P_GU + 1
                return h_ready, 2 * KT + q - P_DN + 1

            def panel(i, bank, units, w=T, shift=None, first=True, last=True, done=None, ready=None):
                s = i % SLOTS
                if shift is None:
                    pe.wait_ge(lo_ready, i + 1)
                else:
                    pe.wait_ge(lo_ready, shift + (i + 1))
                for m, (u, hi, lo) in enumerate(units):
                    if ready is not None:
                        pe.wait_ge(ready[0], ready[1] + m)
                    end = last and m == len(units) - 1
                    dst = LB[bank][:, 0:w]
                    pe.matmul(dst, WH[:, s, u, :], hi, start=first and m == 0, stop=False)
                    pe.matmul(dst, WH[:, s, u, :], lo, start=False, stop=False)
                    ins = pe.matmul(dst, WL[:, s, u, :], hi, start=False, stop=end)
                if last or len(units) == KT:
                    ins.then_inc(chunk_used if done is None else done, 1)

            def free(p):
                s, v = bank_free(p)
                if s is not None:
                    pe.wait_ge(s, v)

            X = [(k, XH[:, k, :], XL[:, k, :]) for k in range(KT)]

            def s_bank(n, turn=None):
                if n >= 3:
                    pe.wait_ge(s_free, n - 2 if turn is None else turn * F_PAIR + (n - 2))
                return SB[n % 3]

            def r_bank(n, turn=None):
                if n >= 2:
                    pe.wait_ge(r_free, n - 1 if turn is None else turn * R_PAIR + (n - 1))
                return RB[n % 2]

            def mean_square(n, count):
                pe.wait_ge(acc_ready, count)
                pe.matmul(s_bank(n)[:, :], ONES[:, :], ACC[:, :], start=True, stop=True).then_inc(s_done, 1)

            pe.wait_ge(ones_ready, 1)
            for _ in range(WARM):
                pe.matmul(OB[:, 0:P], ONES[:, :], ONES[:, :], start=True, stop=True)
            def turn_values(n, p, z):
                pe.wait_ge(panel_free, p + 1)
                bank = r_bank(n)
                for b in range(TB):
                    ins = pe.transpose(bank[:, b * P:(b + 1) * P], Z[:, z, b * P:(b + 1) * P], IDENT)
                ins.then_inc(r_done, 1)

            def hi_products(i, k0, k1):
                pe.wait_ge(hi_ready, i + 1)
                for k in range(k0, k1):
                    pe.wait_ge(xlo_ready, k + 1)
                    pe.matmul(LB[i][:, :], WH[:, i, k, :], XH[:, k, :], start=k == 0, stop=False)
                    pe.matmul(LB[i][:, :], WH[:, i, k, :], XL[:, k, :], start=False, stop=False)

            def lo_products(i, k0, k1):
                pe.wait_ge(lo_ready, i + 1)
                for k in range(k0, k1):
                    ins = pe.matmul(LB[i][:, :], WL[:, i, k, :], XH[:, k, :], start=False, stop=k == KT - 1)
                if k1 == KT:
                    ins.then_inc(chunk_used, 1)

            hi_products(0, 0, 4)
            hi_products(1, 0, 4)
            hi_products(0, 4, 6)
            hi_products(1, 4, 6)
            hi_products(0, 6, KT)
            hi_products(1, 6, KT)
            lo_products(0, 0, KT)
            lo_products(1, 0, 4)
            mean_square(F_XRMS, KT)
            lo_products(1, 4, KT)
            for j in range(2, N_IN):
                i = C_IN + j
                if j > 2:
                    free(i)
                panel(i, 2 if j == 2 else i % 2, X)
                if j == 3:
                    pe.wait_ge(w1_loaded, 16)
                    pe.wait_ge(tables_loaded, 16)
                    pe.wait_ge(g_ready, 2)
                    bank = s_bank(F_HID)
                    for s in range(2):
                        for u in range(CJ):
                            ins = pe.matmul(bank[:, s * 2 * NCMP:(s + 1) * 2 * NCMP], W1[:, s, u, :], G[:, s, u, :],
                                            start=u == 0, stop=u == CJ - 1)
                    ins.then_inc(s_done, 1)
                if j == 4:
                    turn_values(R_SLC, C_IN + 3, 2)
                    pe.wait_ge(gelu_done, 1)
                    bank = s_bank(F_CMP)
                    pe.matmul(bank[:, 0:2 * NCMP], cc("w2k"), HZ[:, 1, 0:2 * NCMP], start=True, stop=True)
                    for g in range(2):
                        a = (2 + g) * NCMP
                        ins = pe.matmul(bank[0:NCMP, P + g * HD:P + (g + 1) * HD], HZ[:, 1, a:a + NCMP], cc("w2v"),
                                        start=True, stop=True)
                    ins.then_inc(s_done, 1)
                if j == 5:
                    turn_values(R_WIN, C_IN + 4, 3)
            pe.wait_ge(panel_free, C_IN + 6)
            bank = r_bank(R_GATE)
            for b in range(TB):
                ins = pe.transpose(bank[:, b * 24:(b + 1) * 24], Z[0:24, 0, b * P:(b + 1) * P], IDENT[0:24, 0:24])
            ins.then_inc(r_done, 1)

            with pe.Fori(0, PAIRS) as c:
                def part(k, a, b):
                    p = P_ATT + k
                    if a == 0:
                        pe.wait_ge(panel_free, c * 4 + (p - 1))
                    panel(C_ATT + k, p % 2, X[a:b], shift=c * 4, first=a == 0, last=b == KT)

                def query_key(dst, e, qb, off, w):
                    for m, keys in enumerate((KH, KL)):
                        ins = pe.matmul(dst, QS[:, e, qb * P:(qb + 1) * P],
                                        keys[:, bass.ds(c // 2, 1), off:off + w].rearrange("p a n -> p (a n)"),
                                        start=m == 0, stop=m == 1)
                    return ins

                def scores(u, qb):
                    bank = s_bank(F_ATT + 2 + 4 * u + qb, c)
                    w = (qb + 1) * P
                    query_key(bank[:, 0:w], u // 2, qb, (KS, KW)[u % 2], w).then_inc(s_done, 1)

                def turn(u, f):
                    bank = r_bank(R_ATT + turn_fill(u, f), c)
                    if f == 0:
                        pe.wait_ge(p_ready, c * 4 + (u + 1))
                    at_ = 0
                    for kb in TURNS[f]:
                        for qb in range(kb, TB):
                            ins = pe.transpose(bank[:, at_:at_ + P],
                                               PP[:, u % 2, unit_off(qb) + kb * P:unit_off(qb) + (kb + 1) * P], IDENT)
                            at_ += P
                    ins.then_inc(r_done, 1)

                def values(u):
                    e, off = u // 2, (VS, VW)[u % 2]
                    for f in range(3):
                        pe.wait_ge(r_free, c * R_PAIR + (R_ATT + turn_fill(u, f) + 1))
                        for kb in TURNS[f]:
                            ins = pe.matmul(OB[e * HD:(e + 1) * HD, kb * P:T],
                                            KVS[:, off + kb * HD:off + (kb + 1) * HD],
                                            PT[:, u % 2, row_off(kb):row_off(kb) + (TB - kb) * P],
                                            start=False, stop=u % 2 == 1 and kb == 2, skip_group_check=True)
                    if u == 3:
                        ins.then_inc(o_done, 1)

                q, u, v, a = range(4)
                part(q, 0, KT)
                part(u, 0, 4)
                pe.wait_ge(keylo_ready, 2)
                for e in range(2):
                    pe.wait_ge(q_ready, c * 2 + (e + 1))
                    bank = s_bank(F_ATT + e, c)
                    for qb in range(TB):
                        ins = query_key(bank[:, qb * 32:(qb + 1) * 32], e, qb, KC_, 32)
                    ins.then_inc(s_done, 1)
                scores(0, 0)
                for qb in range(1, TB):
                    part(u, 3 + qb, 4 + qb)
                    scores(0, qb)
                part(u, 7, KT)
                pe.wait_ge(keylo_ready, 3)
                scores(1, 0)
                scores(1, 1)
                part(v, 0, 1)
                scores(1, 2)
                part(v, 1, 2)
                scores(1, 3)
                part(v, 2, 7)
                for e in range(2):
                    pe.wait_ge(cmp_ready, c * 2 + (e + 1))
                    bank = r_bank(R_ATT + e, c)
                    for qb in range(TB):
                        ins = pe.transpose(bank[0:96, qb * P:(qb + 1) * P], PCS[:, e, qb, :].bitcast(F32), IDENT)
                    ins.then_inc(r_done, 1)
                part(v, 7, KT)
                turn(0, 0)
                turn(0, 1)
                pe.wait_ge(kv_staged, c + 1)
                for e in range(2):
                    pe.wait_ge(r_free, c * R_PAIR + (R_ATT + e + 1))
                    pe.matmul(OB[:, :], VCS[:, (1 - e) * HD:(3 - e) * HD], PCT[:, e, :], start=e == 0, stop=False,
                              skip_group_check=True)
                turn(0, 2)
                scores(2, 0)
                scores(2, 1)
                part(a, 0, 1)
                scores(2, 2)
                part(a, 1, 2)
                scores(2, 3)
                turn(1, 0)
                turn(1, 1)
                values(0)
                turn(1, 2)
                scores(3, 0)
                scores(3, 1)
                part(a, 2, 3)
                scores(3, 2)
                scores(3, 3)
                values(1)
                pe.wait_ge(gelu_done, c * 2 + 3)
                for m in range(2):
                    bank = r_bank(R_ATT + 8 + m, c)
                    for b in range(2):
                        tb = 2 * m + b
                        ins = pe.transpose(bank[:, b * P:(b + 1) * P], Z[:, 3, tb * P:(tb + 1) * P], IDENT)
                    ins.then_inc(r_done, 1)
                part(a, 3, 4)
                turn(2, 0)
                turn(2, 1)
                part(a, 4, 5)
                turn(2, 2)
                part(a, 5, 6)
                values(2)
                turn(3, 0)
                turn(3, 1)
                part(a, 6, 7)
                turn(3, 2)
                part(a, 7, KT)
                values(3)

            def x_panel(i, p):
                free(p)
                panel(i, p % 2, X)

            def two_panels(n):
                free(P_AB[n])
                panel(C_AB[n], P_AB[n] % 2, [(k, ONH[:, k, :], ONL[:, k, :]) for k in range(4)], done=panel_half)
                free(P_AB[n] + 1)
                panel(C_AB[n], (P_AB[n] + 1) % 2, [(4 + k, OSH[:, k, :], OSL[:, k, :]) for k in range(4)])

            for k in range(4):
                x_panel(C_MRG + k, P_MRG + k)
                if k == 1:
                    pe.wait_ge(vn_ready, TB)
                    for g in range(4):
                        bank = s_bank(F_SGU + g)
                        ws, _ = COL["ws"]
                        for b in range(TB):
                            ins = pe.matmul(bank[:, b * P:(b + 1) * P], VT[:, b, g * P:(g + 1) * P],
                                            CST[:, ws + g * P:ws + (g + 1) * P], start=True, stop=True)
                        ins.then_inc(s_done, 1)
            pe.wait_ge(o_free, PAIRS + 1)
            pe.wait_ge(oslo_ready, 4)
            for n in range(4):
                two_panels(n)
            for k in range(8):
                x_panel(C_MRG + 8 + k, P_MRG + 12 + k)
                if k == 6:
                    pe.wait_ge(memsum_ready, 1)
                    pe.matmul(s_bank(F_MEMRMS)[:, 0:MEM], ONES[:, :], MSUM, start=True, stop=True).then_inc(s_done, 1)
            for n in range(4, 8):
                two_panels(n)
            MX = [(k, MXH[:, k, :], MXL[:, k, :]) for k in range(KT)]
            for j in range(KT):
                free(P_OUT + j)
                panel(C_OUT + j, (P_OUT + j) % 2, MX, ready=(mixlo_ready, 1) if j == 0 else None)

            def cross_scores(n):
                pe.wait_ge(panel_free, FREE_X + CROSS.index(f"q{n}") + 1)
                for f in range(2):
                    bank = s_bank(F_CROSS + 2 * n + f)
                    for b in range(2):
                        qb = 2 * f + b
                        ins = pe.matmul(bank[:, b * MEM:(b + 1) * MEM], HQ[:, n % 2, qb * P:(qb + 1) * P],
                                        MK[:, n, :],
                                        start=True, stop=True)
                    ins.then_inc(s_done, 1)

            def cross_turn(n):
                pe.wait_ge(p_ready, 16 + n + 1)
                for b in range(MB):
                    bank = r_bank(R_CT[n] + b)
                    for qb in range(TB):
                        ins = pe.transpose(bank[:, qb * P:(qb + 1) * P], P2[:, n % 2, qb, b * P:(b + 1) * P], IDENT)
                    ins.then_inc(r_done, 1)

            def cross_values(n):
                pe.wait_ge(o_free, PAIRS + n + 1)
                pe.wait_ge(r_free, R_VT[n] + 1)
                for b in range(MB):
                    pe.wait_ge(r_free, R_CT[n] + b + 1)
                    ins = pe.matmul(OB[:, :], MV[:, b, n * P:(n + 1) * P], PT2[:, n % 2, b, :], start=b == 0,
                                    stop=b == MB - 1)
                ins.then_inc(o_done, 1)

            M = [(k, MHH[:, k, :], MHL[:, k, :]) for k in range(KT)]

            def cross_panel(name, ready=None):
                j = CROSS.index(name)
                free(P_X + j)
                panel(C_X + j, (P_X + j) % 2, X if name[0] == "q" else M, T if name[0] == "q" else MEM, ready=ready)

            def memory_turn(n):
                pe.wait_ge(panel_free, FREE_X + CROSS.index(f"v{n}") + 1)
                bank = r_bank(R_VT[n])
                for b in range(MB):
                    ins = pe.transpose(bank[:, b * P:(b + 1) * P], Z[:, n % 2, b * P:(b + 1) * P], IDENT)
                ins.then_inc(r_done, 1)

            cross_panel("k0", ready=(memlo_ready, 1))
            cross_panel("k1")
            mean_square(F_QRMS, 2 * KT)
            cross_panel("q0", ready=(xlo_ready, KT + 1))
            cross_panel("v0")
            cross_scores(0)
            cross_panel("q1")
            memory_turn(0)
            cross_turn(0)
            cross_scores(1)
            cross_panel("v1")
            cross_panel("k2")
            cross_values(0)
            cross_turn(1)
            cross_panel("q2")
            memory_turn(1)
            cross_panel("v2")
            cross_scores(2)
            cross_values(1)
            cross_panel("k3")
            cross_panel("q3")
            memory_turn(2)
            cross_scores(3)
            cross_turn(2)
            cross_panel("v3")
            cross_values(2)

            def mo_heads(k0, k1):
                for b in range(2):
                    if k0 == 0:
                        free(P_MO + b)
                    last = k1 == MH
                    panel(C_MO, (P_MO + b) % 2, [(MH * b + k, OXH[:, k, :], OXL[:, k, :]) for k in range(k0, k1)],
                          first=k0 == 0, last=last, done=panel_half if b == 0 else None, ready=(o_free, PAIRS + 2 + k0))

            mo_heads(0, 1)
            memory_turn(3)
            cross_turn(3)
            mo_heads(1, 2)
            cross_values(3)
            mo_heads(2, 3)
            mo_heads(3, MH)
            OX = [[(MH * b + k, OXH[:, k, :], OXL[:, k, :]) for k in range(MH)] for b in range(2)]
            for m in range(1, KT // 2):
                for b in range(2):
                    free(P_MO + 2 * m + b)
                    panel(C_MO + m, (P_MO + b) % 2, OX[b], done=panel_half if b == 0 else None)
            for j in range(2):
                free(P_GU + j)
                panel(C_GU + j, (P_GU + j) % 2, X, ready=(xlo_ready, 2 * KT + 1) if j == 0 else None)
                if j == 0:
                    mean_square(F_FRMS, 3 * KT)
            for j in range(2, 4):
                free(P_GU + j)
                panel(C_GU + j, (P_GU + j) % 2, X)
            with pe.Fori(1, FT // 2) as r:
                for j in range(4):
                    pe.wait_ge(panel_free, r * 4 + (FREE_GU + j - 1))
                    panel(C_GU + j, (P_GU + j) % 2, X, shift=r * 4)
            HID = [(k % KT, HH[:, k, :], HL[:, k, :]) for k in range(FT)]

            def turn_final(n0, n1):
                pe.wait_ge(scaled_ready, n1)
                for n in range(n0, n1):
                    for b in range(TB):
                        ins = pe.transpose(FB[b][:, n % 4 * P:(n % 4 + 1) * P], HG[:, n, b * P:(b + 1) * P], IDENT)
                return ins

            for n in range(KT):
                free(P_DN + n)
                for m in range(3):
                    if n == KT - 1 and m == 2:
                        pe.wait_ge(final_copied, 1)
                        turn_final(4, KT - 1)
                    panel(C_DN + 3 * n + m, (P_DN + n) % 2, HID[KT * m:KT * (m + 1)], first=m == 0, last=m == 2,
                          ready=(hidlo_ready, KT * m + 1) if n == 0 else None)
                if n == 4:
                    turn_final(0, 4).then_inc(final_turned, 1)
            turn_final(KT - 1, KT).then_inc(last_turned, 1)
            pe.wait_ge(acc_ready, 4 * KT - 1)
            pe.wait_ge(sq_ready, 4 * KT)
            for b in range(TB):
                tok = slice(b * P, (b + 1) * P)
                pe.matmul(OB[:, b:b + 1], ACC[:, tok], ONES[:, 0:1], start=True, stop=False)
                ins = pe.matmul(OB[:, b:b + 1], SQ[:, (KT - 1) % 2, tok], ONES[:, 0:1], start=False, stop=True)
            ins.then_inc(mean_done, 1)


def arena_base(nc, arena, total):
    return nc.sbuf_base - 4 * total


def kernel(**inputs):
    import concourse.bacc as bacc
    from concourse import mybir
    from concourse.bass_utils import run_bass_kernel_spmd

    f = {k: np.asarray(v) for k, v in inputs.items()}

    def tiles(w):
        k, n = w.shape
        return w.reshape(k // P, P, n // P, P).transpose(2, 1, 0, 3)

    w_in = f["w_in"][0]
    win = tiles(w_in[:, :2304])
    gates = np.zeros((D, P), w_in.dtype)
    gates[:, 0:24] = w_in[:, 2304:2328]
    mrg, mkv = tiles(f["w_merge"][0]), tiles(f["w_mkv"][0])
    pa, pb = tiles(f["w_proj_a"][0]), tiles(f["w_proj_b"][0])
    wo, mq, mo = tiles(f["w_out"][0]), tiles(f["w_mq"][0]), tiles(f["w_mo"][0])
    gu, dn = tiles(f["w_gate_up"][0]), tiles(f["w_down"][0])
    pack = np.zeros((NCHUNK, P, KT, P), w_in.dtype)
    at = 0

    def put(x, u0=0):
        nonlocal at
        pack[at, :, u0:u0 + x.shape[1]] = x
        at += 1

    for n in (4, 5, 6, 7, 9):
        put(win[n])
    put(tiles(gates)[0])
    put(win[8])
    for c in range(PAIRS):
        put(win[c])
        put(win[10 + c])
        put(win[14 + c])
        put(mrg[c])
    for half in range(2):
        if half:
            for n in range(4, 8):
                put(mrg[n])
        for n in range(4 * half, 4 * half + 4):
            put(mrg[KT + n])
        for n in range(4 * half, 4 * half + 4):
            pack[at, :, 0:4] = pa[n]
            put(pb[n], 4)
    for n in range(8):
        put(wo[n])
    for name in CROSS:
        n = int(name[1])
        put({"k": mkv[n], "v": mkv[MH + n], "q": mq[n]}[name[0]])
    for m in range(4):
        pack[at, :, 0:4] = mo[2 * m]
        put(mo[2 * m + 1], 4)
    for j in range(FT):
        put(gu[j])
        put(gu[FT + j])
    for n in range(KT):
        for m in range(3):
            put(dn[n][:, KT * m:KT * (m + 1)])
    assert at == NCHUNK

    cst = np.zeros((P, NCOL), w_in.dtype)

    def col(name, a):
        c, w = COL[name]
        cst[:a.shape[0], c:c + w] = a.reshape(a.shape[0], w)

    def by_tile(v):
        return v.reshape(-1, P).T

    col("gmix", by_tile(f["norm_mix"][0]))
    col("gmem", by_tile(f["norm_mem_kv"][0]))
    col("gq", by_tile(f["norm_mem_q"][0]))
    col("gf", by_tile(f["norm_ffn"][0]))
    col("gfin", by_tile(f["norm_final"]))
    col("bm", by_tile(f["b_merge"][0]))
    col("lng", by_tile(f["ln_sgu"][0]))
    col("slope", np.broadcast_to(2.0 ** -(np.arange(8) + 1.0), (P, 8)))
    p = np.arange(P)[:, None]
    col("valid", (np.arange(TB)[None] * P + p >= 31).astype(np.float32))
    col("eps", np.full((P, 1), 1e-6))
    col("eps4", np.full((P, 1), 4e-6))
    col("w2k", np.concatenate([f["w_cmp_k2"][0]] * 2, axis=1))
    col("w2v", f["w_cmp_v2"][0])
    pes = np.stack([f["pe_cmp_k"][0], f["pe_cmp_v"][0]]).reshape(2, CJ, 2, HD).transpose(3, 0, 2, 1).reshape(HD, 64)
    col("pe", np.concatenate([pes, pes]))
    col("ident", np.eye(P))
    col("tri", np.arange(P)[None] >= p)
    x = np.arange(T)[None]
    tab = np.where(384 + p - x >= 0, 384 + p - x, MASKED)
    qb, i = np.arange(TB)[:, None], np.arange(32)[None]
    dist = (P * qb + np.arange(P)[:, None, None] - (16 * i + 31)[None]).reshape(P, P)
    tabc = np.where((dist >= 0) & (np.arange(P)[None] % 32 < NCMP), dist, MASKED)
    col("tab", np.concatenate([tab, tabc], axis=1))
    col("ws", f["w_spatial"][0].transpose(2, 0, 1))

    w1 = np.stack([f["w_cmp_k1"][0], f["w_cmp_v1"][0]]).reshape(2, CJ, P, P).transpose(2, 0, 1, 3)
    arrays = {
        "wpk": pack.reshape(NCHUNK, P, CW),
        "xT": np.ascontiguousarray(f["x"][0].T.reshape(KT, P, T).transpose(1, 0, 2)),
        "memT": np.ascontiguousarray(f["mem"][0].T.reshape(KT, P, MEM).transpose(1, 0, 2)),
        "w1": np.ascontiguousarray(w1),
        "cst": cst,
        "bsp": np.ascontiguousarray(f["b_spatial"][0]),
    }
    nc = bacc.Bacc("TRN2", target_bir_lowering=False, num_devices=1)
    dt = mybir.dt.float32
    args = [nc.dram_tensor(n, a.shape, dt, kind="ExternalInput").ap() for n, a in arrays.items()]
    out = nc.dram_tensor("out", (T, D), dt, kind="ExternalOutput").ap()
    build(nc, *args, out)
    return run_bass_kernel_spmd(nc, [arrays], core_ids=[0]).results[0]["out"][None]
```
